# Optimizing a Trainium2 kernel written in Bass

```python
import math
import jax
import jax.numpy as jnp
from jax import lax
import numpy as np
import jax, jax.numpy as jnp

D_MODEL = 1024
BATCH = 1
SEQ = 256
DEPTH = 2

GRID_W = 64
CTX_LEN = 256
HEAD_DIM = 64
MIX_HEADS = D_MODEL // HEAD_DIM
A_Q_HEADS = MIX_HEADS // 2
A_KV_HEADS = A_Q_HEADS // 4
B_Q_HEADS = MIX_HEADS - A_Q_HEADS
B_KV_HEADS = B_Q_HEADS // 4
WINDOW = 128
BLOCK = 128
NA_ROWS = 8
NA_COLS = 16
NA_QCOLS = 16
NA_KCOLS = NA_QCOLS + NA_COLS
C_HEADS = D_MODEL // (2 * HEAD_DIM)
C_V_DIM = 2 * HEAD_DIM
D_FF = 4 * D_MODEL
ROPE_THETA = 10000.0
EPS = 1e-6

A_QW = A_Q_HEADS * HEAD_DIM
A_KVW = A_KV_HEADS * HEAD_DIM
B_QW = B_Q_HEADS * HEAD_DIM
B_KVW = B_KV_HEADS * HEAD_DIM
EVEN_WIDTHS = (A_QW, A_KVW, A_KVW, B_QW, B_KVW, B_KVW)
EVEN_IN = A_QW + 2 * A_KVW + B_QW + 2 * B_KVW
EVEN_OUT = A_QW + B_QW
C_QKW = C_HEADS * 2 * HEAD_DIM
C_VW = C_HEADS * C_V_DIM
ODD_IN = 2 * C_QKW + C_VW


def _rms_norm(x, g):
    xf = x.astype(jnp.float32)
    y = xf * lax.rsqrt(jnp.mean(xf * xf, axis=-1, keepdims=True) + EPS)
    return (y * g.astype(jnp.float32)).astype(x.dtype)

def _modulate(x, g, shift, scale):
    return _rms_norm(x, g) * (1 + scale) + shift

def _rope_tables(n):
    t = jnp.arange(n, dtype=jnp.int32)
    row = (t // GRID_W).astype(jnp.float32)
    col = (t % GRID_W).astype(jnp.float32)
    quarter = HEAD_DIM // 4
    inv_freq = ROPE_THETA ** (-jnp.arange(quarter, dtype=jnp.float32) / quarter)
    ar = row[:, None] * inv_freq[None, :]
    ac = col[:, None] * inv_freq[None, :]
    ang = jnp.concatenate([ar, ar, ac, ac], axis=-1)
    return jnp.cos(ang), jnp.sin(ang)

def _apply_rope(x, cos, sin):
    xs = x.reshape(x.shape[:-1] + (2, 2, HEAD_DIM // 4))
    rot = jnp.stack([-xs[..., 1, :], xs[..., 0, :]], axis=-2).reshape(x.shape)
    return x * cos[:, None, :].astype(x.dtype) + rot * sin[:, None, :].astype(x.dtype)

def _ctx_attn(q, k, v, sink):
    b, n, hq, d = q.shape
    hkv = k.shape[2]
    g = hq // hkv
    qg = q.reshape(b, n, hkv, g, d)
    s = jnp.einsum('bqhgd,bkhd->bhgqk', qg, k).astype(jnp.float32) * d ** -0.5
    if sink is not None:
        sk = jnp.broadcast_to(sink.astype(jnp.float32).reshape(1, hkv, g, 1, 1), s.shape[:-1] + (1,))
        s = jnp.concatenate([s, sk], axis=-1)
    p = jax.nn.softmax(s, axis=-1)[..., :n].astype(v.dtype)
    return jnp.einsum('bhgqk,bkhd->bqhgd', p, v).reshape(b, n, hq * d)

def _window_attn(q, k, v, kc, vc, sink):
    b, n, hq, d = q.shape
    hkv = k.shape[2]
    g = hq // hkv
    nb = n // BLOCK
    qb = q.reshape(b, nb, BLOCK, hkv, g, d)
    pad = ((0, 0), (BLOCK, BLOCK), (0, 0), (0, 0))

    def band(t):
        tp = jnp.pad(t, pad).reshape(b, nb + 2, BLOCK, hkv, d)
        return jnp.concatenate([tp[:, :-2], tp[:, 1:-1], tp[:, 2:]], axis=2)

    kb, vb = band(k), band(v)
    scale = d ** -0.5
    s_lat = jnp.einsum('bnqhgd,bnkhd->bhgnqk', qb, kb).astype(jnp.float32) * scale
    blk = jnp.arange(nb)[:, None, None] * BLOCK
    qpos = blk + jnp.arange(BLOCK)[None, :, None]
    kpos = blk - BLOCK + jnp.arange(3 * BLOCK)[None, None, :]
    valid = (jnp.abs(qpos - kpos) <= WINDOW) & (kpos >= 0) & (kpos < n)
    s_lat = jnp.where(valid, s_lat, -jnp.inf)
    s_ctx = jnp.einsum('bnqhgd,bchd->bhgnqc', qb, kc).astype(jnp.float32) * scale
    s_sink = jnp.broadcast_to(sink.astype(jnp.float32).reshape(1, hkv, g, 1, 1, 1), s_ctx.shape[:-1] + (1,))
    p = jax.nn.softmax(jnp.concatenate([s_lat, s_ctx, s_sink], axis=-1), axis=-1).astype(v.dtype)
    nk, nc = 3 * BLOCK, kc.shape[1]
    out = (jnp.einsum('bhgnqk,bnkhd->bnqhgd', p[..., :nk], vb)
           + jnp.einsum('bhgnqc,bchd->bnqhgd', p[..., nk:nk + nc], vc))
    return out.reshape(b, n, hq * d)

def _neighbourhood_attn(q, k, v, kc, vc, rpb):
    b, n, hq, d = q.shape
    hkv = k.shape[2]
    g = hq // hkv
    rows = n // GRID_W
    kr = min(NA_ROWS, rows)
    ncb = GRID_W // NA_QCOLS
    nkey = kr * NA_KCOLS
    r = jnp.arange(rows)
    row_idx = jnp.clip(r - kr // 2, 0, rows - kr)[:, None] + jnp.arange(kr)[None, :]
    m = jnp.arange(ncb)
    col_idx = jnp.clip(m * NA_QCOLS - NA_COLS // 2, 0, GRID_W - NA_KCOLS)[:, None] + jnp.arange(NA_KCOLS)[None, :]
    qcol = m[:, None] * NA_QCOLS + jnp.arange(NA_QCOLS)[None, :]
    cstart = jnp.clip(qcol - NA_COLS // 2, 0, GRID_W - NA_COLS)
    kcol = col_idx[:, None, :]
    col_ok = (kcol >= cstart[..., None]) & (kcol < cstart[..., None] + NA_COLS)
    mask = jnp.broadcast_to(col_ok[:, :, None, :], (ncb, NA_QCOLS, kr, NA_KCOLS)).reshape(ncb, NA_QCOLS, nkey)

    def gather(t):
        tg = t.reshape(b, rows, GRID_W, hkv, d)
        tb = tg[:, row_idx[:, None, :, None], col_idx[None, :, None, :]]
        return tb.reshape(b, rows, ncb, nkey, hkv, d)

    kb, vb = gather(k), gather(v)
    roff = row_idx - r[:, None] + (NA_ROWS - 1)
    coff = jnp.clip(kcol - qcol[..., None], 1 - NA_COLS, NA_COLS - 1) + (NA_COLS - 1)
    bias = rpb[:, roff[:, :, None, None, None], coff[None, None]]
    bias = jnp.transpose(bias, (0, 1, 3, 4, 2, 5)).reshape(hkv, g, rows, ncb, NA_QCOLS, nkey).astype(jnp.float32)
    qb = q.reshape(b, rows, ncb, NA_QCOLS, hkv, g, d)
    scale = d ** -0.5
    s_nb = jnp.einsum('brmqhgd,brmkhd->bhgrmqk', qb, kb).astype(jnp.float32) * scale + bias
    s_nb = jnp.where(mask, s_nb, -jnp.inf)
    s_ctx = jnp.einsum('brmqhgd,bchd->bhgrmqc', qb, kc).astype(jnp.float32) * scale
    p = jax.nn.softmax(jnp.concatenate([s_nb, s_ctx], axis=-1), axis=-1).astype(v.dtype)
    out = (jnp.einsum('bhgrmqk,brmkhd->brmqhgd', p[..., :nkey], vb)
           + jnp.einsum('bhgrmqc,bchd->brmqhgd', p[..., nkey:], vc))
    return out.reshape(b, n, hq * d)

def _split_even(p):
    b, n, _ = p.shape
    idx = np.cumsum(EVEN_WIDTHS)[:-1].tolist()
    parts = jnp.split(p, idx, axis=-1)
    return [t.reshape(b, n, -1, HEAD_DIM) for t in parts]

def _even_mixer(hx, hc, w_in, w_out, sink, rpb, cos, sin, with_ctx):
    aq, ak, av, bq, bk, bv = _split_even(hx @ w_in)
    caq, cak, cav, cbq, cbk, cbv = _split_even(hc @ w_in)
    aq = _apply_rope(aq, cos, sin)
    ak = _apply_rope(ak, cos, sin)
    ya = _window_attn(aq, ak, av, cak, cav, sink)
    yb = _neighbourhood_attn(bq, bk, bv, cbk, cbv, rpb)
    y_x = jnp.concatenate([ya, yb], axis=-1) @ w_out
    if not with_ctx:
        return y_x, None
    y_c = jnp.concatenate([_ctx_attn(caq, cak, cav, sink), _ctx_attn(cbq, cbk, cbv, None)], axis=-1) @ w_out
    return y_x, y_c

def _split_odd(p):
    b, n, _ = p.shape
    q, k, v = jnp.split(p, [C_QKW, 2 * C_QKW], axis=-1)
    return (q.reshape(b, n, C_HEADS, 2, HEAD_DIM), k.reshape(b, n, C_HEADS, 2, HEAD_DIM),
            v.reshape(b, n, C_HEADS, C_V_DIM))

def _diff_core(q, k, v, lam, sub_g, lam_init):
    b, nq, h, _, d = q.shape
    s = jnp.einsum('bqhmd,bkhmd->bhmqk', q, k).astype(jnp.float32) * d ** -0.5
    p = jax.nn.softmax(s, axis=-1)
    a = (p[:, :, 0] - lam * p[:, :, 1]).astype(v.dtype)
    o = jnp.einsum('bhqk,bkhe->bqhe', a, v)
    o = _rms_norm(o, sub_g) * (1.0 - lam_init)
    return o.reshape(b, nq, h * v.shape[-1])

def _odd_mixer(hx, hc, w_in, w_out, lq1, lk1, lq2, lk2, sub_g, lam_init, cos, sin, with_ctx):
    q, k, v = _split_odd(hx @ w_in)
    cq, ck, cv = _split_odd(hc @ w_in)
    b, n = q.shape[:2]
    q = _apply_rope(q.reshape(b, n, 2 * C_HEADS, HEAD_DIM), cos, sin).reshape(q.shape)
    k = _apply_rope(k.reshape(b, n, 2 * C_HEADS, HEAD_DIM), cos, sin).reshape(k.shape)
    f32 = jnp.float32
    lam = (jnp.exp(jnp.sum(lq1.astype(f32) * lk1.astype(f32)))
           - jnp.exp(jnp.sum(lq2.astype(f32) * lk2.astype(f32))) + lam_init)
    kf = jnp.concatenate([k, ck], axis=1)
    vf = jnp.concatenate([v, cv], axis=1)
    nb = n // BLOCK
    qb = jnp.swapaxes(q.reshape(b, nb, BLOCK, C_HEADS, 2, HEAD_DIM), 0, 1)
    yx = lax.map(lambda qblk: _diff_core(qblk, kf, vf, lam, sub_g, lam_init), qb)
    yx = jnp.swapaxes(yx, 0, 1).reshape(b, n, C_VW) @ w_out
    if not with_ctx:
        return yx, None
    yc = _diff_core(cq, ck, cv, lam, sub_g, lam_init) @ w_out
    return yx, yc

def _mlp(h, w1, w2):
    a = jax.nn.relu(h @ w1)
    return (a * a) @ w2

def first_inputs(seed: int = 0) -> dict:
    key = jax.random.key(seed)
    ks = jax.random.split(key, 22)
    n_even = (DEPTH + 1) // 2
    n_odd = DEPTH // 2

    def nrm(k, shape, s):
        return jax.random.normal(k, shape, jnp.float32) * s

    return {
        'x': nrm(ks[0], (BATCH, SEQ, D_MODEL), 1.0),
        'c': nrm(ks[1], (BATCH, D_MODEL), 1.0),
        'ctx': nrm(ks[2], (BATCH, CTX_LEN, D_MODEL), 1.0),
        'c_ctx': nrm(ks[3], (D_MODEL,), 1.0),
        'ada_w': nrm(ks[4], (DEPTH, D_MODEL, 6 * D_MODEL), 0.5 * D_MODEL ** -0.5),
        'ada_b': nrm(ks[5], (DEPTH, 6 * D_MODEL), 0.01),
        'norm1_g': 1.0 + nrm(ks[6], (DEPTH, D_MODEL), 0.05),
        'norm2_g': 1.0 + nrm(ks[7], (DEPTH, D_MODEL), 0.05),
        'even_w_in': nrm(ks[8], (n_even, D_MODEL, EVEN_IN), D_MODEL ** -0.5),
        'even_w_out': nrm(ks[9], (n_even, EVEN_OUT, D_MODEL), EVEN_OUT ** -0.5),
        'a_sink': nrm(ks[10], (n_even, A_Q_HEADS), 0.5),
        'b_rpb': nrm(ks[11], (n_even, B_Q_HEADS, 2 * NA_ROWS - 1, 2 * NA_COLS - 1), 0.1),
        'odd_w_in': nrm(ks[12], (n_odd, D_MODEL, ODD_IN), D_MODEL ** -0.5),
        'odd_w_out': nrm(ks[13], (n_odd, C_VW, D_MODEL), C_VW ** -0.5),
        'lam_q1': nrm(ks[14], (n_odd, HEAD_DIM), 0.1),
        'lam_k1': nrm(ks[15], (n_odd, HEAD_DIM), 0.1),
        'lam_q2': nrm(ks[16], (n_odd, HEAD_DIM), 0.1),
        'lam_k2': nrm(ks[17], (n_odd, HEAD_DIM), 0.1),
        'subln_g': 1.0 + nrm(ks[18], (n_odd, C_V_DIM), 0.05),
        'mlp_w1': nrm(ks[19], (DEPTH, D_MODEL, D_FF), D_MODEL ** -0.5),
        'mlp_w2': nrm(ks[20], (DEPTH, D_FF, D_MODEL), D_FF ** -0.5),
        'final_g': 1.0 + nrm(ks[21], (D_MODEL,), 0.05),
    }

def first_block(x, c, ctx, c_ctx, ada_w, ada_b, norm1_g, norm2_g, even_w_in, even_w_out, a_sink, b_rpb,
              odd_w_in, odd_w_out, lam_q1, lam_k1, lam_q2, lam_k2, subln_g, mlp_w1, mlp_w2, final_g):
    n = x.shape[1]
    cos, sin = _rope_tables(n)
    hx, hc = x, ctx
    for i in range(DEPTH):
        with_ctx = i < DEPTH - 1
        j = i // 2
        mx = (jax.nn.silu(c) @ ada_w[i] + ada_b[i])[:, None, :]
        mc = jax.nn.silu(c_ctx) @ ada_w[i] + ada_b[i]
        sx1, cx1, gx1, sx2, cx2, gx2 = jnp.split(mx, 6, axis=-1)
        sc1, cc1, gc1, sc2, cc2, gc2 = jnp.split(mc, 6, axis=-1)
        ax = _modulate(hx, norm1_g[i], sx1, cx1)
        ac = _modulate(hc, norm1_g[i], sc1, cc1)
        if i % 2 == 0:
            yx, yc = _even_mixer(ax, ac, even_w_in[j], even_w_out[j], a_sink[j], b_rpb[j], cos, sin, with_ctx)
        else:
            lam_init = 0.8 - 0.6 * math.exp(-0.3 * i)
            yx, yc = _odd_mixer(ax, ac, odd_w_in[j], odd_w_out[j], lam_q1[j], lam_k1[j], lam_q2[j], lam_k2[j],
                                subln_g[j], lam_init, cos, sin, with_ctx)
        hx = hx + gx1 * yx
        hx = hx + gx2 * _mlp(_modulate(hx, norm2_g[i], sx2, cx2), mlp_w1[i], mlp_w2[i])
        if with_ctx:
            hc = hc + gc1 * yc
            hc = hc + gc2 * _mlp(_modulate(hc, norm2_g[i], sc2, cc2), mlp_w1[i], mlp_w2[i])
    return _rms_norm(hx, final_g)


A_HEADS = 6
A_NOPE = 64
A_ROPE = 32
A_V = 64
Q_LORA = 768
KV_LORA = 256
B_HEADS = 6
DILATED_PATTERNS = ((128, 1), (512, 4), (2048, 16))
C_HEADS_2 = 4
IDX_HEADS = 8
IDX_DIM = 64
TOPK_MAX = 256
Q_BLOCK = 128

A_WIDTH = A_HEADS * A_V
B_WIDTH = B_HEADS * HEAD_DIM
C_WIDTH = C_HEADS_2 * HEAD_DIM
MIX_WIDTH = A_WIDTH + B_WIDTH + C_WIDTH
N_ALIBI = B_HEADS + C_HEADS_2

SPLIT_SIZES = (Q_LORA, KV_LORA, A_ROPE,
               B_WIDTH, B_WIDTH, B_WIDTH,
               C_WIDTH, C_WIDTH, C_WIDTH,
               IDX_HEADS * IDX_DIM, IDX_DIM, IDX_HEADS,
               MIX_WIDTH)
IN_WIDTH = sum(SPLIT_SIZES)
SPLIT_POINTS = [int(v) for v in np.cumsum(SPLIT_SIZES)[:-1]]

ALPHA = (2 * DEPTH) ** 0.25
BETA = (8 * DEPTH) ** -0.25


F32 = jnp.float32

def layer_norm(x, g, b, eps=1e-5):
    xf = x.astype(F32)
    mu = jnp.mean(xf, axis=-1, keepdims=True)
    xc = xf - mu
    var = jnp.mean(xc * xc, axis=-1, keepdims=True)
    return (xc * lax.rsqrt(var + eps) * g.astype(F32) + b.astype(F32)).astype(x.dtype)

def rms_norm(x, g, eps=1e-6):
    xf = x.astype(F32)
    ms = jnp.mean(xf * xf, axis=-1, keepdims=True)
    return (xf * lax.rsqrt(ms + eps) * g.astype(F32)).astype(x.dtype)

def apply_rope(x, cos, sin):
    half = x.shape[-1] // 2
    x1, x2 = x[..., :half].astype(F32), x[..., half:].astype(F32)
    return jnp.concatenate([x1 * cos - x2 * sin, x1 * sin + x2 * cos], axis=-1).astype(x.dtype)

def alibi_slopes():
    return 2.0 ** (-8.0 * jnp.arange(1, N_ALIBI + 1, dtype=F32) / N_ALIBI)

def to_blocks(a):
    b, s = a.shape[0], a.shape[1]
    return a.reshape((b, s // Q_BLOCK, Q_BLOCK) + a.shape[2:]).swapaxes(0, 1)

def from_blocks(a):
    a = a.swapaxes(0, 1)
    return a.reshape((a.shape[0], a.shape[1] * a.shape[2]) + a.shape[3:])

def mla_attention(q_nope, q_rope, k_nope, k_rope, v):
    s_len = q_nope.shape[1]
    nb = s_len // Q_BLOCK
    scale = (A_NOPE + A_ROPE) ** -0.5
    key_pos = jnp.arange(s_len)

    def block(args):
        qn, qr, start = args
        qpos = start + jnp.arange(Q_BLOCK)
        s = (jnp.einsum('bqhd,bshd->bhqs', qn, k_nope, preferred_element_type=F32)
             + jnp.einsum('bqhr,bsr->bhqs', qr, k_rope, preferred_element_type=F32)) * scale
        s = jnp.where(key_pos[None, :] <= qpos[:, None], s, -jnp.inf)
        p = jax.nn.softmax(s, axis=-1)
        return jnp.einsum('bhqs,bshd->bqhd', p.astype(v.dtype), v)

    out = lax.map(block, (to_blocks(q_nope), to_blocks(q_rope), jnp.arange(nb) * Q_BLOCK))
    return from_blocks(out)

def dilated_attention(q, k, v, slopes):
    bsz, s_len, nh, dh = q.shape
    outs, lses = [], []
    for window, dil in DILATED_PATTERNS:
        n = window // dil
        L = s_len // dil
        nb = -(-L // n)
        Lp = nb * n

        def gather(a):
            a = a.reshape(bsz, L, dil, nh, dh).swapaxes(1, 2)
            a = jnp.pad(a, ((0, 0), (0, 0), (0, Lp - L), (0, 0), (0, 0)))
            return a.reshape(bsz, dil, nb, n, nh, dh)

        def band(a):
            prev = jnp.pad(a, ((0, 0), (0, 0), (1, 0), (0, 0), (0, 0), (0, 0)))[:, :, :-1]
            return jnp.concatenate([prev, a], axis=3)

        qb = gather(q)
        kb = band(gather(k))
        vb = band(gather(v))
        s = jnp.einsum('brnqhd,brnkhd->brnhqk', qb, kb, preferred_element_type=F32) * dh ** -0.5
        kj = jnp.arange(2 * n)
        step = jnp.arange(n)[:, None] + n - kj[None, :]
        valid = ((step >= 0) & (step <= n))[None] & ((jnp.arange(nb)[:, None, None] > 0) | (kj >= n)[None, None, :])
        s = s - slopes[:, None, None] * (step * dil).astype(F32)
        s = jnp.where(valid[:, None], s, -jnp.inf)
        m = jnp.max(s, axis=-1, keepdims=True)
        p = jnp.exp(s - m)
        den = jnp.sum(p, axis=-1, keepdims=True)
        o = jnp.einsum('brnhqk,brnkhd->brnqhd', (p / den).astype(v.dtype), vb)
        lse = (m + jnp.log(den))[..., 0].swapaxes(-1, -2)

        def ungather(a):
            tr = a.shape[4:]
            a = a.reshape((bsz, dil, Lp) + tr)[:, :, :L]
            return a.swapaxes(1, 2).reshape((bsz, s_len) + tr)

        outs.append(ungather(o))
        lses.append(ungather(lse))
    w = jax.nn.softmax(jnp.stack(lses, axis=0), axis=0)
    out = jnp.sum(w[..., None] * jnp.stack(outs, axis=0).astype(F32), axis=0)
    return out.astype(q.dtype)

def sparse_attention(q, k, v, q_idx, k_idx, w_idx, slopes):
    s_len, dh = q.shape[1], q.shape[3]
    topk = min(TOPK_MAX, s_len // 4)
    nb = s_len // Q_BLOCK
    key_pos = jnp.arange(s_len)
    take = jax.vmap(lambda a, i: a[i])

    def block(args):
        qb, qib, wb, start = args
        qpos = start + jnp.arange(Q_BLOCK)
        logits = jnp.einsum('bqhd,bsd->bqhs', qib, k_idx, preferred_element_type=F32) * IDX_DIM ** -0.5
        score = jnp.einsum('bqh,bqhs->bqs', wb.astype(F32) * IDX_HEADS ** -0.5, jax.nn.relu(logits))
        score = jnp.where(key_pos[None, None, :] <= qpos[None, :, None], score, -jnp.inf)
        _, idx = lax.top_k(score, topk)
        valid = idx <= qpos[None, :, None]
        kg = take(k, idx)
        vg = take(v, idx)
        s = jnp.einsum('bqhd,bqkhd->bhqk', qb, kg, preferred_element_type=F32) * dh ** -0.5
        dist = (qpos[None, :, None] - idx).astype(F32)
        s = s - slopes[None, :, None, None] * dist[:, None]
        s = jnp.where(valid[:, None], s, -jnp.inf)
        p = jax.nn.softmax(s, axis=-1)
        return jnp.einsum('bhqk,bqkhd->bqhd', p.astype(v.dtype), vg)

    out = lax.map(block, (to_blocks(q), to_blocks(q_idx), to_blocks(w_idx), jnp.arange(nb) * Q_BLOCK))
    return from_blocks(out)

def second_inputs(seed: int = 0) -> dict:
    key = jax.random.key(seed)
    ks = jax.random.split(key, 14)
    nrm = jax.random.normal
    return {
        "x": nrm(ks[0], (BATCH, SEQ, D_MODEL), F32),
        "c": nrm(ks[1], (BATCH, D_MODEL), F32),
        "w_ada": nrm(ks[2], (DEPTH, D_MODEL, 3 * D_MODEL), F32) * (0.1 * D_MODEL ** -0.5),
        "b_ada": nrm(ks[3], (DEPTH, 3 * D_MODEL), F32) * 0.02,
        "w_in": nrm(ks[4], (DEPTH, D_MODEL, IN_WIDTH), F32) * D_MODEL ** -0.5,
        "q_norm_g": 1.0 + 0.02 * nrm(ks[5], (DEPTH, Q_LORA), F32),
        "kv_norm_g": 1.0 + 0.02 * nrm(ks[6], (DEPTH, KV_LORA), F32),
        "w_uq": nrm(ks[7], (DEPTH, Q_LORA, A_HEADS * (A_NOPE + A_ROPE)), F32) * Q_LORA ** -0.5,
        "w_uk": nrm(ks[8], (DEPTH, KV_LORA, A_HEADS * A_NOPE), F32) * KV_LORA ** -0.5,
        "w_uv": nrm(ks[9], (DEPTH, KV_LORA, A_HEADS * A_V), F32) * KV_LORA ** -0.5,
        "w_out": nrm(ks[10], (DEPTH, MIX_WIDTH, D_MODEL), F32) * (BETA * MIX_WIDTH ** -0.5),
        "ln_g": 1.0 + 0.02 * nrm(ks[11], (DEPTH, D_MODEL), F32),
        "ln_b": 0.02 * nrm(ks[12], (DEPTH, D_MODEL), F32),
    }

def second_block(x, c, w_ada, b_ada, w_in, q_norm_g, kv_norm_g, w_uq, w_uk, w_uv, w_out, ln_g, ln_b):
    bsz, s_len, _ = x.shape
    slopes = alibi_slopes()
    slopes_b, slopes_c = slopes[:B_HEADS], slopes[B_HEADS:]
    pos = jnp.arange(s_len, dtype=F32)
    freqs = ROPE_THETA ** (-jnp.arange(0, A_ROPE, 2, dtype=F32) / A_ROPE)
    ang = pos[:, None] * freqs[None, :]
    cos, sin = jnp.cos(ang), jnp.sin(ang)

    def heads(a, n):
        return a.reshape(bsz, s_len, n, -1)

    for l in range(DEPTH):
        mod = jax.nn.silu(c) @ w_ada[l] + b_ada[l]
        shift, scale, gate = jnp.split(mod, 3, axis=-1)
        h = x * (1.0 + scale[:, None, :]) + shift[:, None, :]
        (p_cq, p_ckv, p_kr, p_qb, p_kb, p_vb, p_qc, p_kc, p_vc,
         p_qi, p_ki, p_wi, p_gate) = jnp.split(h @ w_in[l], SPLIT_POINTS, axis=-1)

        cq = rms_norm(p_cq, q_norm_g[l])
        ckv = rms_norm(p_ckv, kv_norm_g[l])
        qa = heads(cq @ w_uq[l], A_HEADS)
        qa_nope = qa[..., :A_NOPE]
        qa_rope = apply_rope(qa[..., A_NOPE:], cos[:, None, :], sin[:, None, :])
        ka_nope = heads(ckv @ w_uk[l], A_HEADS)
        va = heads(ckv @ w_uv[l], A_HEADS)
        ka_rope = apply_rope(p_kr, cos, sin)
        o_a = mla_attention(qa_nope, qa_rope, ka_nope, ka_rope, va)

        o_b = dilated_attention(heads(p_qb, B_HEADS), heads(p_kb, B_HEADS), heads(p_vb, B_HEADS), slopes_b)

        o_c = sparse_attention(heads(p_qc, C_HEADS_2), heads(p_kc, C_HEADS_2), heads(p_vc, C_HEADS_2),
                               heads(p_qi, IDX_HEADS), p_ki, p_wi, slopes_c)

        y = jnp.concatenate([o_a.reshape(bsz, s_len, A_WIDTH),
                             o_b.reshape(bsz, s_len, B_WIDTH),
                             o_c.reshape(bsz, s_len, C_WIDTH)], axis=-1) * jax.nn.silu(p_gate)
        sub = y @ w_out[l]
        x = layer_norm(ALPHA * x + (1.0 + gate[:, None, :]) * sub, ln_g[l], ln_b[l])
    return x


def setup_inputs(seed=0):
    out = dict(first_inputs(seed))
    for name, value in second_inputs(seed + 1).items():
        if name != "x":
            out[name + "_2"] = value
    return out


def reference(
    x, c, ctx, c_ctx, ada_w, ada_b, norm1_g, norm2_g, even_w_in, even_w_out, a_sink, b_rpb,
    odd_w_in, odd_w_out, lam_q1, lam_k1, lam_q2, lam_k2, subln_g, mlp_w1, mlp_w2, final_g, c_2,
    w_ada_2, b_ada_2, w_in_2, q_norm_g_2, kv_norm_g_2, w_uq_2, w_uk_2, w_uv_2, w_out_2, ln_g_2,
    ln_b_2,
):
    x = first_block(
        x, c, ctx, c_ctx, ada_w, ada_b, norm1_g, norm2_g, even_w_in, even_w_out, a_sink, b_rpb,
        odd_w_in, odd_w_out, lam_q1, lam_k1, lam_q2, lam_k2, subln_g, mlp_w1, mlp_w2, final_g,
    )
    return second_block(
        x, c_2, w_ada_2, b_ada_2, w_in_2, q_norm_g_2, kv_norm_g_2, w_uq_2, w_uk_2, w_uv_2,
        w_out_2, ln_g_2, ln_b_2,
    )


_drawn_inputs = setup_inputs


def setup_inputs(seed=0):
    import zlib

    import numpy as np

    out = dict(_drawn_inputs(seed))
    spreads = {}
    factors = {'norm1_g': 5.11,
     'a_sink': 8.0,
     'b_rpb': 8.0,
     'lam_q1': 8.0,
     'lam_k1': 3.142,
     'lam_q2': 3.138,
     'subln_g': 6.192,
     'b_ada_2': 5.642,
     'q_norm_g_2': 8.0,
     'kv_norm_g_2': 8.0}
    for name, (base, spread) in spreads.items():
        noise = np.random.default_rng([zlib.crc32(name.encode()), seed]).standard_normal(out[name].shape)
        drawn = base * np.exp(spread * noise) if base else spread * noise
        out[name] = jnp.asarray(drawn.astype(out[name].dtype))
    for name, factor in factors.items():
        out[name] = (out[name] * factor).astype(out[name].dtype)
    return out
```

```python
import math
from contextlib import ExitStack

import concourse.bass as bass
import numpy as np
from concourse import mybir

F32 = mybir.dt.float32
F32R = mybir.dt.float32r
ALU = mybir.AluOpType
ACT = mybir.ActivationFunctionType
AX = mybir.AxisListType

P = 128
D = 1024
KT = D // P
N = 256
SLOTS = 4
AHEAD = 3
ADA_SLOTS = 4
ADA_N = 384
GROUP = 4 * ADA_N
QUARTERS = 4
NEG = -1.0e30
TAKEN = -3.0e38
TOPK = 64
LAM_INIT = 0.8 - 0.6 * math.exp(-0.3)
ALPHA = 4 ** 0.25

C_ID, C_ONE, C_RQ, C_RM = 0, 128, 256, 384
C_COS, C_SIN, C_COSM, C_SINM = 512, 768, 1024, 1280
C_WIN, C_NBR, C_CAU = 1536, 2048, 2560
C_END = 2944
P_CV, P_AB, P_N1, P_N2, P_FIN, P_LNG, P_LNB, P_QN, P_KVN, P_SUB, P_SINK, P_LAM = (
    0, 24, 168, 184, 200, 208, 224, 240, 252, 256, 257, 265)
P_END = 269

U_L0 = 0
L0_FM = 10
U_L0_OUT = L0_FM + 2
U_L0_MLP = U_L0_OUT + KT
MLP_UNITS = QUARTERS * 16
U_L1 = U_L0_MLP + MLP_UNITS
L1_FM = 16
U_L1_OUT = U_L1 + L1_FM + 8
U_L1_MLP = U_L1_OUT + KT
U_B2 = U_L1_MLP + MLP_UNITS
B2_FM1 = 9
B2_FM2 = 14
B2_UNITS = B2_FM1 + B2_FM2 + 6 + KT + 6 + 1 + 1 + KT
UNITS = U_B2 + 2 * B2_UNITS
ADA_UNITS = 12 * KT


def program(nc, wall, aall, const, prm, xin, rpb, ali, out):
    with ExitStack() as top:
        def sb(name, shape, dt=F32, scope=top):
            return scope.enter_context(nc.sbuf_tensor(name, shape, dt))

        sems = {}

        def sem(name):
            if name not in sems:
                sems[name] = top.enter_context(nc.semaphore(name))
            return sems[name]

        ps = top.enter_context(nc.psum_tensor("ps", [P, 8, 512], F32))

        X = sb("X", [P, KT, 2 * N])
        raw = sb("raw", [P, SLOTS, 1024])
        whi = sb("whi", [P, SLOTS, 1024], F32R)
        wlo = sb("wlo", [P, SLOTS, 1024], F32R)
        wk1 = sb("wk1", [P, 4, 512])
        wk2 = sb("wk2", [P, 4, 512])
        RS = sb("RS", [P, 512])
        VS = sb("VS", [P, 2, 16])
        VR = sb("VR", [P, 2, 4])
        cst = sb("cst", [P, C_END])
        par = sb("par", [P, P_END])
        ada = sb("ada", [P, 3, 3, 48])
        SC = sb("SC", [P, 24, 8])
        small = sb("small", [P, 2, 16])
        lam = sb("lam", [P, 8])
        nsink = sb("nsink", [P, 8])
        mhalf = sb("mhalf", [P, 1])

        ident = cst[:, C_ID:C_ID + P]
        ones = cst[:, C_ONE:C_ONE + P]
        E = wk1[:, :, :].rearrange("p (g r) n -> p g r n", g=2)
        PT = wk2[:, :, :].rearrange("p (g r) n -> p g r n", g=2)
        SQ = wk1
        Y = wk2[:, 0:2, :]
        M = wk2[:, 2:4, :]

        b1 = ExitStack()
        Hh = sb("Hh", [P, KT, 2 * N], F32R, b1)
        Hl = sb("Hl", [P, KT, 2 * N], F32R, b1)
        aring = sb("aring", [P, ADA_SLOTS, GROUP], F32, b1)
        AR = sb("AR", [P, ADA_N], F32, b1)
        scs = sb("scs", [P, KT, 32], F32, b1)
        stp = sb("stp", [P, 2, KT, 3], F32, b1)
        s0 = ExitStack()
        Q0 = sb("Q0", [P, 8, 2 * N], F32, s0)
        K0 = sb("K0", [P, 2, 2, 2 * N], F32, s0)
        V0 = sb("V0", [P, 4, N], F32, s0)
        BI = sb("BI", [P, 2, 8, N], F32, s0)
        s0.close()
        s1 = ExitStack()
        Q1 = sb("Q1", [P, 8, 2, N], F32, s1)
        K1 = sb("K1", [P, 8, 2 * N], F32, s1)
        V1 = sb("V1", [P, 4, D], F32, s1)
        s1.close()

        def OY(h):
            return aring[:, h // 4, N * (h % 4):N * (h % 4) + N]

        sm = ExitStack()
        HIDh = sb("HIDh", [P, KT, 2 * N], F32R, sm)
        HIDl = sb("HIDl", [P, KT, 2 * N], F32R, sm)
        sm.close()
        b1.close()
        b2 = ExitStack()
        Gh = sb("Gh", [P, KT, N], F32R, b2)
        Gl = sb("Gl", [P, KT, N], F32R, b2)
        QZ = sb("QZ", [P, 5, 2, N], F32, b2)
        KQ = sb("KQ", [P, 9, N], F32, b2)
        V2 = sb("V2", [P, 2, 3 * N], F32, b2)
        GT = sb("GT", [P, KT, N], F32, b2)
        QA = sb("QA", [P, 6, N], F32, b2)
        KA = sb("KA", [P, 6, N], F32, b2)
        VA = sb("VA", [P, 2, 384], F32, b2)
        KK = sb("KK", [P, N], F32, b2)
        KI = sb("KI", [P, 2, N], F32, b2)
        AL = sb("AL", [P, 10, 384], F32, b2)
        MO = sb("MO", [P, 2, P], F32, b2)
        WI = sb("WI", [P, 2, 8], F32, b2)
        sa = ExitStack()
        PQ = sb("PQ", [P, 8, N], F32, sa)
        CQh = sb("CQh", [P, 8, N], F32R, sa)
        CQl = sb("CQl", [P, 8, N], F32R, sa)
        sa.close()
        sbx = ExitStack()
        RI = sb("RI", [P, 8, 384], F32, sbx)
        SB = sb("SB", [P, 4, 384], F32, sbx)
        IX = sb("IX", [P, 384], F32, sbx)
        SEL = sb("SEL", [P, 384], F32, sbx)
        M8 = sb("M8", [P, 16], F32, sbx)
        sbx.close()
        b2.close()

        KOFF, KLEN = (0, P), (P, 2 * P)

        class Norm:

            def __init__(self, src, n, T, width, streams, dst, eps=1e-6, keep=None, ready=()):
                self.src, self.n, self.T, self.width, self.eps = src, n, T, width, eps
                self.streams = streams
                self.dst = dst
                self.keep = keep
                self.ready = ready

        def adacol(s, v, t):
            return ada[:, s, v, t:t + 1]

        def xt(k, T):
            return X[:, k, 0:T]

        def mod(scale_row, s, v, t0):
            return lambda k: SC[:, scale_row, k:k + 1], lambda k: adacol(s, v, t0 + k)

        Hd = (lambda k: Hh[:, k, :], lambda k: Hl[:, k, :])
        Hdx = (lambda k: Hh[:, k, 0:N], lambda k: Hl[:, k, 0:N])
        Gd = (lambda k: Gh[:, k, :], lambda k: Gl[:, k, :])

        x_in = [("x_landed", 16)]
        norms = {}
        norms["l0a"] = Norm(xt, 8, 512, D, [(0, *mod(0, 0, 0, 0)), (N, *mod(1, 0, 1, 0))], Hd, ready=x_in)
        norms["l0b"] = Norm(xt, 8, 512, D, [(0, *mod(2, 0, 0, 24)), (N, *mod(3, 0, 1, 24))], Hd,
                            ready=[("out_added", 8)])
        norms["l1a"] = Norm(xt, 8, 512, D, [(0, *mod(4, 1, 0, 0)), (N, *mod(5, 1, 1, 0))], Hd,
                            ready=[("mlp_added", 33)])
        norms["l1b"] = Norm(xt, 8, 256, D, [(0, *mod(6, 1, 0, 24))], Hdx, ready=[("out_added", 16)])
        norms["fin"] = Norm(xt, 8, 256, D, [(0, *mod(8, 2, 2, 0))], Gd, ready=[("mlp_added", 65)],
                            keep=(lambda k: X[:, k, 0:N], lambda k: par[:, P_FIN + k:P_FIN + k + 1], None))
        for l in range(2):
            norms[f"q{l}"] = Norm(lambda k, T: PQ[:, k, 0:T], 6, 256, 768,
                                  [(0, lambda k, l=l: par[:, P_QN + 6 * l + k:P_QN + 6 * l + k + 1], None)],
                                  (lambda k: CQh[:, k, :], lambda k: CQl[:, k, :]),
                                  ready=[])
            norms[f"kv{l}"] = Norm(lambda k, T: PQ[:, 6 + k, 0:T], 2, 256, 256,
                                   [(0, lambda k, l=l: par[:, P_KVN + 2 * l + k:P_KVN + 2 * l + k + 1], None)],
                                   (lambda k: CQh[:, 6 + k, :], lambda k: CQl[:, 6 + k, :]),
                                   ready=[])
            norms[f"ln{l}"] = Norm(xt, 8, 256, D, [(0, *mod(9, 2, 2, 24))] if l == 0 else [],
                                   Gd if l == 0 else None, eps=1e-5, ready=[("centred", 8 * (l + 1))],
                                   keep=(lambda k: X[:, k, 0:N],
                                         lambda k, l=l: par[:, P_LNG + 8 * l + k:P_LNG + 8 * l + k + 1],
                                         lambda k, l=l: par[:, P_LNB + 8 * l + k:P_LNB + 8 * l + k + 1]))

        order = ["l0a", "l0b", "l1a", "l1b", "fin", "q0", "kv0", "ln0", "q1", "kv1", "ln1"]
        tiles = split_tiles = 0
        for idx, name in enumerate(order):
            n = norms[name]
            n.t0, n.h0, n.idx = tiles, split_tiles, idx
            tiles += n.n
            split_tiles += n.n if n.dst else 0

        class Tile:

            def __init__(self, T, rope, dst, rest=()):
                self.T, self.rope = T, rope
                self.dst = dst if isinstance(dst, list) else [(slice(0, dst.shape[0]), dst)]
                self.rest = rest

        class Proj:
            outs = 0
            ropes = 0

            def __init__(self, u0, tiles):
                self.u0, self.tiles = u0, tiles
                self.o0, self.r0 = Proj.outs, Proj.ropes
                Proj.outs += len(tiles)
                Proj.ropes += sum(t.rope is not None for t in tiles)

            def rope_index(self, i):
                return self.r0 + sum(t.rope is not None for t in self.tiles[:i])

        def rows(r):
            return slice(64 * r, 64 * r + 64)

        def halves(ap):
            return [(rows(r), ap(r)[rows(r)]) for r in range(2)]

        def l0_tile(i):
            if i < 4:
                return Tile(512, "q", Q0[:, i, 0:N], [(slice(0, P), Q0[:, i, N:2 * N])])
            if i == 4:
                return Tile(512, "q", halves(lambda r: K0[:, 0, r, 0:N]), halves(lambda r: K0[:, 0, r, N:2 * N]))
            if i < 9:
                return Tile(512, None, Q0[:, i - 1, :])
            return Tile(512, None, halves(lambda r: K0[:, 1, r, :]))

        p_l0 = Proj(U_L0, [l0_tile(i) for i in range(L0_FM)])
        V_L0 = Proj.outs
        Proj.outs += 4
        p_l1 = Proj(U_L1, [Tile(256, "q", halves(lambda r, i=i: Q1[:, i, r, :])) for i in range(8)]
                    + [Tile(512, "q", K1[:, i, 0:N], [(slice(0, P), K1[:, i, N:2 * N])]) for i in range(8)])

        def b2_tile(i):
            if i < 3 or 6 <= i < 8:
                n = i if i < 3 else i - 3
                return Tile(256, None, halves(lambda r: QZ[:, n, r, :]))
            return Tile(256, None, KQ[:, i - 3 if i < 6 else i - 5, :])

        V_L1 = Proj.outs
        Proj.outs += 16
        p_a, p_b, V_B2, p_g, p_uq, p_uk, V_UV = [], [], [], [], [], [], []
        for l in range(2):
            u = U_B2 + l * B2_UNITS
            p_a.append(Proj(u, [Tile(256, None, PQ[:, i, :]) for i in range(8)] + [Tile(256, "m", KK[0:96, :])]))
            p_b.append(Proj(u + 9, [b2_tile(i) for i in range(B2_FM2)]))
            V_B2.append(Proj.outs)
            Proj.outs += 6
            p_g.append(Proj(u + 29, [Tile(256, None, GT[:, i, :]) for i in range(KT)]))
            p_uq.append(Proj(u + 37, [Tile(256, "m", QA[0:96, i, :]) for i in range(6)]))
            p_uk.append(Proj.outs)
            Proj.outs += 3
            V_UV.append(Proj.outs)
            Proj.outs += 2

        class Job:

            def __init__(self, q, k, nk, bias, pre, post, v, dst, sink=None, diff=False, gate=None, fence=None):
                self.q, self.k, self.nk, self.bias, self.pre, self.post = q, k, nk, bias, pre, post
                self.v, self.dst, self.sink, self.diff, self.gate, self.fence = v, dst, sink, diff, gate, fence

        def two(ap, n):
            return ap[:, None, :].to_broadcast([P, 2, n])

        jobs = []
        for kind in range(2):
            for i in range(4):
                for t in range(4):
                    ctx_q = t >= 2
                    t2 = t % 2
                    bias = None
                    if not ctx_q:
                        bias = (two(cst[:, C_WIN + N * t2:C_WIN + N * t2 + N], N) if kind == 0
                                else BI[:, t2, 2 * i:2 * i + 2, :])
                    k0 = N if ctx_q else 0
                    jobs.append(Job(
                        q=[Q0[:, 4 * kind + i, P * t:P * t + P] for r in range(2)],
                        k=[K0[:, kind, r, k0:2 * N] for r in range(2)],
                        nk=2 * N - k0, bias=bias, pre=1.0, post=0.125,
                        v=(lambda kt, r, kind=kind, k0=k0: V0[:, k0 // P + kt, P * kind + 64 * r:P * kind + 64 * r + 64]),
                        dst=(Hh[:, 4 * kind + i, P * t:P * t + P], Hl[:, 4 * kind + i, P * t:P * t + P]),
                        sink=(2 * i if kind == 0 else None)))
        J_L0 = (0, len(jobs))
        for h in range(8):
            for t in range(2):
                jobs.append(Job(
                    q=[Q1[:, h, r, P * t:P * t + P] for r in range(2)],
                    k=[K1[:, h, :] for r in range(2)], nk=2 * N, bias=None, pre=1.0, post=0.125,
                    v=(lambda kt, r, h=h: V1[:, kt, P * h:P * h + P]),
                    dst=OY(h)[:, P * t:P * t + P], diff=True))
        J_L1 = (J_L0[1], len(jobs))
        J_B2 = []
        for l in range(2):
            j0 = len(jobs)
            for i in range(3):
                for t in range(2):
                    jobs.append(Job(
                        q=[QA[0:96, 2 * i + r, P * t:P * t + P] for r in range(2)],
                        k=[KA[0:96, 2 * i + r, 0:KLEN[t]] for r in range(2)], nk=KLEN[t],
                        bias=two(cst[:, C_CAU + KOFF[t]:C_CAU + KOFF[t] + KLEN[t]], KLEN[t]),
                        pre=96 ** -0.5, post=1.0,
                        v=(lambda kt, r, i=i: VA[:, kt, 64 * (2 * i + r):64 * (2 * i + r) + 64]),
                        dst=(Gh[:, i, P * t:P * t + P], Gl[:, i, P * t:P * t + P]), gate=GT[:, i, P * t:P * t + P]))
            for i in range(3):
                for t in range(2):
                    jobs.append(Job(
                        q=[QZ[:, i, r, P * t:P * t + P] for r in range(2)],
                        k=[KQ[:, i, 0:KLEN[t]] for r in range(2)], nk=KLEN[t],
                        bias=AL[:, 2 * i:2 * i + 2, KOFF[t]:KOFF[t] + KLEN[t]], pre=0.125, post=1.0,
                        v=(lambda kt, r, i=i: V2[:, kt, 64 * (2 * i + r):64 * (2 * i + r) + 64]),
                        dst=(Gh[:, 3 + i, P * t:P * t + P], Gl[:, 3 + i, P * t:P * t + P]),
                        gate=GT[:, 3 + i, P * t:P * t + P]))
            for i in range(2):
                for t in range(2):
                    jobs.append(Job(
                        q=[QZ[:, 3 + i, r, P * t:P * t + P] for r in range(2)],
                        k=[KQ[:, 3 + i, 0:KLEN[t]] for r in range(2)], nk=KLEN[t],
                        bias=SB[:, 2 * i:2 * i + 2, KOFF[t]:KOFF[t] + KLEN[t]], pre=0.125, post=1.0,
                        v=(lambda kt, r, i=i: V2[:, kt, 384 + 64 * (2 * i + r):384 + 64 * (2 * i + r) + 64]),
                        dst=(Gh[:, 6 + i, P * t:P * t + P], Gl[:, 6 + i, P * t:P * t + P]),
                        gate=GT[:, 6 + i, P * t:P * t + P], fence=l + 1))
            J_B2.append((j0, len(jobs)))
        GJOB = {g: n for n, g in enumerate(g for g in range(len(jobs)) if jobs[g].gate is not None)}
        HL = {}
        for g in range(len(jobs)):
            HL[g] = sum(1 for j in jobs[:g + 1] if not j.diff)

        block = top.enter_context(nc.Block())


        for l in range(2):
            norms[f"q{l}"].ready = [("proj_out", p_a[l].o0 + 9), ("rope_out", p_a[l].r0 + 1)]

        @block.sync
        def _(sp):
            def weight(u, slot):
                if not isinstance(u, int) or u >= SLOTS:
                    sp.wait_ge(sem("w_lo"), u - (SLOTS - 1))
                src = wall[u] if isinstance(u, int) else wall[bass.ds(u, 1), :, :].rearrange("a p n -> p (a n)")
                sp.dma_start(raw[:, slot, :], src).then_inc(sem(f"w_landed{slot}"), 16)

            def ada_unit(a, slot):
                if not isinstance(a, int) or a >= ADA_SLOTS:
                    sp.wait_ge(sem("a_used"), a - (ADA_SLOTS - 1))
                src = aall[a] if isinstance(a, int) else aall[bass.ds(a, 1), :, :].rearrange("a p n -> p (a n)")
                sp.dma_start(aring[:, slot, :], src).then_inc(sem(f"a_landed{slot}"), 16)

            def mlp_loads(u0, a0):
                with sp.Fori(0, QUARTERS) as it:
                    for j in range(16):
                        weight(16 * it + (u0 + j), (u0 + j) % SLOTS)
                        if j % 2:
                            ada_unit(8 * it + (a0 + j // 2), (a0 + j // 2) % ADA_SLOTS)

            sp.dma_start(par[:, :], prm).then_inc(sem("par_landed"), 16)
            for a in range(ADA_SLOTS):
                ada_unit(a, a)
            sp.dma_start(cst[:, :], const).then_inc(sem("cst_landed"), 16)
            sp.dma_start(X[:, :, :], xin).then_inc(sem("x_landed"), 16)
            for u in range(SLOTS):
                weight(u, u)
            for a in range(ADA_SLOTS, 2 * KT):
                ada_unit(a, a % ADA_SLOTS)
            for qr in range(4):
                sp.dma_start(BI[64 * (qr % 2):64 * (qr % 2) + 64, qr // 2, :, :],
                             rpb[:, :, 64 * (3 - qr):64 * (3 - qr) + N]).then_inc(sem("rpb_landed"), 16)
            for u in range(SLOTS, U_L0_MLP):
                weight(u, u % SLOTS)
                i = u - SLOTS
                if i < 12:
                    for a in range(2 * KT * i // 12, 2 * KT * (i + 1) // 12):
                        ada_unit(2 * KT + a, a % ADA_SLOTS)
            mlp_loads(U_L0_MLP, 4 * KT)
            for u in range(U_L1, U_L1_MLP):
                weight(u, u % SLOTS)
            mlp_loads(U_L1_MLP, 8 * KT)
            for u in range(U_B2, UNITS):
                weight(u, u % SLOTS)
                if u == U_B2 + 8:
                    sp.wait_ge(sem("mlp_added"), 65)
                    sp.dma_start(AL[:, :, :], ali).then_inc(sem("ali_landed"), 16)
            sp.wait_ge(sem("modded"), norms["ln1"].t0 + 8)
            sp.dma_start(out, X[:, :, 0:N]).then_inc(sem("stored"), 16)
            sp.wait_ge(sem("stored"), 16)

        @block.scalar
        def _(act):
            def split_hi(u, slot, lap):
                act.wait_ge(sem(f"w_landed{slot}"), 16 * lap)
                if not isinstance(u, int) or u >= SLOTS:
                    act.wait_ge(sem("w_used"), u - (SLOTS - 1))
                act.activation(whi[:, slot, :], raw[:, slot, :], ACT.Copy).then_inc(sem("w_hi"), 1)

            def ahead(u):
                if u + AHEAD < UNITS:
                    v = u + AHEAD
                    split_hi(v, v % SLOTS, v // SLOTS + 1)

            def ada_rows(g):
                act.wait_ge(sem("a_used"), 8 * g + 8)
                if not isinstance(g, int) or g:
                    act.wait_ge(sem("ada_tr"), g)
                act.activation(AR[:, :], ps[:, 6, 0:ADA_N], ACT.Copy).then_inc(sem("ar_ready"), 1)

            def squares(n):
                for name, value in n.ready:
                    act.wait_ge(sem(name), value)
                for k in range(n.n):
                    t = n.t0 + k
                    if t >= 4:
                        act.wait_ge(sem("ss"), t - 3)
                    act.activation(SQ[:, t % 4, 0:n.T], n.src(k, n.T), ACT.Square).then_inc(sem("sq"), 1)

            def his(n):
                for k in range(n.n):
                    act.wait_ge(sem("modded"), n.t0 + k + 1)
                    for c0, _, shift in n.streams:
                        c1 = min(c0 + N, n.T)
                        o, m = n.dst[0](k)[:, c0:c1], M[:, (n.t0 + k) % 2, c0:c1]
                        if n.keep or shift is None:
                            ins = act.activation(o, m, ACT.Copy)
                        else:
                            ins = act.activation(o, m, ACT.Identity, bias=shift(k))
                    ins.then_inc(sem("nhi"), 1)

            def evac(pr, i):
                t, o = pr.tiles[i], pr.o0 + i
                act.wait_ge(sem("w_used"), pr.u0 + i + 1)
                bank = ps[:, o % 4, :]
                if t.rope is None:
                    for p, dst in t.dst:
                        ins = act.activation(dst, bank[p, 0:t.T], ACT.Copy)
                    ins.then_inc(sem("proj_out"), 1)
                    return
                r = pr.rope_index(i)
                n = 128 if t.rope == "q" else 96
                if r >= 2:
                    act.wait_ge(sem("rope_out"), r - 1)
                ins = act.activation(wk1[0:n, r % 2, 0:N], bank[0:n, 0:N], ACT.Copy)
                for p, dst in t.rest:
                    ins = act.activation(dst, bank[p, N:2 * N], ACT.Copy)
                ins.then_inc(sem("proj_out"), 1)

            def evac_v(u, o0, dsts):
                act.wait_ge(sem("w_used"), u + 1)
                for t, dst in enumerate(dsts):
                    act.activation(dst, ps[:, (o0 + t) % 4, 0:dst.shape[1]], ACT.Copy).then_inc(sem("proj_out"), 1)

            def attend(j0, j1):
                for s in range(j0, j1 + 3):
                    if j0 <= s - 2 < j1:
                        g = s - 2
                        act.wait_ge(sem("t_done"), g + 1)
                        if g >= 2:
                            act.wait_ge(sem("pv_done"), g - 1)
                        act.activation(PT[:, g % 2, 0, 0:jobs[g].nk], ps[:, 4, 0:jobs[g].nk], ACT.Copy)\
                           .then_inc(sem("ev_a"), 1)
                    if j0 <= s - 3 < j1:
                        g = s - 3
                        j = jobs[g]
                        if j.diff:
                            act.wait_ge(sem("pv_done"), g + 1)
                            act.activation(j.dst, ps[:, 6 + g % 2, 0:P], ACT.Copy).then_inc(sem("oy"), 1)
                        elif j.gate is None:
                            act.wait_ge(sem("pv_done"), g + 1)
                            act.activation(j.dst[0], ps[:, 6 + g % 2, 0:P], ACT.Copy).then_inc(sem("o_hi"), 1)
                        else:
                            act.wait_ge(sem("o_m"), GJOB[g] + 1)
                            act.activation(j.dst[0], MO[:, g % 2, :], ACT.Copy).then_inc(sem("o_hi"), 1)
                    if s < j1:
                        j = jobs[s]
                        act.wait_ge(sem("m_done"), s + 1)
                        if s >= 2:
                            act.wait_ge(sem("t_done"), s - 1)
                        st = small[:, s % 2, :]
                        if j.sink is not None:
                            act.activation(st[:, 8:10], st[:, 8:10], ACT.Exp)
                        for r in range(2):
                            ins = act.activation(E[:, s % 2, r, 0:j.nk], ps[:, 2 * (s % 2) + r, 0:j.nk], ACT.Exp,
                                                 bias=st[:, 2 + r:3 + r], scale=j.post,
                                                 accum_out=st[:, 4 + r:5 + r])
                        ins.then_inc(sem("x_done"), 1)

            def mlp(u0, h0, T, g0):
                with act.Fori(0, QUARTERS) as it:
                    for j in range(16):
                        v = u0 + j + AHEAD
                        split_hi(16 * it + v, v % SLOTS, 4 * it + (v // SLOTS + 1))
                        if j < 8:
                            act.wait_ge(sem("w_used"), 16 * it + (u0 + j + 1))
                            act.wait_ge(sem("hid"), 8 * it + (h0 + j + 1))
                            act.activation(Y[:, j % 2, 0:T], ps[:, j % 2, 0:T], ACT.Relu).then_inc(sem("hid_r"), 1)
                            act.wait_ge(sem("hid_r"), 8 * it + (h0 + j + 1))
                            act.activation(HIDh[:, j, 0:T], Y[:, j % 2, 0:T], ACT.Square).then_inc(sem("hid_h"), 1)
                    ada_rows(1 * it + g0)

            act.wait_ge(sem("par_landed"), 16)
            act.activation(stp[:, 0, :, :], par[:, P_CV:P_CV + 24].rearrange("p (k v) -> p k v", v=3), ACT.Exp,
                           scale=-1.0).then_inc(sem("silu_e"), 1)
            for v in range(AHEAD):
                split_hi(v, v, 1)
            act.wait_ge(sem("lam_sum"), 1)
            act.activation(lam[:, 2:4], ps[:, 5, 0:2], ACT.Exp).then_inc(sem("lam_e"), 1)
            squares(norms["l0a"])
            for g in range(2):
                ada_rows(g)
            his(norms["l0a"])
            for i in range(L0_FM):
                ahead(U_L0 + i)
                evac(p_l0, i)
                if i == 5:
                    ada_rows(2)
            for h in range(2):
                ahead(U_L0 + L0_FM + h)
            evac_v(U_L0 + L0_FM + 1, V_L0, [V0[:, t, :] for t in range(4)])
            ada_rows(3)
            attend(*J_L0)
            for i in range(KT):
                ahead(U_L0_OUT + i)
            squares(norms["l0b"])
            his(norms["l0b"])
            mlp(U_L0_MLP, 0, 512, 4)
            squares(norms["l1a"])
            his(norms["l1a"])
            for i in range(L1_FM):
                ahead(U_L1 + i)
                evac(p_l1, i)
            for c in range(4):
                u = U_L1 + L1_FM + 2 * c
                ahead(u)
                ahead(u + 1)
                evac_v(u + 1, V_L1 + 4 * c, [V1[:, t, N * c:N * c + N] for t in range(4)])
            attend(*J_L1)
            act.wait_ge(sem("oy"), 16)
            for k in range(8):
                if k >= 4:
                    act.wait_ge(sem("sub_ss"), k - 3)
                act.activation(SQ[:, k % 4, 0:N], OY(k), ACT.Square).then_inc(sem("sub_sq"), 1)
            for k in range(8):
                act.wait_ge(sem("sub_y"), k + 1)
                act.activation(Hh[:, k, 0:N], OY(k), ACT.Copy).then_inc(sem("sub_hi"), 1)
            for i in range(KT):
                ahead(U_L1_OUT + i)
            squares(norms["l1b"])
            his(norms["l1b"])
            mlp(U_L1_MLP, 32, 256, 8)
            squares(norms["fin"])
            his(norms["fin"])
            for l in range(2):
                u0 = U_B2 + l * B2_UNITS
                for i in range(B2_FM1):
                    ahead(u0 + i)
                    evac(p_a[l], i)
                act.wait_ge(sem("rope_out"), p_a[l].r0 + 1)
                if l == 0:
                    act.wait_ge(sem("b2_zeros"), 1)
                for r in range(2):
                    ins = act.activation(KI[rows(r), r, :], KK[0:64, :], ACT.Copy)
                ins.then_inc(sem("ki_shift"), 1)
                squares(norms[f"q{l}"])
                squares(norms[f"kv{l}"])
                for i in range(4):
                    ahead(u0 + 9 + i)
                    evac(p_b[l], i)
                his(norms[f"q{l}"])
                for i in range(4, 7):
                    ahead(u0 + 9 + i)
                    evac(p_b[l], i)
                his(norms[f"kv{l}"])
                for i in range(7, B2_FM2):
                    ahead(u0 + 9 + i)
                    evac(p_b[l], i)
                for c in range(3):
                    u = u0 + 23 + 2 * c
                    ahead(u)
                    ahead(u + 1)
                    evac_v(u + 1, V_B2[l] + 2 * c, [V2[:, t, N * c:N * c + N] for t in range(2)])
                for i in range(KT):
                    u = u0 + 29 + i
                    ahead(u)
                    act.wait_ge(sem("w_used"), u + 1)
                    bank = ps[:, (p_g[l].o0 + i) % 4, 0:N]
                    act.activation(PQ[:, i, :], bank, ACT.Exp, scale=-1.0)
                    act.activation(GT[:, i, :], bank, ACT.Copy).then_inc(sem("proj_out"), 1)
                for i in range(6):
                    ahead(u0 + 37 + i)
                    evac(p_uq[l], i)
                ahead(u0 + 43)
                act.wait_ge(sem("w_used"), u0 + 44)
                for i in range(3):
                    bank = ps[:, (p_uk[l] + i) % 4, 0:N]
                    act.activation(KA[0:64, 2 * i, :], bank[0:64, :], ACT.Copy)
                    act.activation(KA[0:64, 2 * i + 1, :], bank[64:128, :], ACT.Copy).then_inc(sem("proj_out"), 1)
                ahead(u0 + 44)
                evac_v(u0 + 44, V_UV[l], [VA[:, t, :] for t in range(2)])
                act.wait_ge(sem("ix_ps"), l + 1)
                for b in range(4):
                    h = 4 * (b % 2) + b // 2
                    act.activation(RI[:, h:h + 3:2, P:3 * P], ps[:, b, :].rearrange("p (h n) -> p h n", h=2),
                                   ACT.Relu, scale=0.125)
                for b in range(2):
                    ins = act.activation(RI[:, b:b + 7:2, 0:P],
                                         ps[:, 4 + b, :].rearrange("p (h n) -> p h n", h=4), ACT.Relu, scale=0.125)
                ins.then_inc(sem("ri"), 1)
                attend(*J_B2[l])
                for i in range(KT):
                    ahead(u0 + 45 + i)
                squares(norms[f"ln{l}"])
                if l == 0:
                    his(norms["ln0"])

        @block.vector
        def _(dve):
            linked = [0]

            def link(ins):
                linked[0] += 1
                ins.then_inc(sem("dve_link"), 1)
                dve.wait_ge(sem("dve_link"), linked[0])

            def split_lo(u, slot):
                dve.wait_ge(sem("w_hi"), u + 1)
                dve.tensor_tensor(wlo[:, slot, :], raw[:, slot, :], whi[:, slot, :].bitcast(F32), ALU.subtract)\
                   .then_inc(sem("w_lo"), 1)

            def ahead(u):
                if u + AHEAD < UNITS:
                    split_lo(u + AHEAD, (u + AHEAD) % SLOTS)

            def ada_cols(g, s, gl, vecs):
                dve.wait_ge(sem("ada_tr"), g + 1)
                src = ps[:, 7, 0:ADA_N].rearrange("p (c j r) -> p r j c", c=3, j=4)
                for v in vecs:
                    if isinstance(gl, int):
                        dst = ada[:, s, v, 12 * gl:12 * gl + 12]
                        bias = par[:, P_AB + 48 * s + 12 * gl:P_AB + 48 * s + 12 * gl + 12]
                    else:
                        dst = ada[:, s, v, bass.ds(12 * gl, 12)]
                        bias = par[:, bass.ds(12 * gl + (P_AB + 48 * s), 12)]
                    ins = dve.tensor_tensor(dst.rearrange("p (j c) -> p j c", j=4), src[:, v, :, :],
                                            bias.rearrange("p (j c) -> p j c", j=4), ALU.add)
                ins.then_inc(sem("ada_ready"), 1)

            def scale_row(row, s, v, t0, gain):
                src = ada[:, s, v, t0:t0 + 8]
                if gain is None:
                    link(dve.tensor_scalar(SC[:, row, :], src, 1.0, None, ALU.add))
                else:
                    link(dve.scalar_tensor_tensor(SC[:, row, :], src, 1.0, par[:, gain:gain + 8], ALU.add, ALU.mult))

            def variance(n):
                dve.wait_ge(sem("ss"), n.t0 + n.n)
                for t in range(n.T // P):
                    link(dve.tensor_tensor_reduce(RS[:, P * t:P * t + P], ps[:, 7, P * t:P * t + P], ident, 1.0, 0.0,
                                                  ALU.mult, ALU.add, VR[:, 0, t:t + 1]))
                dve.tensor_scalar(VR[:, 0, 0:n.T // P], VR[:, 0, 0:n.T // P], 1.0 / n.width, n.eps, ALU.mult, ALU.add)\
                   .then_inc(sem("var"), 1)

            def diagonals(n):
                dve.wait_ge(sem("rstd"), n.idx + 1)
                for t in range(n.T // P):
                    ins = dve.tensor_scalar(RS[:, P * t:P * t + P], ident, VR[:, 1, t:t + 1], None, ALU.mult)
                ins.then_inc(sem("diag"), 1)

            def modulate(n):
                root = ps[:, 7, :]

                def lo(k):
                    dve.wait_ge(sem("nhi"), n.h0 + k + 1)
                    m = M[:, (n.t0 + k) % 2, :]
                    for c0, _, shift in n.streams:
                        c1 = min(c0 + N, n.T)
                        h, o = n.dst[0](k)[:, c0:c1].bitcast(F32), n.dst[1](k)[:, c0:c1]
                        if n.keep or shift is None:
                            ins = dve.tensor_tensor(o, m[:, c0:c1], h, ALU.subtract)
                        else:
                            ins = dve.scalar_tensor_tensor(o, m[:, c0:c1], shift(k), h, ALU.add, ALU.subtract)
                    ins.then_inc(sem("nlo"), 1)

                dve.wait_ge(sem("spread"), n.idx + 1)
                for k in range(n.n):
                    t = n.t0 + k
                    if n.dst and n.h0 + k > 1:
                        dve.wait_ge(sem("nlo"), n.h0 + max(k - 1, 0))
                    src = n.src(k, n.T)
                    if n.keep:
                        x, g, b = n.keep[0](k), n.keep[1](k), n.keep[2]
                        ins = dve.scalar_tensor_tensor(x, src, g, root[:, 0:n.T], ALU.mult, ALU.mult)
                        if b is not None:
                            link(ins)
                            ins = dve.tensor_scalar(x, x, b(k), None, ALU.add)
                        if n.streams:
                            link(ins)
                            ins = dve.tensor_scalar(M[:, t % 2, 0:n.T], x, n.streams[0][1](k), n.streams[0][2](k),
                                                    ALU.mult, ALU.add)
                    else:
                        for c0, scale, _ in n.streams:
                            c1 = min(c0 + N, n.T)
                            ins = dve.scalar_tensor_tensor(M[:, t % 2, c0:c1], src[:, c0:c1], scale(k), root[:, c0:c1],
                                                           ALU.mult, ALU.mult)
                    ins.then_inc(sem("modded"), 1)
                    if n.dst and k:
                        lo(k - 1)
                if n.dst:
                    lo(n.n - 1)

            def rope(pr, i):
                t = pr.tiles[i]
                r = pr.rope_index(i)
                n, c, s = (128, C_COS, C_SIN) if t.rope == "q" else (96, C_COSM, C_SINM)
                dve.wait_ge(sem("rope_rot"), r + 1)
                if r >= 2:
                    dve.wait_ge(sem("rope_out"), r - 1)
                link(dve.tensor_tensor(wk1[0:n, 2 + r % 2, 0:N], wk1[0:n, r % 2, 0:N], cst[0:n, c:c + N], ALU.mult))
                link(dve.tensor_tensor(wk1[0:n, r % 2, 0:N], ps[0:n, 4 + r % 2, 0:N], cst[0:n, s:s + N], ALU.mult))
                for p, dst in t.dst:
                    ins = dve.tensor_tensor(dst, wk1[p, 2 + r % 2, 0:N], wk1[p, r % 2, 0:N], ALU.add)
                ins.then_inc(sem("rope_out"), 1)

            def steps(pr, lo, hi):
                for i in range(lo, hi):
                    ahead(pr.u0 + i)
                    if i and pr.tiles[i - 1].rope:
                        rope(pr, i - 1)
                if hi == len(pr.tiles) and pr.tiles[-1].rope:
                    rope(pr, hi - 1)

            def attend(j0, j1, side=None):
                for s in range(j0, j1 + 4):
                    if j0 <= s - 4 < j1:
                        g = s - 4
                        j = jobs[g]
                        if not j.diff:
                            dve.wait_ge(sem("o_hi"), HL[g])
                            src = MO[:, g % 2, :] if j.gate is not None else ps[:, 6 + g % 2, 0:P]
                            dve.tensor_tensor(j.dst[1], src, j.dst[0].bitcast(F32), ALU.subtract)\
                               .then_inc(sem("o_lo"), 1)
                    if j0 <= s - 3 < j1 and jobs[s - 3].gate is not None:
                        g = s - 3
                        dve.wait_ge(sem("pv_done"), g + 1)
                        if g - 2 >= j0:
                            dve.wait_ge(sem("o_lo"), HL[g - 2])
                        dve.tensor_tensor(MO[:, g % 2, :], ps[:, 6 + g % 2, 0:P], jobs[g].gate, ALU.mult)\
                           .then_inc(sem("o_m"), 1)
                    if j0 <= s - 2 < j1 and not jobs[s - 2].diff:
                        g = s - 2
                        dve.wait_ge(sem("t_done"), g + 1)
                        if g >= 2:
                            dve.wait_ge(sem("pv_done"), g - 1)
                        dve.tensor_copy(PT[:, g % 2, 1, 0:jobs[g].nk], ps[:, 5, 0:jobs[g].nk]).then_inc(sem("ev_v"), 1)
                    if j0 <= s - 1 < j1:
                        g = s - 1
                        j = jobs[g]
                        st = small[:, g % 2, :]
                        dve.wait_ge(sem("x_done"), g + 1)
                        if j.sink is not None:
                            link(dve.tensor_tensor(st[:, 4:6], st[:, 4:6], st[:, 8:10], ALU.add))
                        ins = dve.reciprocal(st[:, 6:8], st[:, 4:6])
                        if j.diff:
                            link(ins)
                            ins = dve.tensor_tensor(st[:, 7:8], st[:, 7:8], lam[:, 4:5], ALU.mult)
                        ins.then_inc(sem("rc_done"), 1)
                        dve.wait_ge(sem("rc_done"), g + 1)
                        e0, e1 = E[:, g % 2, 0, 0:j.nk], E[:, g % 2, 1, 0:j.nk]
                        if j.diff:
                            dve.wait_ge(sem("n_p"), g + 1)
                            ins = dve.scalar_tensor_tensor(e0, e0, st[:, 6:7], e1, ALU.mult, ALU.subtract)
                        else:
                            ins = dve.tensor_scalar(e0, e0, st[:, 6:7], None, ALU.mult)
                        ins.then_inc(sem("n_v"), 1)
                    if s < j1:
                        j = jobs[s]
                        st = small[:, s % 2, :]
                        dve.wait_ge(sem("s_done"), s + 1)
                        if j.fence:
                            dve.wait_ge(sem("sb_done"), j.fence)
                        b0 = 2 * (s % 2)
                        if j.bias is not None:
                            nb = j.bias.shape[2]
                            w = ps[:, b0:b0 + 2, 0:nb]
                            if j.pre == 1.0:
                                link(dve.tensor_tensor(w, w, j.bias, ALU.add))
                            else:
                                link(dve.scalar_tensor_tensor(w, w, j.pre, j.bias, ALU.mult, ALU.add))
                        link(dve.tensor_reduce(st[:, 0:2], ps[:, b0:b0 + 2, 0:j.nk], AX.X, ALU.max))
                        if j.sink is None:
                            dve.tensor_scalar(st[:, 2:4], st[:, 0:2], -j.post, None, ALU.mult)\
                               .then_inc(sem("m_done"), 1)
                        else:
                            link(dve.scalar_tensor_tensor(st[:, 2:4], st[:, 0:2], -j.post,
                                                          nsink[:, j.sink:j.sink + 2], ALU.mult, ALU.min))
                            dve.tensor_tensor(st[:, 8:10], st[:, 2:4], nsink[:, j.sink:j.sink + 2], ALU.subtract)\
                               .then_inc(sem("m_done"), 1)
                    if side:
                        side(s - j0)

            def topk(l):
                def side(s):
                    if s in (0, 1):
                        sl = slice(KOFF[s], KOFF[s] + KLEN[s])
                        if s == 0:
                            dve.wait_ge(sem("ri"), l + 1)
                            link(dve.tensor_scalar(WI[:, :, :], V2[:, :, 640:648], 8 ** -0.5, None, ALU.mult))
                        link(dve.tensor_scalar(IX[:, sl], RI[:, 0, sl], WI[:, s, 0:1], None, ALU.mult))
                        for h in range(1, 8):
                            link(dve.scalar_tensor_tensor(IX[:, sl], RI[:, h, sl], WI[:, s, h:h + 1], IX[:, sl],
                                                          ALU.mult, ALU.add))
                        link(dve.tensor_tensor(IX[:, sl], IX[:, sl], cst[:, C_CAU + KOFF[s]:C_CAU + KOFF[s] + KLEN[s]],
                                               ALU.add))
                    elif s < 2 + TOPK // 8:
                        for t in range(2):
                            w = IX[:, KOFF[t]:KOFF[t] + KLEN[t]]
                            link(dve.max(M8[:, 8 * t:8 * t + 8], w))
                            link(dve.match_replace(w, M8[:, 8 * t:8 * t + 8], w, TAKEN))
                    elif s == 2 + TOPK // 8:
                        dve.tensor_scalar(SEL[:, :], IX[:, :], -2.0e38, NEG, ALU.is_gt, ALU.mult)\
                           .then_inc(sem("sel_done"), 1)
                return side

            def add_out(u0, o0, add):
                for i in range(KT):
                    ahead(u0 + i)
                    dve.wait_ge(sem("w_used"), u0 + i + 1)
                    add(i, ps[:, i % 4, :]).then_inc(sem("out_added"), 1)

            def gated(s, t0, T):
                def add(i, bank):
                    for v in range(T // N):
                        x = X[:, i, N * v:N * v + N]
                        ins = dve.scalar_tensor_tensor(x, bank[:, N * v:N * v + N], adacol(s, v, t0 + i), x,
                                                       ALU.mult, ALU.add)
                    return ins
                return add

            def mlp(u0, h0, T, s, g0, s_next, vecs):
                with dve.Fori(0, QUARTERS) as it:
                    def lo(j):
                        dve.wait_ge(sem("hid_h"), 8 * it + (h0 + j + 1))
                        dve.tensor_tensor(HIDl[:, j, 0:T], M[:, j % 2, 0:T], HIDh[:, j, 0:T].bitcast(F32),
                                          ALU.subtract).then_inc(sem("hid"), 1)
                    for j in range(16):
                        v = u0 + j + AHEAD
                        split_lo(16 * it + v, v % SLOTS)
                        if j < 8:
                            dve.wait_ge(sem("hid_r"), 8 * it + (h0 + j + 1))
                            dve.wait_ge(sem("hid"), 8 * it + (h0 + j + 1))
                            dve.tensor_tensor(M[:, j % 2, 0:T], Y[:, j % 2, 0:T], Y[:, j % 2, 0:T], ALU.mult)\
                               .then_inc(sem("hid_a"), 1)
                            dve.wait_ge(sem("hid_a"), 8 * it + (h0 + j + 1))
                            lo(j)
                        else:
                            i = j - 8
                            dve.wait_ge(sem("w_used"), 16 * it + (u0 + j + 1))
                            gated(s, 40, T)(i, ps[:, 2 + i % 2, :]).then_inc(sem("mlp_added"), 1)
                    ada_cols(1 * it + g0, s_next, it, vecs)

            dve.memset(scs[:, :, :], 0.0).then_inc(sem("dve_link"), 1)
            linked[0] += 1
            dve.memset(mhalf[:, :], -0.5).then_inc(sem("mhalf_set"), 1)
            dve.memset(lam[:, 5:6], 0.0).then_inc(sem("hid"), 1)
            dve.memset(lam[:, 6:7], 0.0).then_inc(sem("hid"), 1)
            dve.memset(lam[:, 7:8], 0.0).then_inc(sem("mlp_added"), 1)
            dve.wait_ge(sem("silu_e"), 1)
            link(dve.tensor_scalar(stp[:, 1, :, :], stp[:, 0, :, :], 1.0, None, ALU.add))
            link(dve.reciprocal(stp[:, 0, :, :], stp[:, 1, :, :]))
            dve.tensor_tensor(scs[:, :, 0:3], par[:, P_CV:P_CV + 24].rearrange("p (k v) -> p k v", v=3),
                              stp[:, 0, :, :], ALU.mult).then_inc(sem("scs_ready"), 1)
            link(dve.tensor_scalar(nsink[:, :], par[:, P_SINK:P_SINK + 8], -1.0, None, ALU.mult))
            dve.tensor_tensor(lam[:, 0:2], par[:, P_LAM:P_LAM + 2], par[:, P_LAM + 2:P_LAM + 4], ALU.mult)\
               .then_inc(sem("lam_prod"), 1)
            link(dve.tensor_scalar(SC[:, 12, 0:1], par[:, P_SUB:P_SUB + 1], 1.0 - LAM_INIT, None, ALU.mult))
            for u in range(AHEAD):
                split_lo(u, u)
            dve.wait_ge(sem("lam_e"), 1)
            link(dve.tensor_tensor(lam[:, 4:5], lam[:, 2:3], lam[:, 3:4], ALU.subtract))
            link(dve.tensor_scalar(lam[:, 4:5], lam[:, 4:5], LAM_INIT, None, ALU.add))
            variance(norms["l0a"])
            diagonals(norms["l0a"])
            for g in range(2):
                ada_cols(g, 0, g, (0, 1))
            dve.wait_ge(sem("ada_ready"), 2)
            scale_row(0, 0, 0, 8, P_N1)
            scale_row(1, 0, 1, 8, P_N1)
            modulate(norms["l0a"])
            steps(p_l0, 0, 8)
            ada_cols(2, 0, 2, (0, 1))
            steps(p_l0, 8, L0_FM)
            for h in range(2):
                ahead(U_L0 + L0_FM + h)
            ada_cols(3, 0, 3, (0, 1))
            dve.wait_ge(sem("rpb_done"), 1)
            attend(*J_L0)
            dve.wait_ge(sem("ada_ready"), 4)
            add_out(U_L0_OUT, 0, gated(0, 16, 512))
            scale_row(2, 0, 0, 32, P_N2)
            scale_row(3, 0, 1, 32, P_N2)
            variance(norms["l0b"])
            diagonals(norms["l0b"])
            modulate(norms["l0b"])
            mlp(U_L0_MLP, 0, 512, 0, 4, 1, (0, 1))
            dve.wait_ge(sem("ada_ready"), 8)
            scale_row(4, 1, 0, 8, P_N1 + 8)
            scale_row(5, 1, 1, 8, P_N1 + 8)
            scale_row(6, 1, 0, 32, P_N2 + 8)
            variance(norms["l1a"])
            diagonals(norms["l1a"])
            modulate(norms["l1a"])
            steps(p_l1, 0, L1_FM)
            for v in range(8):
                ahead(U_L1 + L1_FM + v)
            attend(*J_L1)
            for k in range(8):
                dve.wait_ge(sem("sub_ss"), 2 * (k // 2) + 2)
                for t in range(2):
                    c = N * (k % 2) + P * t
                    link(dve.tensor_tensor_reduce(RS[:, P * t:P * t + P], ps[:, k // 2, c:c + P], ident, 1.0, 0.0,
                                                  ALU.mult, ALU.add, VS[:, 0, 2 * k + t:2 * k + t + 1]))
            dve.tensor_scalar(VS[:, 0, :], VS[:, 0, :], 1.0 / P, 1e-6, ALU.mult, ALU.add).then_inc(sem("sub_var"), 1)
            dve.wait_ge(sem("sub_rs"), 1)
            for b in range(4):
                for c in range(4):
                    ins = dve.tensor_scalar(wk2[:, b, P * c:P * c + P], ident, VS[:, 1, 4 * b + c:4 * b + c + 1], None,
                                            ALU.mult)
                ins.then_inc(sem("sub_diag"), 1)
            for k in range(8):
                dve.wait_ge(sem("sub_spread"), k // 2 + 1)
                dve.scalar_tensor_tensor(OY(k), OY(k), SC[:, 12, 0:1],
                                         ps[:, k // 2, N * (k % 2):N * (k % 2) + N], ALU.mult, ALU.mult)\
                   .then_inc(sem("sub_y"), 1)
            for k in range(8):
                dve.wait_ge(sem("sub_hi"), k + 1)
                dve.tensor_tensor(Hl[:, k, 0:N], OY(k), Hh[:, k, 0:N].bitcast(F32), ALU.subtract)\
                   .then_inc(sem("sub_lo"), 1)
            add_out(U_L1_OUT, 8, gated(1, 16, 256))
            variance(norms["l1b"])
            diagonals(norms["l1b"])
            modulate(norms["l1b"])
            mlp(U_L1_MLP, 32, 256, 1, 8, 2, (2,))
            dve.wait_ge(sem("ada_ready"), 12)
            scale_row(8, 2, 2, 8, None)
            scale_row(9, 2, 2, 32, None)
            scale_row(10, 2, 2, 16, None)
            scale_row(11, 2, 2, 40, None)
            variance(norms["fin"])
            diagonals(norms["fin"])
            modulate(norms["fin"])
            for l in range(2):
                u0 = U_B2 + l * B2_UNITS
                steps(p_a[l], 0, B2_FM1)
                steps(p_b[l], 0, 2)
                variance(norms[f"q{l}"])
                diagonals(norms[f"q{l}"])
                steps(p_b[l], 2, 4)
                modulate(norms[f"q{l}"])
                steps(p_b[l], 4, 5)
                variance(norms[f"kv{l}"])
                diagonals(norms[f"kv{l}"])
                steps(p_b[l], 5, 7)
                modulate(norms[f"kv{l}"])
                steps(p_b[l], 7, B2_FM2)
                for v in range(6):
                    ahead(u0 + 23 + v)
                for i in range(KT):
                    ahead(u0 + 29 + i)
                    dve.wait_ge(sem("proj_out"), p_g[l].o0 + i + 1)
                    link(dve.tensor_scalar(PQ[:, i, :], PQ[:, i, :], 1.0, None, ALU.add))
                    link(dve.reciprocal(PQ[:, i, :], PQ[:, i, :]))
                    dve.tensor_tensor(GT[:, i, :], GT[:, i, :], PQ[:, i, :], ALU.mult)
                steps(p_uq[l], 0, 6)
                ahead(u0 + 43)
                ahead(u0 + 44)
                if l == 0:
                    dve.wait_ge(sem("ali_landed"), 16)
                attend(*J_B2[l], side=topk(l))

                def add(i, bank, l=l):
                    x = X[:, i, 0:N]
                    link(dve.tensor_scalar(x, x, ALPHA, None, ALU.mult))
                    return dve.scalar_tensor_tensor(x, bank[:, 0:N], SC[:, 10 + l, i:i + 1], x, ALU.mult, ALU.add)
                add_out(u0 + 45, 16 + 8 * l, add)
                dve.wait_ge(sem("mean_sum"), l + 1)
                link(dve.tensor_scalar(RS[:, 0:N], ps[:, 7, 0:N], 1.0 / D, None, ALU.mult))
                for k in range(KT):
                    dve.tensor_tensor(X[:, k, 0:N], X[:, k, 0:N], RS[:, 0:N], ALU.subtract)\
                       .then_inc(sem("centred"), 1)
                variance(norms[f"ln{l}"])
                diagonals(norms[f"ln{l}"])
                modulate(norms[f"ln{l}"])

        @block.gpsimd
        def _(pool):
            def root(dst, src, T):
                return pool.tensor_tensor(dst, src, mhalf[:, 0:1].to_broadcast([P, T]), ALU.pow)

            def roots(n):
                pool.wait_ge(sem("var"), n.idx + 1)
                root(VR[:, 1, 0:n.T // P], VR[:, 0, 0:n.T // P], n.T // P).then_inc(sem("rstd"), 1)

            def attend(j0, j1):
                for g in range(j0, j1):
                    j = jobs[g]
                    pool.wait_ge(sem("rc_done"), g + 1)
                    e = E[:, g % 2, 1, 0:j.nk]
                    pool.tensor_scalar(e, e, small[:, g % 2, 7:8], None, ALU.mult).then_inc(sem("n_p"), 1)

            def zeros(pairs, name):
                for ap in pairs:
                    for r in range(2):
                        ins = pool.memset(ap(r)[rows(1 - r)], 0.0)
                ins.then_inc(sem(name), 1)

            zeros([lambda r: K0[:, :, r, :]], "l0_zeros")
            pool.wait_ge(sem("l0_zeros"), 1)
            pool.wait_ge(sem("mhalf_set"), 1)
            roots(norms["l0a"])
            pool.wait_ge(sem("rpb_landed"), 16 * 4)
            pool.wait_ge(sem("cst_landed"), 16)
            for t in range(2):
                pool.tensor_scalar(BI[:, t, :, :], BI[:, t, :, :], 8.0, None, ALU.mult).then_inc(sem("rpb_x8"), 1)
            pool.wait_ge(sem("rpb_x8"), 2)
            for t in range(2):
                ins = pool.tensor_tensor(BI[:, t, :, :], BI[:, t, :, :],
                                         cst[:, None, C_NBR + N * t:C_NBR + N * t + N].to_broadcast([P, 8, N]), ALU.add)
            ins.then_inc(sem("rpb_done"), 1)
            attend(*J_L0)
            roots(norms["l0b"])
            roots(norms["l1a"])
            pool.wait_ge(sem("nlo"), norms["l1a"].h0 + 8)
            zeros([lambda r: Q1[:, :, r, :]], "l1_zeros")
            pool.wait_ge(sem("l1_zeros"), 1)
            attend(*J_L1)
            pool.wait_ge(sem("sub_var"), 1)
            root(VS[:, 1, :], VS[:, 0, :], 16).then_inc(sem("sub_rs"), 1)
            roots(norms["l1b"])
            roots(norms["fin"])
            pool.wait_ge(sem("nlo"), norms["fin"].h0 + 8)
            zeros([lambda r: QZ[:, :, r, :], lambda r: KI[:, r, :]], "b2_zeros")
            pool.wait_ge(sem("b2_zeros"), 1)
            for l in range(2):
                pool.wait_ge(sem("rope_out"), p_a[l].r0 + 1)
                pool.tensor_copy(KA[64:96, :, :], KK[64:96, None, :].to_broadcast([32, 6, N])).then_inc(sem("kr_done"), 1)
                pool.wait_ge(sem("kr_done"), l + 1)
                roots(norms[f"q{l}"])
                roots(norms[f"kv{l}"])
                j0, j1 = J_B2[l]
                attend(j0, j0 + 10)
                pool.wait_ge(sem("sel_done"), l + 1)
                pool.tensor_tensor(SB[:, :, :], AL[:, 6:10, :], SEL[:, None, :].to_broadcast([P, 4, 384]), ALU.add)\
                    .then_inc(sem("sb_done"), 1)
                attend(j0 + 10, j1)
                roots(norms[f"ln{l}"])

        @block.tensor
        def _(pe):
            def mm3(o, a, b, first, last):
                pe.matmul(o, a[0], b[0], start=first, stop=False)
                pe.matmul(o, a[0], b[1], start=False, stop=False)
                return pe.matmul(o, a[1], b[0], start=False, stop=last)

            def wtile(slot, c0, n):
                return whi[:, slot, c0:c0 + n], wlo[:, slot, c0:c0 + n]

            def ada_mm(a, kt, slot, lap, g):
                pe.wait_ge(sem(f"a_landed{slot}"), 16 * lap)
                if kt == 0 and (not isinstance(g, int) or g):
                    pe.wait_ge(sem("ar_ready"), g)
                for j in range(4):
                    ins = pe.matmul(ps[32 * j:32 * j + 32, 6, 0:ADA_N], scs[:, kt, :],
                                    aring[:, slot, ADA_N * j:ADA_N * j + ADA_N], start=(kt == 0), stop=(kt == KT - 1))
                ins.then_inc(sem("a_used"), 1)

            def ada_turn(g):
                pe.wait_ge(sem("ar_ready"), g + 1)
                if not isinstance(g, int) or g:
                    pe.wait_ge(sem("ada_ready"), g)
                for c in range(3):
                    ins = pe.transpose(ps[:, 7, P * c:P * c + P], AR[:, P * c:P * c + P], ident)
                ins.then_inc(sem("ada_tr"), 1)

            def sums(n):
                if n.idx:
                    pe.wait_ge(sem("modded"), n.t0)
                for k in range(n.n):
                    t = n.t0 + k
                    pe.wait_ge(sem("sq"), t + 1)
                    pe.matmul(ps[:, 7, 0:n.T], ones, SQ[:, t % 4, 0:n.T], start=(k == 0), stop=(k == n.n - 1))\
                      .then_inc(sem("ss"), 1)

            def spread(n):
                pe.wait_ge(sem("diag"), n.idx + 1)
                pe.matmul(ps[:, 7, 0:n.T], ones, RS[:, 0:n.T], start=True, stop=True).then_inc(sem("spread"), 1)

            def rot(pr, i):
                t = pr.tiles[i]
                if t.rope is None:
                    return
                r = pr.rope_index(i)
                n, c = (128, C_RQ) if t.rope == "q" else (96, C_RM)
                pe.wait_ge(sem("proj_out"), pr.o0 + i + 1)
                if r >= 2:
                    pe.wait_ge(sem("rope_out"), r - 1)
                pe.matmul(ps[0:n, 4 + r % 2, 0:N], cst[0:n, c:c + n], wk1[0:n, r % 2, 0:N], start=True, stop=True)\
                  .then_inc(sem("rope_rot"), 1)

            def project(pr, lo, hi, x, kts=KT, ready=None, after=None):
                for i in range(lo, hi):
                    u, o, t = pr.u0 + i, pr.o0 + i, pr.tiles[i]
                    pe.wait_ge(sem("w_lo"), u + 1)
                    if o >= 4:
                        pe.wait_ge(sem("proj_out"), o - 3)
                    for k in range(kts):
                        if i == 0 and ready is not None:
                            pe.wait_ge(sem("nlo"), ready + k + 1)
                        ins = mm3(ps[:, o % 4, 0:t.T], wtile(u % SLOTS, P * k, P),
                                  (x[0](k)[:, 0:t.T], x[1](k)[:, 0:t.T]), k == 0, k == kts - 1)
                    ins.then_inc(sem("w_used"), 1)
                    if i:
                        rot(pr, i - 1)
                    if after:
                        after(i)
                if hi == len(pr.tiles):
                    rot(pr, hi - 1)

            def values(u, o0, toks, x, after=None):
                for half in range(2):
                    pe.wait_ge(sem("w_lo"), u + half + 1)
                    for t in range(toks):
                        o = o0 + t
                        if half == 0:
                            pe.wait_ge(sem("proj_out"), o - 3)
                        for k in range(4):
                            kk = 4 * half + k
                            ins = mm3(ps[:, o % 4, 0:N],
                                      (x[0](kk)[:, P * t:P * t + P], x[1](kk)[:, P * t:P * t + P]),
                                      wtile((u + half) % SLOTS, N * k, N), kk == 0, kk == KT - 1)
                    ins.then_inc(sem("w_used"), 1)
                    if after:
                        after(half)

            def attend(j0, j1):
                for s in range(j0, j1 + 2):
                    if s < j1:
                        j = jobs[s]
                        if s - j0 >= 2:
                            pe.wait_ge(sem("x_done"), s - 1)
                        for r in range(2):
                            ins = pe.matmul(ps[:, 2 * (s % 2) + r, 0:j.nk], j.q[r], j.k[r], start=True, stop=True)
                        ins.then_inc(sem("s_done"), 1)
                    if j0 <= s - 2 < j1:
                        g = s - 2
                        j = jobs[g]
                        pe.wait_ge(sem("ev_a"), g + 1)
                        if not j.diff:
                            pe.wait_ge(sem("ev_v"), HL[g])
                        if g - 2 >= j0:
                            if j.diff:
                                pe.wait_ge(sem("oy"), g - 2 - J_L1[0] + 1)
                            elif j.gate is None:
                                pe.wait_ge(sem("o_lo"), HL[g - 2])
                            else:
                                pe.wait_ge(sem("o_m"), GJOB[g - 2] + 1)
                        nkt = j.nk // P
                        for r in range(1 if j.diff else 2):
                            o = ps[:, 6 + g % 2, 0:P] if j.diff else ps[64 * r:64 * r + 64, 6 + g % 2, 0:P]
                            for kt in range(nkt):
                                ins = pe.matmul(o, j.v(kt, r), PT[:, g % 2, r, P * kt:P * kt + P],
                                                start=(kt == 0), stop=(kt == nkt - 1))
                        ins.then_inc(sem("pv_done"), 1)
                    if j0 <= s - 1 < j1:
                        g = s - 1
                        j = jobs[g]
                        pe.wait_ge(sem("n_v"), g + 1)
                        for r in range(1 if j.diff else 2):
                            if r:
                                pe.wait_ge(sem("n_p"), g + 1)
                            for kt in range(j.nk // P):
                                ins = pe.transpose(ps[:, 4 + r, P * kt:P * kt + P],
                                                   E[:, g % 2, r, P * kt:P * kt + P], ident)
                        ins.then_inc(sem("t_done"), 1)

            def project_out(u0, o0, T, x):
                for i in range(KT):
                    u = u0 + i
                    pe.wait_ge(sem("w_lo"), u + 1)
                    if i >= 4:
                        pe.wait_ge(sem("out_added"), o0 + i - 3)
                    for k in range(KT):
                        ins = mm3(ps[:, i % 4, 0:T], wtile(u % SLOTS, P * k, P), (x[0](k)[:, 0:T], x[1](k)[:, 0:T]),
                                  k == 0, k == KT - 1)
                    ins.then_inc(sem("w_used"), 1)

            def mlp(u0, h0, T, ready, a0, g0):
                for k in range(KT):
                    pe.wait_ge(sem("nlo"), ready + k + 1)
                with pe.Fori(0, QUARTERS) as it:
                    for j in range(16):
                        pe.wait_ge(sem("w_lo"), 16 * it + (u0 + j + 1))
                        i = j % 8
                        if j < 8:
                            if j >= 2:
                                pe.wait_ge(sem("hid"), 8 * it + (2 + h0 + j - 1))
                        elif i >= 2:
                            pe.wait_ge(sem("mlp_added"), 8 * it + (1 + h0 + i - 1))
                        else:
                            pe.wait_ge(sem("mlp_added"), 8 * it + (1 + h0))
                        for k in range(KT):
                            if j == 8:
                                pe.wait_ge(sem("hid"), 8 * it + (2 + h0 + k + 1))
                            b = ((Hh, Hl) if j < 8 else (HIDh, HIDl))
                            ins = mm3(ps[:, 2 * (j // 8) + j % 2, 0:T], wtile((u0 + j) % SLOTS, P * k, P),
                                      (b[0][:, k, 0:T], b[1][:, k, 0:T]), k == 0, k == KT - 1)
                        ins.then_inc(sem("w_used"), 1)
                        if j % 2:
                            a = a0 + j // 2
                            ada_mm(None, j // 2, a % ADA_SLOTS, 2 * it + (a // ADA_SLOTS + 1), 1 * it + g0)
                    ada_turn(1 * it + g0)

            Hx = (lambda k: Hh[:, k, :], lambda k: Hl[:, k, :])
            Gx = (lambda k: Gh[:, k, :], lambda k: Gl[:, k, :])
            Cx = (lambda k: CQh[:, k, :], lambda k: CQl[:, k, :])

            def ada_static(a):
                ada_mm(a, a % KT, a % ADA_SLOTS, a // ADA_SLOTS + 1, a // KT)

            pe.wait_ge(sem("cst_landed"), 16)
            pe.wait_ge(sem("lam_prod"), 1)
            pe.matmul(ps[:, 5, 0:2], ones, lam[:, 0:2], start=True, stop=True).then_inc(sem("lam_sum"), 1)
            sums(norms["l0a"])
            pe.wait_ge(sem("scs_ready"), 1)
            pe.wait_ge(sem("var"), 1)
            for a in range(2 * KT):
                ada_static(a)
                if a % KT == KT - 1:
                    ada_turn(a // KT)
            pe.wait_ge(sem("ada_ready"), 2)
            spread(norms["l0a"])

            def ada_between(i):
                if i == 6:
                    ada_turn(2)
                for a in range(2 * KT * i // 12, 2 * KT * (i + 1) // 12):
                    ada_static(2 * KT + a)

            project(p_l0, 0, L0_FM, Hx, ready=norms["l0a"].h0, after=ada_between)
            values(U_L0 + L0_FM, V_L0, 4, Hx, after=lambda h: ada_between(L0_FM + h))
            ada_turn(3)
            pe.wait_ge(sem("proj_out"), V_L0 + 4)
            pe.wait_ge(sem("rope_out"), 5)
            pe.wait_ge(sem("ada_ready"), 4)
            pe.wait_ge(sem("l0_zeros"), 1)
            attend(*J_L0)
            pe.wait_ge(sem("o_lo"), HL[J_L0[1] - 1])
            project_out(U_L0_OUT, 0, 512, Hx)
            sums(norms["l0b"])
            spread(norms["l0b"])
            mlp(U_L0_MLP, 0, 512, norms["l0b"].h0, 4 * KT, 4)
            pe.wait_ge(sem("ada_ready"), 8)
            sums(norms["l1a"])
            spread(norms["l1a"])
            project(p_l1, 0, L1_FM, Hx, ready=norms["l1a"].h0)
            for c in range(4):
                values(U_L1 + L1_FM + 2 * c, V_L1 + 4 * c, 4, Hx)
            pe.wait_ge(sem("proj_out"), V_L1 + 16)
            pe.wait_ge(sem("rope_out"), p_l1.r0 + 16)
            pe.wait_ge(sem("l1_zeros"), 1)
            attend(*J_L1)
            for k in range(8):
                pe.wait_ge(sem("sub_sq"), k + 1)
                pe.matmul(ps[:, k // 2, N * (k % 2):N * (k % 2) + N], ones, SQ[:, k % 4, 0:N], start=True, stop=True)\
                  .then_inc(sem("sub_ss"), 1)
            for b in range(4):
                pe.wait_ge(sem("sub_diag"), b + 1)
                pe.matmul(ps[:, b, :], ones, wk2[:, b, :], start=True, stop=True).then_inc(sem("sub_spread"), 1)
            pe.wait_ge(sem("sub_lo"), 8)
            project_out(U_L1_OUT, 8, 256, Hx)
            sums(norms["l1b"])
            spread(norms["l1b"])
            mlp(U_L1_MLP, 32, 256, norms["l1b"].h0, 8 * KT, 8)
            pe.wait_ge(sem("ada_ready"), 12)
            sums(norms["fin"])
            spread(norms["fin"])
            for l in range(2):
                u0 = U_B2 + l * B2_UNITS
                project(p_a[l], 0, B2_FM1, Gx, ready=norms["fin" if l == 0 else "ln0"].h0)
                project(p_b[l], 0, 2, Gx)
                sums(norms[f"q{l}"])
                project(p_b[l], 2, 4, Gx)
                spread(norms[f"q{l}"])
                project(p_b[l], 4, 5, Gx)
                sums(norms[f"kv{l}"])
                project(p_b[l], 5, 7, Gx)
                spread(norms[f"kv{l}"])
                project(p_b[l], 7, B2_FM2, Gx)
                for c in range(3):
                    values(u0 + 23 + 2 * c, V_B2[l] + 2 * c, 2, Gx)
                project(p_g[l], 0, KT, Gx)
                project(p_uq[l], 0, 6, Cx, kts=6, ready=norms[f"q{l}"].h0)
                pe.wait_ge(sem("nlo"), norms[f"kv{l}"].h0 + 2)
                u = u0 + 43
                pe.wait_ge(sem("w_lo"), u + 1)
                for m in range(3):
                    o = p_uk[l] + m
                    pe.wait_ge(sem("proj_out"), o - 3)
                    for k in range(2):
                        ins = mm3(ps[:, o % 4, 0:N], wtile(u % SLOTS, P * (2 * m + k), P),
                                  (Cx[0](6 + k), Cx[1](6 + k)), k == 0, k == 1)
                ins.then_inc(sem("w_used"), 1)
                u = u0 + 44
                pe.wait_ge(sem("w_lo"), u + 1)
                for t in range(2):
                    o = V_UV[l] + t
                    pe.wait_ge(sem("proj_out"), o - 3)
                    for k in range(2):
                        ins = mm3(ps[:, o % 4, 0:384], (Cx[0](6 + k)[:, P * t:P * t + P], Cx[1](6 + k)[:, P * t:P * t + P]),
                                  wtile(u % SLOTS, 384 * k, 384), k == 0, k == 1)
                ins.then_inc(sem("w_used"), 1)
                pe.wait_ge(sem("proj_out"), V_UV[l] + 2)
                pe.wait_ge(sem("rope_out"), p_uq[l].r0 + 6)
                pe.wait_ge(sem("ki_shift"), l + 1)
                pe.wait_ge(sem("kr_done"), l + 1)
                for h in range(8):
                    ki = KI[:, h % 2, :]
                    q = KQ[:, 5 + h // 2, :]
                    c = h // 2 % 2
                    pe.matmul(ps[:, h // 4 + 2 * (h % 2), N * c:N * c + N], q[:, P:2 * P], ki, start=True, stop=True)
                    ins = pe.matmul(ps[:, 4 + h % 2, P * (h // 2):P * (h // 2) + P], q[:, 0:P], ki[:, 0:P],
                                    start=True, stop=True)
                ins.then_inc(sem("ix_ps"), 1)
                pe.wait_ge(sem("ri"), l + 1)
                attend(*J_B2[l])
                pe.wait_ge(sem("o_lo"), HL[J_B2[l][1] - 1])
                project_out(u0 + 45, 16 + 8 * l, 256, Gx)
                for k in range(KT):
                    pe.wait_ge(sem("out_added"), 16 + 8 * l + k + 1)
                    ins = pe.matmul(ps[:, 7, 0:N], ones, X[:, k, 0:N], start=(k == 0), stop=(k == KT - 1))
                ins.then_inc(sem("mean_sum"), 1)
                sums(norms[f"ln{l}"])
                spread(norms[f"ln{l}"])


def feature_units(w):
    k, n = w.shape
    u = w.reshape(k // P, P, n // P, P).transpose(2, 1, 0, 3).reshape(n // P, P, k)
    return np.concatenate([u, np.zeros((n // P, P, 1024 - k), w.dtype)], axis=2) if k < 1024 else u


def value_units(w):
    c = w.shape[1] // N
    return w.reshape(2, 4, P, c, N).transpose(3, 0, 2, 1, 4).reshape(2 * c, P, 1024)


def mlp_units(w1, w2):
    parts = []
    for q in range(QUARTERS):
        parts += [feature_units(w1[:, 1024 * q:1024 * q + 1024]), feature_units(w2[1024 * q:1024 * q + 1024, :])]
    return np.concatenate(parts)


def one_unit(parts):
    row = np.concatenate(parts, axis=1)
    return np.concatenate([row, np.zeros((P, 1024 - row.shape[1]), row.dtype)], axis=1)[None]


def cols(v):
    return v.reshape(-1, P).T


PAIRS = [0, 4, 1, 5, 2, 6, 3, 7]


def weight_stream(a):
    we, wo = a["even_w_in"][0], a["odd_w_in"][0]
    aq, ak, av, bq, bk, bv = (we[:, x:y] for x, y in ((0, 512), (512, 640), (640, 768), (768, 1280), (1280, 1408),
                                                      (1408, 1536)))

    def pair(w):
        return w.reshape(1024, 8, 64)[:, PAIRS].reshape(1024, 512)

    w_out = a["even_w_out"][0].reshape(2, 8, 64, 1024)[:, PAIRS].reshape(1024, 1024)
    parts = [feature_units(np.concatenate([pair(aq), ak, pair(bq), bk], axis=1)),
             value_units(np.concatenate([av, bv], axis=1)), feature_units(w_out),
             mlp_units(a["mlp_w1"][0], a["mlp_w2"][0]),
             feature_units(wo[:, 0:2048]), value_units(wo[:, 2048:3072]), feature_units(a["odd_w_out"][0]),
             mlp_units(a["mlp_w1"][1], a["mlp_w2"][1])]
    for l in range(2):
        w = a["w_in_2"][l]
        s = np.cumsum([0, 768, 256, 32, 384, 384, 384, 256, 256, 256, 512, 64, 8, 1024])
        cq, ckv, kr, qb, kb, vb, qc, kc, vc, qi, ki, wi, gate = (w[:, s[i]:s[i + 1]] for i in range(13))
        z = np.zeros((1024, 120), w.dtype)
        uq = a["w_uq_2"][l].reshape(768, 6, 96)
        uq = np.concatenate([uq, np.zeros((768, 6, 32), w.dtype)], axis=2).reshape(768, 768)
        uk, uv = a["w_uk_2"][l], a["w_uv_2"][l]
        parts += [feature_units(np.concatenate([cq, ckv, ki, kr, z[:, 0:32], qb, kb, qc, kc, qi], axis=1)),
                  value_units(np.concatenate([vb, vc, wi, z], axis=1)), feature_units(gate), feature_units(uq),
                  one_unit([uk[P * k:P * k + P, P * m:P * m + P] for m in range(3) for k in range(2)]),
                  one_unit([uv[0:P], uv[P:2 * P]]), feature_units(a["w_out_2"][l])]
    return np.concatenate(parts)


def ada_stream(a):
    w = np.concatenate([a["ada_w"][0], a["ada_w"][1], a["w_ada_2"][0], a["w_ada_2"][1]], axis=1)
    return w.reshape(KT, P, 12, GROUP).transpose(2, 0, 1, 3).reshape(12 * KT, P, GROUP)


def constants():
    c = np.zeros((P, C_END), np.float32)
    c[:, C_ID:C_ID + P] = np.eye(P)
    c[:, C_ONE:C_ONE + P] = 1.0
    for m in range(P):
        k, v = (m + 16, -1.0) if m % 32 < 16 else (m - 16, 1.0)
        c[k, C_RQ + m] = v
        if 64 <= m < 96:
            c[k, C_RM + m] = v
    t = np.arange(N)
    inv = (10000.0 ** (-np.arange(16) / 16.0)).astype(np.float32)
    row, col = (t // 64).astype(np.float32), (t % 64).astype(np.float32)
    ang = np.concatenate([np.outer(inv, row)] * 2 + [np.outer(inv, col)] * 2).astype(np.float32)
    c[:, C_COS:C_COS + N] = np.cos(np.concatenate([ang, ang]))
    c[:, C_SIN:C_SIN + N] = np.sin(np.concatenate([ang, ang]))
    angm = np.outer(inv, t.astype(np.float32)).astype(np.float32)
    c[:, C_COSM:C_COSM + N] = 1.0
    c[64:96, C_COSM:C_COSM + N] = np.cos(np.concatenate([angm, angm]))
    c[64:96, C_SINM:C_SINM + N] = np.sin(np.concatenate([angm, angm]))
    q, k = np.arange(N)[:, None], np.arange(N)[None, :]
    win = np.where(np.abs(q - k) <= 128, 0.0, NEG)
    start = np.clip(q % 64 - 8, 0, 48)
    nbr = np.where((k % 64 >= start) & (k % 64 < start + 16), 0.0, NEG)
    cau = np.where(k <= q, 0.0, NEG)
    for x, c0 in ((win, C_WIN), (nbr, C_NBR)):
        c[:, c0:c0 + 2 * N] = x.reshape(2, P, N).transpose(1, 0, 2).reshape(P, 2 * N)
    c[:, C_CAU:C_CAU + P] = cau[0:P, 0:P]
    c[:, C_CAU + P:C_CAU + 3 * P] = cau[P:]
    d = q - k
    count = ((d >= 0) & (d <= 128)) * 1.0 + ((d >= 0) & (d % 4 == 0)) + ((d >= 0) & (d % 16 == 0))
    ali = np.zeros((P, 10, 384), np.float32)
    for h in range(10):
        slope = 2.0 ** (-8.0 * (h + 1) / 10)
        x = -slope * d + (np.where(count > 0, np.log(np.maximum(count, 1.0)), NEG) if h < 6
                          else np.where(d >= 0, 0.0, NEG))
        ali[:, h, 0:P] = x[0:P, 0:P]
        ali[:, h, P:] = x[P:]
    return c, ali


def parameters(a):
    p = np.zeros((P, P_END), np.float32)
    p[:, P_CV:P_CV + 24] = np.stack([cols(a["c"][0]), cols(a["c_ctx"]), cols(a["c_2"][0])], axis=2).reshape(P, 24)
    p[:, P_AB:P_AB + 144] = cols(np.concatenate([a["ada_b"][0], a["ada_b"][1], a["b_ada_2"][0], a["b_ada_2"][1]]))
    p[:, P_N1:P_N1 + 16] = cols(a["norm1_g"].reshape(-1))
    p[:, P_N2:P_N2 + 16] = cols(a["norm2_g"].reshape(-1))
    p[:, P_FIN:P_FIN + 8] = cols(a["final_g"])
    p[:, P_LNG:P_LNG + 16] = cols(a["ln_g_2"].reshape(-1))
    p[:, P_LNB:P_LNB + 16] = cols(a["ln_b_2"].reshape(-1))
    p[:, P_QN:P_QN + 12] = cols(a["q_norm_g_2"].reshape(-1))
    p[:, P_KVN:P_KVN + 4] = cols(a["kv_norm_g_2"].reshape(-1))
    p[:, P_SUB:P_SUB + 1] = cols(a["subln_g"].reshape(-1))
    p[:, P_SINK:P_SINK + 8] = np.broadcast_to(a["a_sink"][0][PAIRS], (P, 8))
    for i, name in enumerate(("lam_q1", "lam_q2", "lam_k1", "lam_k2")):
        p[0:64, P_LAM + i] = a[name][0]
    return p


def tokens(x):
    return x.reshape(N, KT, P).transpose(2, 1, 0)


def kernel(**inputs):
    import concourse.bacc as bacc
    from concourse.bass_utils import run_bass_kernel_spmd

    a = {k: np.asarray(v) for k, v in inputs.items()}
    const, ali = constants()
    pad = np.zeros((8, 7, 127), np.float32)
    pad[:, :, 48:79] = a["b_rpb"][0][PAIRS][:, 4:11]
    rpb = np.stack([pad[:, :, 63 - q:127 - q] for q in range(64)]).reshape(64, 8, 7 * 64)
    arrays = {
        "wall": weight_stream(a), "aall": ada_stream(a), "const": const, "prm": parameters(a),
        "xin": np.concatenate([tokens(a["x"][0]), tokens(a["ctx"][0])], axis=2), "rpb": rpb, "ali": ali,
    }
    arrays = {k: np.ascontiguousarray(v) for k, v in arrays.items()}
    assert arrays["wall"].shape == (UNITS, P, 1024) and arrays["aall"].shape == (ADA_UNITS, P, GROUP)
    nc = bacc.Bacc("TRN2", target_bir_lowering=False, num_devices=1)
    args = [nc.dram_tensor(k, v.shape, mybir.dt.from_np(v.dtype), kind="ExternalInput").ap() for k, v in arrays.items()]
    out = nc.dram_tensor("out", (P, KT, N), F32, kind="ExternalOutput").ap()
    program(nc, *args, out)
    r = run_bass_kernel_spmd(nc, [arrays], core_ids=[0])
    return r.results[0]["out"].transpose(2, 1, 0).reshape(1, N, D)
```

```python
import math
from contextlib import ExitStack

import concourse.bass as bass
import numpy as np
from concourse import mybir

F32 = mybir.dt.float32
F32R = mybir.dt.float32r
ALU = mybir.AluOpType
ACT = mybir.ActivationFunctionType
AX = mybir.AxisListType

P = 128
D = 1024
KT = D // P
N = 256
SLOTS = 4
AHEAD = 3
ADA_SLOTS = 4
ADA_N = 384
GROUP = 4 * ADA_N
QUARTERS = 4
NEG = -1.0e30
TAKEN = -3.0e38
TOPK = 64
LAM_INIT = 0.8 - 0.6 * math.exp(-0.3)
ALPHA = 4 ** 0.25

C_ID, C_ONE, C_RQ, C_RM = 0, 128, 256, 384
C_COS, C_SIN, C_COSM, C_SINM = 512, 768, 1024, 1280
C_WIN, C_NBR, C_CAU = 1536, 2048, 2560
C_END = 2944
P_CV, P_AB, P_N1, P_N2, P_FIN, P_LNG, P_LNB, P_QN, P_KVN, P_SUB, P_SINK, P_LAM = (
    0, 24, 168, 184, 200, 208, 224, 240, 252, 256, 257, 265)
P_END = 269

U_L0 = 0
L0_FM = 10
U_L0_OUT = L0_FM + 2
U_L0_MLP = U_L0_OUT + KT
MLP_UNITS = QUARTERS * 16
U_L1 = U_L0_MLP + MLP_UNITS
L1_FM = 16
U_L1_OUT = U_L1 + L1_FM + 8
U_L1_MLP = U_L1_OUT + KT
U_B2 = U_L1_MLP + MLP_UNITS
B2_FM1 = 9
B2_FM2 = 14
B2_UNITS = B2_FM1 + B2_FM2 + 6 + KT + 6 + 1 + 1 + KT
UNITS = U_B2 + 2 * B2_UNITS
ADA_UNITS = 12 * KT


def program(nc, wall, aall, const, prm, xin, rpb, ali, out):
    with ExitStack() as top:
        def sb(name, shape, dt=F32, scope=top):
            return scope.enter_context(nc.sbuf_tensor(name, shape, dt))

        sems = {}

        def sem(name):
            if name not in sems:
                sems[name] = top.enter_context(nc.semaphore(name))
            return sems[name]

        ps = top.enter_context(nc.psum_tensor("ps", [P, 8, 512], F32))

        X = sb("X", [P, KT, 2 * N])
        raw = sb("raw", [P, SLOTS, 1024])
        whi = sb("whi", [P, SLOTS, 1024], F32R)
        wlo = sb("wlo", [P, SLOTS, 1024], F32R)
        wk1 = sb("wk1", [P, 4, 512])
        wk2 = sb("wk2", [P, 4, 512])
        RS = sb("RS", [P, 512])
        VR = sb("VR", [P, 2, 4])
        cst = sb("cst", [P, C_END])
        par = sb("par", [P, P_END])
        ada = sb("ada", [P, 3, 3, 48])
        SC = sb("SC", [P, 24, 8])
        small = sb("small", [P, 4, 16])
        lam = sb("lam", [P, 8])
        nsink = sb("nsink", [P, 8])
        mhalf = sb("mhalf", [P, 1])

        ident = cst[:, C_ID:C_ID + P]
        ones = cst[:, C_ONE:C_ONE + P]
        E = wk1[:, :, :].rearrange("p (g r) n -> p g r n", g=2)
        PT = wk2[:, :, :].rearrange("p (g r) n -> p g r n", g=2)
        SQ = wk1
        Y = wk2[:, 0:2, :]
        DG = RS[:, :].rearrange("p (g r n) -> p g r n", g=2, r=2)
        OS = RS[:, 0:N].rearrange("p (g n) -> p g n", g=2)
        DS = RS[:, N:2 * N].rearrange("p (g n) -> p g n", g=2)
        M = wk2[:, 2:4, :]
        SEL = wk2[:, 0, 0:384]

        def RI(h):
            return (wk2 if h < 4 else wk1)[:, h % 4, 0:384]


        b1 = ExitStack()
        Hh = sb("Hh", [P, KT, 2 * N], F32R, b1)
        Hl = sb("Hl", [P, KT, 2 * N], F32R, b1)
        aring = sb("aring", [P, ADA_SLOTS, GROUP], F32, b1)
        AR = sb("AR", [P, ADA_N], F32, b1)
        scs = sb("scs", [P, KT, 32], F32, b1)
        stp = sb("stp", [P, 2, KT, 3], F32, b1)
        s0 = ExitStack()
        Q0 = sb("Q0", [P, 8, 2 * N], F32, s0)
        K0 = sb("K0", [P, 2, 2, 2 * N], F32, s0)
        V0 = sb("V0", [P, 4, N], F32, s0)
        BI = sb("BI", [P, 2, 8, N], F32, s0)
        s0.close()
        s1 = ExitStack()
        Q1 = sb("Q1", [P, 8, 2, N], F32, s1)
        K1 = sb("K1", [P, 8, 2 * N], F32, s1)
        V1 = sb("V1", [P, 4, D], F32, s1)
        s1.close()

        sm = ExitStack()
        HIDh = sb("HIDh", [P, KT, 2 * N], F32R, sm)
        HIDl = sb("HIDl", [P, KT, 2 * N], F32R, sm)
        sm.close()
        b1.close()
        b2 = ExitStack()
        Gh = sb("Gh", [P, KT, N], F32R, b2)
        Gl = sb("Gl", [P, KT, N], F32R, b2)
        QZ = sb("QZ", [P, 5, 2, N], F32, b2)
        KQ = sb("KQ", [P, 9, N], F32, b2)
        V2 = sb("V2", [P, 2, 3 * N], F32, b2)
        GT = sb("GT", [P, KT, N], F32, b2)
        QA = sb("QA", [P, 6, N], F32, b2)
        KA = sb("KA", [P, 6, N], F32, b2)
        VA = sb("VA", [P, 2, 384], F32, b2)
        KK = sb("KK", [P, N], F32, b2)
        KI = sb("KI", [P, 2, N], F32, b2)
        AL = sb("AL", [P, 10, 384], F32, b2)
        MO = sb("MO", [P, 2, P], F32, b2)
        WI = sb("WI", [P, 2, 8], F32, b2)
        IX = sb("IX", [P, 384], F32, b2)
        M8 = sb("M8", [P, 16], F32, b2)
        PQ = sb("PQ", [P, 8, N], F32, b2)
        CQh = sb("CQh", [P, 8, N], F32R, b2)
        CQl = sb("CQl", [P, 8, N], F32R, b2)
        b2.close()

        KOFF, KLEN = (0, P), (P, 2 * P)

        class Norm:

            def __init__(self, src, n, T, width, streams, dst, eps=1e-6, keep=None, ready=()):
                self.src, self.n, self.T, self.width, self.eps = src, n, T, width, eps
                self.streams = streams
                self.dst = dst
                self.keep = keep
                self.ready = ready

        def adacol(s, v, t):
            return ada[:, s, v, t:t + 1]

        def xt(k, T):
            return X[:, k, 0:T]

        def mod(scale_row, s, v, t0):
            return lambda k: SC[:, scale_row, k:k + 1], lambda k: adacol(s, v, t0 + k)

        Hd = (lambda k: Hh[:, k, :], lambda k: Hl[:, k, :])
        Hdx = (lambda k: Hh[:, k, 0:N], lambda k: Hl[:, k, 0:N])
        Gd = (lambda k: Gh[:, k, :], lambda k: Gl[:, k, :])

        x_in = [("x_landed", 16)]
        norms = {}
        norms["l0a"] = Norm(xt, 8, 512, D, [(0, *mod(0, 0, 0, 0)), (N, *mod(1, 0, 1, 0))], Hd, ready=x_in)
        norms["l0b"] = Norm(xt, 8, 512, D, [(0, *mod(2, 0, 0, 24)), (N, *mod(3, 0, 1, 24))], Hd,
                            ready=[("out_added", 8)])
        norms["l1a"] = Norm(xt, 8, 512, D, [(0, *mod(4, 1, 0, 0)), (N, *mod(5, 1, 1, 0))], Hd,
                            ready=[("mlp_added", 33)])
        norms["l1b"] = Norm(xt, 8, 256, D, [(0, *mod(6, 1, 0, 24))], Hdx, ready=[("out_added", 16)])
        norms["fin"] = Norm(xt, 8, 256, D, [(0, *mod(8, 2, 2, 0))], Gd, ready=[("mlp_added", 65)],
                            keep=(lambda k: X[:, k, 0:N], lambda k: par[:, P_FIN + k:P_FIN + k + 1], None))
        for l in range(2):
            norms[f"q{l}"] = Norm(lambda k, T: PQ[:, k, 0:T], 6, 256, 768,
                                  [(0, lambda k, l=l: par[:, P_QN + 6 * l + k:P_QN + 6 * l + k + 1], None)],
                                  (lambda k: CQh[:, k, :], lambda k: CQl[:, k, :]),
                                  ready=[])
            norms[f"kv{l}"] = Norm(lambda k, T: PQ[:, 6 + k, 0:T], 2, 256, 256,
                                   [(0, lambda k, l=l: par[:, P_KVN + 2 * l + k:P_KVN + 2 * l + k + 1], None)],
                                   (lambda k: CQh[:, 6 + k, :], lambda k: CQl[:, 6 + k, :]),
                                   ready=[])
            norms[f"ln{l}"] = Norm(xt, 8, 256, D, [(0, *mod(9, 2, 2, 24))] if l == 0 else [],
                                   Gd if l == 0 else None, eps=1e-5, ready=[("centred", 8 * (l + 1))],
                                   keep=(lambda k: X[:, k, 0:N],
                                         lambda k, l=l: par[:, P_LNG + 8 * l + k:P_LNG + 8 * l + k + 1],
                                         lambda k, l=l: par[:, P_LNB + 8 * l + k:P_LNB + 8 * l + k + 1]))

        order = ["l0a", "l0b", "l1a", "l1b", "fin", "q0", "kv0", "ln0", "q1", "kv1", "ln1"]
        tiles = split_tiles = 0
        for idx, name in enumerate(order):
            n = norms[name]
            n.t0, n.h0, n.idx = tiles, split_tiles, idx
            tiles += n.n
            split_tiles += n.n if n.dst else 0

        class Tile:

            def __init__(self, T, rope, dst, rest=()):
                self.T, self.rope = T, rope
                self.dst = dst if isinstance(dst, list) else [(slice(0, dst.shape[0]), dst)]
                self.rest = rest

        class Proj:
            outs = 0
            ropes = 0

            def __init__(self, u0, tiles):
                self.u0, self.tiles = u0, tiles
                self.o0, self.r0 = Proj.outs, Proj.ropes
                Proj.outs += len(tiles)
                Proj.ropes += sum(t.rope is not None for t in tiles)

            def rope_index(self, i):
                return self.r0 + sum(t.rope is not None for t in self.tiles[:i])

        def rows(r):
            return slice(64 * r, 64 * r + 64)

        def halves(ap):
            return [(rows(r), ap(r)[rows(r)]) for r in range(2)]

        def l0_tile(i):
            if i < 4:
                return Tile(512, "q", Q0[:, i, 0:N], [(slice(0, P), Q0[:, i, N:2 * N])])
            if i == 4:
                return Tile(512, "q", halves(lambda r: K0[:, 0, r, 0:N]), halves(lambda r: K0[:, 0, r, N:2 * N]))
            if i < 9:
                return Tile(512, None, Q0[:, i - 1, :])
            return Tile(512, None, halves(lambda r: K0[:, 1, r, :]))

        p_l0 = Proj(U_L0, [l0_tile(i) for i in range(L0_FM)])
        V_L0 = Proj.outs
        Proj.outs += 4
        p_l1 = Proj(U_L1, [Tile(256, "q", halves(lambda r, i=i: Q1[:, i, r, :])) for i in range(8)]
                    + [Tile(512, "q", K1[:, i, 0:N], [(slice(0, P), K1[:, i, N:2 * N])]) for i in range(8)])

        def b2_tile(i):
            if i < 3 or 6 <= i < 8:
                n = i if i < 3 else i - 3
                return Tile(256, None, halves(lambda r: QZ[:, n, r, :]))
            return Tile(256, None, KQ[:, i - 3 if i < 6 else i - 5, :])

        V_L1 = Proj.outs
        Proj.outs += 16
        O_IX = []
        p_a, p_b, V_B2, p_g, p_uq, p_uk, V_UV = [], [], [], [], [], [], []
        for l in range(2):
            u = U_B2 + l * B2_UNITS
            p_a.append(Proj(u, [Tile(256, None, PQ[:, i, :]) for i in range(8)] + [Tile(256, "m", KK[0:96, :])]))
            p_b.append(Proj(u + 9, [b2_tile(i) for i in range(B2_FM2)]))
            V_B2.append(Proj.outs)
            Proj.outs += 2
            O_IX.append(Proj.outs)
            Proj.outs += 8
            Proj.outs += 4
            p_g.append(Proj(u + 29, [Tile(256, None, GT[:, i, :]) for i in range(KT)]))
            p_uq.append(Proj(u + 37, [Tile(256, "m", QA[0:96, i, :]) for i in range(6)]))
            p_uk.append(Proj.outs)
            Proj.outs += 3
            V_UV.append(Proj.outs)
            Proj.outs += 2

        class Job:

            def __init__(self, q, k, nk, bias, pre, post, v, dst, sink=None, diff=False, gate=None):
                self.q, self.k, self.nk, self.bias, self.pre, self.post = q, k, nk, bias, pre, post
                self.v, self.dst, self.sink, self.diff, self.gate = v, dst, sink, diff, gate

        def two(ap, n):
            return ap[:, None, :].to_broadcast([P, 2, n])

        jobs = []
        for kind in range(2):
            for i in range(4):
                for t in range(4):
                    ctx_q = t >= 2
                    t2 = t % 2
                    bias = None
                    if not ctx_q:
                        bias = (two(cst[:, C_WIN + N * t2:C_WIN + N * t2 + N], N) if kind == 0
                                else BI[:, t2, 2 * i:2 * i + 2, :])
                    k0 = N if ctx_q else 0
                    jobs.append(Job(
                        q=[Q0[:, 4 * kind + i, P * t:P * t + P] for r in range(2)],
                        k=[K0[:, kind, r, k0:2 * N] for r in range(2)],
                        nk=2 * N - k0, bias=bias, pre=1.0, post=0.125,
                        v=(lambda kt, r, kind=kind, k0=k0: V0[:, k0 // P + kt, P * kind + 64 * r:P * kind + 64 * r + 64]),
                        dst=(Hh[:, 4 * kind + i, P * t:P * t + P], Hl[:, 4 * kind + i, P * t:P * t + P]),
                        sink=(2 * i if kind == 0 else None)))
        J_L0 = (0, len(jobs))
        for h in range(8):
            for t in range(2):
                jobs.append(Job(
                    q=[Q1[:, h, r, P * t:P * t + P] for r in range(2)],
                    k=[K1[:, h, :] for r in range(2)], nk=2 * N, bias=None, pre=1.0, post=0.125,
                    v=(lambda kt, r, h=h: V1[:, kt, P * h:P * h + P]),
                    dst=(Hh[:, h, P * t:P * t + P], Hl[:, h, P * t:P * t + P]), diff=True))
        J_L1 = (J_L0[1], len(jobs))
        J_B2 = []
        for l in range(2):
            j0 = len(jobs)
            for i in range(3):
                for t in range(2):
                    jobs.append(Job(
                        q=[QA[0:96, 2 * i + r, P * t:P * t + P] for r in range(2)],
                        k=[KA[0:96, 2 * i + r, 0:KLEN[t]] for r in range(2)], nk=KLEN[t],
                        bias=two(cst[:, C_CAU + KOFF[t]:C_CAU + KOFF[t] + KLEN[t]], KLEN[t]),
                        pre=96 ** -0.5, post=1.0,
                        v=(lambda kt, r, i=i: VA[:, kt, 64 * (2 * i + r):64 * (2 * i + r) + 64]),
                        dst=(Gh[:, i, P * t:P * t + P], Gl[:, i, P * t:P * t + P]), gate=GT[:, i, P * t:P * t + P]))
            for i in range(3):
                for t in range(2):
                    jobs.append(Job(
                        q=[QZ[:, i, r, P * t:P * t + P] for r in range(2)],
                        k=[KQ[:, i, 0:KLEN[t]] for r in range(2)], nk=KLEN[t],
                        bias=AL[:, 2 * i:2 * i + 2, KOFF[t]:KOFF[t] + KLEN[t]], pre=0.125, post=1.0,
                        v=(lambda kt, r, i=i: V2[:, kt, N + 64 * (2 * i + r):N + 64 * (2 * i + r) + 64]),
                        dst=(Gh[:, 3 + i, P * t:P * t + P], Gl[:, 3 + i, P * t:P * t + P]),
                        gate=GT[:, 3 + i, P * t:P * t + P]))
            for i in range(2):
                for t in range(2):
                    jobs.append(Job(
                        q=[QZ[:, 3 + i, r, P * t:P * t + P] for r in range(2)],
                        k=[KQ[:, 3 + i, 0:KLEN[t]] for r in range(2)], nk=KLEN[t],
                        bias=AL[:, 6 + 2 * i:8 + 2 * i, KOFF[t]:KOFF[t] + KLEN[t]], pre=0.125, post=1.0,
                        v=(lambda kt, r, i=i: V2[:, kt, 640 * (1 - i) + 64 * r:640 * (1 - i) + 64 * r + 64]),
                        dst=(Gh[:, 6 + i, P * t:P * t + P], Gl[:, 6 + i, P * t:P * t + P]),
                        gate=GT[:, 6 + i, P * t:P * t + P]))
            J_B2.append((j0, len(jobs)))
        GJOB = {g: n for n, g in enumerate(g for g in range(len(jobs)) if jobs[g].gate is not None)}
        HL = {}
        for g in range(len(jobs)):
            HL[g] = sum(1 for j in jobs[:g + 1] if not j.diff)

        block = top.enter_context(nc.Block())


        for l in range(2):
            norms[f"q{l}"].ready = [("proj_out", p_a[l].o0 + 9), ("rope_out", p_a[l].r0 + 1)]

        @block.sync
        def _(sp):
            def weight(u, slot):
                if not isinstance(u, int) or u >= SLOTS:
                    sp.wait_ge(sem("w_lo"), u - (SLOTS - 1))
                src = wall[u] if isinstance(u, int) else wall[bass.ds(u, 1), :, :].rearrange("a p n -> p (a n)")
                sp.dma_start(raw[:, slot, :], src).then_inc(sem(f"w_landed{slot}"), 16)

            def ada_unit(a, slot):
                if not isinstance(a, int) or a >= ADA_SLOTS:
                    sp.wait_ge(sem("a_used"), a - (ADA_SLOTS - 1))
                src = aall[a] if isinstance(a, int) else aall[bass.ds(a, 1), :, :].rearrange("a p n -> p (a n)")
                sp.dma_start(aring[:, slot, :], src).then_inc(sem(f"a_landed{slot}"), 16)

            def mlp_loads(u0, a0):
                with sp.Fori(0, QUARTERS) as it:
                    for j in range(16):
                        weight(16 * it + (u0 + j), (u0 + j) % SLOTS)
                        if j % 2:
                            ada_unit(8 * it + (a0 + j // 2), (a0 + j // 2) % ADA_SLOTS)

            sp.dma_start(par[:, :], prm).then_inc(sem("par_landed"), 16)
            for a in range(ADA_SLOTS):
                ada_unit(a, a)
            sp.dma_start(cst[:, :], const).then_inc(sem("cst_landed"), 16)
            sp.dma_start(X[:, :, :], xin).then_inc(sem("x_landed"), 16)
            for u in range(SLOTS):
                weight(u, u)
            for a in range(ADA_SLOTS, 2 * KT):
                ada_unit(a, a % ADA_SLOTS)
            for qr in range(4):
                sp.dma_start(BI[64 * (qr % 2):64 * (qr % 2) + 64, qr // 2, :, :],
                             rpb[:, :, 64 * (3 - qr):64 * (3 - qr) + N]).then_inc(sem("rpb_landed"), 16)
            for u in range(SLOTS, U_L0_MLP):
                weight(u, u % SLOTS)
                i = u - SLOTS
                if i < 12:
                    for a in range(2 * KT * i // 12, 2 * KT * (i + 1) // 12):
                        ada_unit(2 * KT + a, a % ADA_SLOTS)
            mlp_loads(U_L0_MLP, 4 * KT)
            for u in range(U_L1, U_L1_MLP):
                weight(u, u % SLOTS)
            mlp_loads(U_L1_MLP, 8 * KT)
            for u in range(U_B2, UNITS):
                weight(u, u % SLOTS)
                if u == U_B2 + 8:
                    sp.wait_ge(sem("mlp_added"), 65)
                    sp.dma_start(AL[:, :, :], ali).then_inc(sem("ali_landed"), 16)
                if u == U_B2 + B2_UNITS + 8:
                    sp.wait_ge(sem("m_done"), J_B2[0][1])
                    sp.dma_start(AL[:, 6:10, :], ali[:, 6:10, :]).then_inc(sem("ali_landed"), 16)
            sp.wait_ge(sem("modded"), norms["ln1"].t0 + 8)
            sp.dma_start(out, X[:, :, 0:N]).then_inc(sem("stored"), 16)
            sp.wait_ge(sem("stored"), 16)

        @block.scalar
        def _(act):
            def split_hi(u, slot, lap):
                act.wait_ge(sem(f"w_landed{slot}"), 16 * lap)
                if not isinstance(u, int) or u >= SLOTS:
                    act.wait_ge(sem("w_used"), u - (SLOTS - 1))
                act.activation(whi[:, slot, :], raw[:, slot, :], ACT.Copy).then_inc(sem("w_hi"), 1)

            def ahead(u):
                if u + AHEAD < UNITS:
                    v = u + AHEAD
                    split_hi(v, v % SLOTS, v // SLOTS + 1)

            def ada_rows(g):
                act.wait_ge(sem("a_used"), 8 * g + 8)
                if not isinstance(g, int) or g:
                    act.wait_ge(sem("ada_tr"), g)
                act.activation(AR[:, :], ps[:, 6, 0:ADA_N], ACT.Copy).then_inc(sem("ar_ready"), 1)

            def squares(n):
                for name, value in n.ready:
                    act.wait_ge(sem(name), value)
                for k in range(n.n):
                    t = n.t0 + k
                    if t >= 4:
                        act.wait_ge(sem("ss"), t - 3)
                    act.activation(SQ[:, t % 4, 0:n.T], n.src(k, n.T), ACT.Square).then_inc(sem("sq"), 1)

            def his(n):
                for k in range(n.n):
                    act.wait_ge(sem("modded"), n.t0 + k + 1)
                    for c0, _, shift in n.streams:
                        c1 = min(c0 + N, n.T)
                        o, m = n.dst[0](k)[:, c0:c1], M[:, (n.t0 + k) % 2, c0:c1]
                        if n.keep or shift is None:
                            ins = act.activation(o, m, ACT.Copy)
                        else:
                            ins = act.activation(o, m, ACT.Identity, bias=shift(k))
                    ins.then_inc(sem("nhi"), 1)

            def evac(pr, i):
                t, o = pr.tiles[i], pr.o0 + i
                act.wait_ge(sem("w_used"), pr.u0 + i + 1)
                bank = ps[:, o % 4, :]
                if t.rope is None:
                    for p, dst in t.dst:
                        ins = act.activation(dst, bank[p, 0:t.T], ACT.Copy)
                    ins.then_inc(sem("proj_out"), 1)
                    return
                r = pr.rope_index(i)
                n = 128 if t.rope == "q" else 96
                if r >= 2:
                    act.wait_ge(sem("rope_out"), r - 1)
                ins = act.activation(wk1[0:n, r % 2, 0:N], bank[0:n, 0:N], ACT.Copy)
                for p, dst in t.rest:
                    ins = act.activation(dst, bank[p, N:2 * N], ACT.Copy)
                ins.then_inc(sem("proj_out"), 1)

            def evac_v(u, o0, dsts):
                act.wait_ge(sem("w_used"), u + 1)
                for t, dst in enumerate(dsts):
                    act.activation(dst, ps[:, (o0 + t) % 4, 0:dst.shape[1]], ACT.Copy).then_inc(sem("proj_out"), 1)

            def attend(j0, j1):
                for s in range(j0, j1 + (6 if jobs[j0].diff else 4)):
                    if j0 <= s - 6 < j1 and jobs[s - 6].diff:
                        g = s - 6
                        act.wait_ge(sem("sub_tr"), g - j0 + 1)
                        act.activation(jobs[g].dst[0], ps[:, 5, 0:P], ACT.Identity, scale=SC[:, 12, 0:1])\
                           .then_inc(sem("sub_hi"), 1)
                    if j0 <= s - 2 < j1:
                        g = s - 2
                        act.wait_ge(sem("t_done"), g + 1)
                        if g >= 2:
                            act.wait_ge(sem("pv_done"), g - 1)
                        act.activation(PT[:, g % 2, 0, 0:jobs[g].nk], ps[:, 4, 0:jobs[g].nk], ACT.Copy)\
                           .then_inc(sem("ev_a"), 1)
                    if j0 <= s - 4 < j1:
                        g = s - 4
                        j = jobs[g]
                        if j.diff:
                            act.wait_ge(sem("pv_done"), g + 1)
                            if g - 2 >= j0:
                                act.wait_ge(sem("sub_tr"), g - 2 - j0 + 1)
                            st = small[:, g % 4, :]
                            act.activation(OS[:, g % 2, :], ps[:, 6 + g % 2, 0:P], ACT.Identity, scale=st[:, 6:7])\
                               .then_inc(sem("sub_o"), 1)
                            act.wait_ge(sem("sub_o"), g - j0 + 1)
                            act.activation(DS[:, g % 2, :], OS[:, g % 2, :], ACT.Square, accum_out=st[:, 11:12])\
                               .then_inc(sem("sub_sq"), 1)
                        elif j.gate is None:
                            act.wait_ge(sem("pv_done"), g + 1)
                            act.activation(j.dst[0], ps[:, 6 + g % 2, 0:P], ACT.Copy).then_inc(sem("o_hi"), 1)
                        else:
                            act.wait_ge(sem("o_m"), GJOB[g] + 1)
                            act.activation(j.dst[0], MO[:, g % 2, :], ACT.Copy).then_inc(sem("o_hi"), 1)
                    if s < j1:
                        j = jobs[s]
                        act.wait_ge(sem("m_done"), s + 1)
                        if s >= 2:
                            act.wait_ge(sem("t_done"), s - 1)
                        st = small[:, s % 4, :]
                        if j.sink is not None:
                            act.activation(st[:, 8:10], st[:, 8:10], ACT.Exp)
                        for r in range(2):
                            ins = act.activation(E[:, s % 2, r, 0:j.nk], ps[:, 2 * (s % 2) + r, 0:j.nk], ACT.Exp,
                                                 bias=st[:, 2 + r:3 + r], scale=j.post,
                                                 accum_out=st[:, 4 + r:5 + r])
                        ins.then_inc(sem("x_done"), 1)

            def mlp(u0, h0, T, g0):
                with act.Fori(0, QUARTERS) as it:
                    for j in range(16):
                        v = u0 + j + AHEAD
                        split_hi(16 * it + v, v % SLOTS, 4 * it + (v // SLOTS + 1))
                        if j < 8:
                            act.wait_ge(sem("w_used"), 16 * it + (u0 + j + 1))
                            act.wait_ge(sem("hid"), 8 * it + (h0 + j + 1))
                            act.activation(Y[:, j % 2, 0:T], ps[:, j % 2, 0:T], ACT.Relu).then_inc(sem("hid_r"), 1)
                            act.wait_ge(sem("hid_r"), 8 * it + (h0 + j + 1))
                            act.activation(HIDh[:, j, 0:T], Y[:, j % 2, 0:T], ACT.Square).then_inc(sem("hid_h"), 1)
                    ada_rows(1 * it + g0)

            act.wait_ge(sem("par_landed"), 16)
            act.activation(stp[:, 0, :, :], par[:, P_CV:P_CV + 24].rearrange("p (k v) -> p k v", v=3), ACT.Exp,
                           scale=-1.0).then_inc(sem("silu_e"), 1)
            for v in range(AHEAD):
                split_hi(v, v, 1)
            act.wait_ge(sem("lam_sum"), 1)
            act.activation(lam[:, 2:4], ps[:, 5, 0:2], ACT.Exp).then_inc(sem("lam_e"), 1)
            squares(norms["l0a"])
            for g in range(2):
                ada_rows(g)
            his(norms["l0a"])
            for i in range(L0_FM):
                ahead(U_L0 + i)
                evac(p_l0, i)
                if i == 5:
                    ada_rows(2)
            for h in range(2):
                ahead(U_L0 + L0_FM + h)
            evac_v(U_L0 + L0_FM + 1, V_L0, [V0[:, t, :] for t in range(4)])
            ada_rows(3)
            attend(*J_L0)
            for i in range(KT):
                ahead(U_L0_OUT + i)
            squares(norms["l0b"])
            his(norms["l0b"])
            mlp(U_L0_MLP, 0, 512, 4)
            squares(norms["l1a"])
            his(norms["l1a"])
            for i in range(L1_FM):
                ahead(U_L1 + i)
                evac(p_l1, i)
            for c in range(4):
                u = U_L1 + L1_FM + 2 * c
                ahead(u)
                ahead(u + 1)
                evac_v(u + 1, V_L1 + 4 * c, [V1[:, t, N * c:N * c + N] for t in range(4)])
            attend(*J_L1)
            for i in range(KT):
                ahead(U_L1_OUT + i)
            squares(norms["l1b"])
            his(norms["l1b"])
            mlp(U_L1_MLP, 32, 256, 8)
            squares(norms["fin"])
            his(norms["fin"])
            for l in range(2):
                u0 = U_B2 + l * B2_UNITS
                for i in range(B2_FM1):
                    ahead(u0 + i)
                    evac(p_a[l], i)
                act.wait_ge(sem("rope_out"), p_a[l].r0 + 1)
                if l == 0:
                    act.wait_ge(sem("b2_zeros"), 1)
                for r in range(2):
                    ins = act.activation(KI[rows(r), r, :], KK[0:64, :], ACT.Copy)
                ins.then_inc(sem("ki_shift"), 1)
                squares(norms[f"q{l}"])
                squares(norms[f"kv{l}"])
                for i in range(4):
                    ahead(u0 + 9 + i)
                    evac(p_b[l], i)
                his(norms[f"q{l}"])
                for i in range(4, 7):
                    ahead(u0 + 9 + i)
                    evac(p_b[l], i)
                his(norms[f"kv{l}"])
                for i in range(7, B2_FM2):
                    ahead(u0 + 9 + i)
                    evac(p_b[l], i)
                for c in range(3):
                    u = u0 + 23 + 2 * c
                    ahead(u)
                    ahead(u + 1)
                    evac_v(u + 1, V_B2[l] + 2 * c + (8 if c else 0), [V2[:, t, N * c:N * c + N] for t in range(2)])
                    if c == 0:
                        act.wait_ge(sem("nlo"), norms[f"kv{l}"].h0 + 2)
                        for h in range(8):
                            act.wait_ge(sem("ix_ps"), 8 * l + h + 1)
                            act.activation(RI(h), ps[:, (O_IX[l] + h) % 4, 0:384], ACT.Relu, scale=0.125)\
                               .then_inc(sem("proj_out"), 1)
                for i in range(KT):
                    u = u0 + 29 + i
                    ahead(u)
                    act.wait_ge(sem("w_used"), u + 1)
                    bank = ps[:, (p_g[l].o0 + i) % 4, 0:N]
                    act.activation(PQ[:, i, :], bank, ACT.Tanh, scale=0.5)
                    act.activation(GT[:, i, :], bank, ACT.Copy, scale=0.5).then_inc(sem("proj_out"), 1)
                act.wait_ge(sem("ix_used"), 4 * (l + 1))
                for i in range(6):
                    ahead(u0 + 37 + i)
                    evac(p_uq[l], i)
                ahead(u0 + 43)
                act.wait_ge(sem("w_used"), u0 + 44)
                for i in range(3):
                    bank = ps[:, (p_uk[l] + i) % 4, 0:N]
                    act.activation(KA[0:64, 2 * i, :], bank[0:64, :], ACT.Copy)
                    act.activation(KA[0:64, 2 * i + 1, :], bank[64:128, :], ACT.Copy).then_inc(sem("proj_out"), 1)
                ahead(u0 + 44)
                evac_v(u0 + 44, V_UV[l], [VA[:, t, :] for t in range(2)])
                act.wait_ge(sem("sb_done"), l + 1)
                attend(*J_B2[l])
                for i in range(KT):
                    ahead(u0 + 45 + i)
                squares(norms[f"ln{l}"])
                if l == 0:
                    his(norms["ln0"])

        @block.vector
        def _(dve):
            linked = [0]

            def link(ins):
                linked[0] += 1
                ins.then_inc(sem("dve_link"), 1)
                dve.wait_ge(sem("dve_link"), linked[0])

            def split_lo(u, slot):
                dve.wait_ge(sem("w_hi"), u + 1)
                dve.tensor_tensor(wlo[:, slot, :], raw[:, slot, :], whi[:, slot, :].bitcast(F32), ALU.subtract)\
                   .then_inc(sem("w_lo"), 1)

            def ahead(u):
                if u + AHEAD < UNITS:
                    split_lo(u + AHEAD, (u + AHEAD) % SLOTS)

            def ada_cols(g, s, gl, vecs):
                dve.wait_ge(sem("ada_tr"), g + 1)
                src = ps[:, 7, 0:ADA_N].rearrange("p (c j r) -> p r j c", c=3, j=4)
                for v in vecs:
                    if isinstance(gl, int):
                        dst = ada[:, s, v, 12 * gl:12 * gl + 12]
                        bias = par[:, P_AB + 48 * s + 12 * gl:P_AB + 48 * s + 12 * gl + 12]
                    else:
                        dst = ada[:, s, v, bass.ds(12 * gl, 12)]
                        bias = par[:, bass.ds(12 * gl + (P_AB + 48 * s), 12)]
                    ins = dve.tensor_tensor(dst.rearrange("p (j c) -> p j c", j=4), src[:, v, :, :],
                                            bias.rearrange("p (j c) -> p j c", j=4), ALU.add)
                ins.then_inc(sem("ada_ready"), 1)

            def scale_row(row, s, v, t0, gain):
                src = ada[:, s, v, t0:t0 + 8]
                if gain is None:
                    link(dve.tensor_scalar(SC[:, row, :], src, 1.0, None, ALU.add))
                else:
                    link(dve.scalar_tensor_tensor(SC[:, row, :], src, 1.0, par[:, gain:gain + 8], ALU.add, ALU.mult))

            def variance(n):
                dve.wait_ge(sem("ss"), n.t0 + n.n)
                for t in range(n.T // P):
                    link(dve.tensor_tensor_reduce(RS[:, P * t:P * t + P], ps[:, 7, P * t:P * t + P], ident, 1.0, 0.0,
                                                  ALU.mult, ALU.add, VR[:, 0, t:t + 1]))
                dve.tensor_scalar(VR[:, 0, 0:n.T // P], VR[:, 0, 0:n.T // P], 1.0 / n.width, n.eps, ALU.mult, ALU.add)\
                   .then_inc(sem("var"), 1)

            def diagonals(n):
                dve.wait_ge(sem("rstd"), n.idx + 1)
                for t in range(n.T // P):
                    ins = dve.tensor_scalar(RS[:, P * t:P * t + P], ident, VR[:, 1, t:t + 1], None, ALU.mult)
                ins.then_inc(sem("diag"), 1)

            def modulate(n):
                root = ps[:, 7, :]

                def lo(k):
                    dve.wait_ge(sem("nhi"), n.h0 + k + 1)
                    m = M[:, (n.t0 + k) % 2, :]
                    for c0, _, shift in n.streams:
                        c1 = min(c0 + N, n.T)
                        h, o = n.dst[0](k)[:, c0:c1].bitcast(F32), n.dst[1](k)[:, c0:c1]
                        if n.keep or shift is None:
                            ins = dve.tensor_tensor(o, m[:, c0:c1], h, ALU.subtract)
                        else:
                            ins = dve.scalar_tensor_tensor(o, m[:, c0:c1], shift(k), h, ALU.add, ALU.subtract)
                    ins.then_inc(sem("nlo"), 1)

                dve.wait_ge(sem("spread"), n.idx + 1)
                for k in range(n.n):
                    t = n.t0 + k
                    if n.dst and n.h0 + k > 1:
                        dve.wait_ge(sem("nlo"), n.h0 + max(k - 1, 0))
                    src = n.src(k, n.T)
                    if n.keep:
                        x, g, b = n.keep[0](k), n.keep[1](k), n.keep[2]
                        ins = dve.scalar_tensor_tensor(x, src, g, root[:, 0:n.T], ALU.mult, ALU.mult)
                        if b is not None:
                            link(ins)
                            ins = dve.tensor_scalar(x, x, b(k), None, ALU.add)
                        if n.streams:
                            link(ins)
                            ins = dve.tensor_scalar(M[:, t % 2, 0:n.T], x, n.streams[0][1](k), n.streams[0][2](k),
                                                    ALU.mult, ALU.add)
                    else:
                        for c0, scale, _ in n.streams:
                            c1 = min(c0 + N, n.T)
                            ins = dve.scalar_tensor_tensor(M[:, t % 2, c0:c1], src[:, c0:c1], scale(k), root[:, c0:c1],
                                                           ALU.mult, ALU.mult)
                    ins.then_inc(sem("modded"), 1)
                    if n.dst and k:
                        lo(k - 1)
                if n.dst:
                    lo(n.n - 1)

            def rope(pr, i):
                t = pr.tiles[i]
                r = pr.rope_index(i)
                n, c, s = (128, C_COS, C_SIN) if t.rope == "q" else (96, C_COSM, C_SINM)
                dve.wait_ge(sem("rope_rot"), r + 1)
                if r >= 2:
                    dve.wait_ge(sem("rope_out"), r - 1)
                link(dve.tensor_tensor(wk1[0:n, 2 + r % 2, 0:N], wk1[0:n, r % 2, 0:N], cst[0:n, c:c + N], ALU.mult))
                link(dve.tensor_tensor(wk1[0:n, r % 2, 0:N], ps[0:n, 4 + r % 2, 0:N], cst[0:n, s:s + N], ALU.mult))
                for p, dst in t.dst:
                    ins = dve.tensor_tensor(dst, wk1[p, 2 + r % 2, 0:N], wk1[p, r % 2, 0:N], ALU.add)
                ins.then_inc(sem("rope_out"), 1)

            def steps(pr, lo, hi):
                for i in range(lo, hi):
                    ahead(pr.u0 + i)
                    if i and pr.tiles[i - 1].rope:
                        rope(pr, i - 1)
                if hi == len(pr.tiles) and pr.tiles[-1].rope:
                    rope(pr, hi - 1)

            def attend(j0, j1):
                for s in range(j0, j1 + (6 if jobs[j0].diff else 5)):
                    if j0 <= s - 6 < j1 and jobs[s - 6].diff:
                        g = s - 6
                        dve.wait_ge(sem("sub_hi"), g - j0 + 1)
                        dve.scalar_tensor_tensor(jobs[g].dst[1], ps[:, 5, 0:P], SC[:, 12, 0:1],
                                                 jobs[g].dst[0].bitcast(F32), ALU.mult, ALU.subtract)\
                           .then_inc(sem("sub_lo"), 1)
                    if j0 <= s - 5 < j1:
                        g = s - 5
                        j = jobs[g]
                        if not j.diff:
                            dve.wait_ge(sem("o_hi"), HL[g])
                            src = MO[:, g % 2, :] if j.gate is not None else ps[:, 6 + g % 2, 0:P]
                            dve.tensor_tensor(j.dst[1], src, j.dst[0].bitcast(F32), ALU.subtract)\
                               .then_inc(sem("o_lo"), 1)
                    if j0 <= s - 4 < j1 and jobs[s - 4].gate is not None:
                        g = s - 4
                        dve.wait_ge(sem("pv_done"), g + 1)
                        if g - 2 >= j0:
                            dve.wait_ge(sem("o_lo"), HL[g - 2])
                        dve.tensor_tensor(MO[:, g % 2, :], ps[:, 6 + g % 2, 0:P], jobs[g].gate, ALU.mult)\
                           .then_inc(sem("o_m"), 1)
                    if s < j1:
                        j = jobs[s]
                        st = small[:, s % 4, :]
                        dve.wait_ge(sem("s_done"), s + 1)
                        b0 = 2 * (s % 2)
                        if j.bias is not None:
                            nb = j.bias.shape[2]
                            w = ps[:, b0:b0 + 2, 0:nb]
                            if j.pre == 1.0:
                                link(dve.tensor_tensor(w, w, j.bias, ALU.add))
                            else:
                                link(dve.scalar_tensor_tensor(w, w, j.pre, j.bias, ALU.mult, ALU.add))
                        link(dve.tensor_reduce(st[:, 0:2], ps[:, b0:b0 + 2, 0:j.nk], AX.X, ALU.max))
                        if j.sink is None:
                            dve.tensor_scalar(st[:, 2:4], st[:, 0:2], -j.post, None, ALU.mult)\
                               .then_inc(sem("m_done"), 1)
                        else:
                            link(dve.scalar_tensor_tensor(st[:, 2:4], st[:, 0:2], -j.post,
                                                          nsink[:, j.sink:j.sink + 2], ALU.mult, ALU.min))
                            dve.tensor_tensor(st[:, 8:10], st[:, 2:4], nsink[:, j.sink:j.sink + 2], ALU.subtract)\
                               .then_inc(sem("m_done"), 1)
                    if j0 <= s - 1 < j1:
                        g = s - 1
                        j = jobs[g]
                        st = small[:, g % 4, :]
                        dve.wait_ge(sem("x_done"), g + 1)
                        if j.sink is not None:
                            link(dve.tensor_tensor(st[:, 4:6], st[:, 4:6], st[:, 8:10], ALU.add))
                        link(dve.reciprocal(st[:, 6:8], st[:, 4:6]))
                        if j.diff:
                            link(dve.scalar_tensor_tensor(st[:, 10:11], st[:, 4:5], st[:, 7:8], lam[:, 4:5],
                                                          ALU.mult, ALU.mult))
                            e0, e1 = E[:, g % 2, 0, 0:j.nk], E[:, g % 2, 1, 0:j.nk]
                            ins = dve.scalar_tensor_tensor(e0, e1, st[:, 10:11], e0, ALU.mult, ALU.add)
                        else:
                            if g - 2 >= j0:
                                dve.wait_ge(sem("t_done"), g - 1)
                            for r in range(2):
                                ins = dve.tensor_scalar(DG[:, g % 2, r, :], ident, st[:, 6 + r:7 + r], None, ALU.mult)
                        ins.then_inc(sem("n_v"), 1)
                    if j0 <= s - 2 < j1 and not jobs[s - 2].diff:
                        g = s - 2
                        dve.wait_ge(sem("t_done"), g + 1)
                        if g >= 2:
                            dve.wait_ge(sem("pv_done"), g - 1)
                        dve.tensor_copy(PT[:, g % 2, 1, 0:jobs[g].nk], ps[:, 5, 0:jobs[g].nk]).then_inc(sem("ev_v"), 1)

            def index_heads(l, p):
                if p == 0:
                    dve.wait_ge(sem("proj_out"), O_IX[l])
                    link(dve.tensor_scalar(WI[:, :, :], V2[:, :, P:P + 8], 8 ** -0.5, None, ALU.mult))
                for h in (2 * p, 2 * p + 1):
                    dve.wait_ge(sem("proj_out"), O_IX[l] + h + 1)
                    for t in range(2):
                        sl = slice(KOFF[t], KOFF[t] + KLEN[t])
                        base = IX[:, sl] if h else cst[:, C_CAU + KOFF[t]:C_CAU + KOFF[t] + KLEN[t]]
                        ins = dve.scalar_tensor_tensor(IX[:, sl], RI(h)[:, sl], WI[:, t, h:h + 1], base,
                                                       ALU.mult, ALU.add)
                    if h % 2 == 0:
                        link(ins)
                ins.then_inc(sem("ix_used"), 1)
                dve.wait_ge(sem("ix_used"), 4 * l + p + 1)

            def topk_round(l, p):
                ws = [IX[:, KOFF[t]:KOFF[t] + KLEN[t]] for t in range(2)]
                for t in range(2):
                    ins = dve.max(M8[:, 8 * t:8 * t + 8], ws[t])
                link(ins)
                for t in range(2):
                    ins = dve.match_replace(ws[t], M8[:, 8 * t:8 * t + 8], ws[t], TAKEN)
                link(ins)
                if p == TOPK // 8 - 1:
                    dve.tensor_scalar(SEL, IX[:, :], -2.0e38, NEG, ALU.is_gt, ALU.mult).then_inc(sem("sel_done"), 1)

            def add_out(u0, o0, add):
                for i in range(KT):
                    ahead(u0 + i)
                    dve.wait_ge(sem("w_used"), u0 + i + 1)
                    add(i, ps[:, i % 4, :]).then_inc(sem("out_added"), 1)

            def gated(s, t0, T):
                def add(i, bank):
                    for v in range(T // N):
                        x = X[:, i, N * v:N * v + N]
                        ins = dve.scalar_tensor_tensor(x, bank[:, N * v:N * v + N], adacol(s, v, t0 + i), x,
                                                       ALU.mult, ALU.add)
                    return ins
                return add

            def mlp(u0, h0, T, s, g0, s_next, vecs):
                with dve.Fori(0, QUARTERS) as it:
                    def lo(j):
                        dve.wait_ge(sem("hid_h"), 8 * it + (h0 + j + 1))
                        dve.tensor_tensor(HIDl[:, j, 0:T], M[:, j % 2, 0:T], HIDh[:, j, 0:T].bitcast(F32),
                                          ALU.subtract).then_inc(sem("hid"), 1)
                    for j in range(16):
                        v = u0 + j + AHEAD
                        split_lo(16 * it + v, v % SLOTS)
                        if j < 8:
                            dve.wait_ge(sem("hid_r"), 8 * it + (h0 + j + 1))
                            dve.wait_ge(sem("hid"), 8 * it + (h0 + j + 1))
                            dve.tensor_tensor(M[:, j % 2, 0:T], Y[:, j % 2, 0:T], Y[:, j % 2, 0:T], ALU.mult)\
                               .then_inc(sem("hid_a"), 1)
                            dve.wait_ge(sem("hid_a"), 8 * it + (h0 + j + 1))
                            lo(j)
                        else:
                            i = j - 8
                            dve.wait_ge(sem("w_used"), 16 * it + (u0 + j + 1))
                            gated(s, 40, T)(i, ps[:, 2 + i % 2, :]).then_inc(sem("mlp_added"), 1)
                    ada_cols(1 * it + g0, s_next, it, vecs)

            dve.memset(scs[:, :, :], 0.0).then_inc(sem("dve_link"), 1)
            linked[0] += 1
            dve.memset(mhalf[:, :], -0.5).then_inc(sem("mhalf_set"), 1)
            dve.memset(lam[:, 5:6], 0.0).then_inc(sem("hid"), 1)
            dve.memset(lam[:, 6:7], 0.0).then_inc(sem("hid"), 1)
            dve.memset(lam[:, 7:8], 0.0).then_inc(sem("mlp_added"), 1)
            dve.wait_ge(sem("silu_e"), 1)
            link(dve.tensor_scalar(stp[:, 1, :, :], stp[:, 0, :, :], 1.0, None, ALU.add))
            link(dve.reciprocal(stp[:, 0, :, :], stp[:, 1, :, :]))
            dve.tensor_tensor(scs[:, :, 0:3], par[:, P_CV:P_CV + 24].rearrange("p (k v) -> p k v", v=3),
                              stp[:, 0, :, :], ALU.mult).then_inc(sem("scs_ready"), 1)
            link(dve.tensor_scalar(nsink[:, :], par[:, P_SINK:P_SINK + 8], -1.0, None, ALU.mult))
            dve.tensor_tensor(lam[:, 0:2], par[:, P_LAM:P_LAM + 2], par[:, P_LAM + 2:P_LAM + 4], ALU.mult)\
               .then_inc(sem("lam_prod"), 1)
            link(dve.tensor_scalar(SC[:, 12, 0:1], par[:, P_SUB:P_SUB + 1], 1.0 - LAM_INIT, None, ALU.mult))
            for u in range(AHEAD):
                split_lo(u, u)
            dve.wait_ge(sem("lam_e"), 1)
            link(dve.tensor_tensor(lam[:, 4:5], lam[:, 3:4], lam[:, 2:3], ALU.subtract))
            link(dve.tensor_scalar(lam[:, 4:5], lam[:, 4:5], -LAM_INIT, None, ALU.add))
            variance(norms["l0a"])
            diagonals(norms["l0a"])
            for g in range(2):
                ada_cols(g, 0, g, (0, 1))
            dve.wait_ge(sem("ada_ready"), 2)
            scale_row(0, 0, 0, 8, P_N1)
            scale_row(1, 0, 1, 8, P_N1)
            modulate(norms["l0a"])
            steps(p_l0, 0, 8)
            ada_cols(2, 0, 2, (0, 1))
            steps(p_l0, 8, L0_FM)
            for h in range(2):
                ahead(U_L0 + L0_FM + h)
            ada_cols(3, 0, 3, (0, 1))
            dve.wait_ge(sem("rpb_done"), 1)
            attend(*J_L0)
            dve.wait_ge(sem("ada_ready"), 4)
            add_out(U_L0_OUT, 0, gated(0, 16, 512))
            scale_row(2, 0, 0, 32, P_N2)
            scale_row(3, 0, 1, 32, P_N2)
            variance(norms["l0b"])
            diagonals(norms["l0b"])
            modulate(norms["l0b"])
            mlp(U_L0_MLP, 0, 512, 0, 4, 1, (0, 1))
            dve.wait_ge(sem("ada_ready"), 8)
            scale_row(4, 1, 0, 8, P_N1 + 8)
            scale_row(5, 1, 1, 8, P_N1 + 8)
            scale_row(6, 1, 0, 32, P_N2 + 8)
            variance(norms["l1a"])
            diagonals(norms["l1a"])
            modulate(norms["l1a"])
            steps(p_l1, 0, L1_FM)
            for v in range(8):
                ahead(U_L1 + L1_FM + v)
            attend(*J_L1)
            add_out(U_L1_OUT, 8, gated(1, 16, 256))
            variance(norms["l1b"])
            diagonals(norms["l1b"])
            modulate(norms["l1b"])
            mlp(U_L1_MLP, 32, 256, 1, 8, 2, (2,))
            dve.wait_ge(sem("ada_ready"), 12)
            scale_row(8, 2, 2, 8, None)
            scale_row(9, 2, 2, 32, None)
            scale_row(10, 2, 2, 16, None)
            scale_row(11, 2, 2, 40, None)
            variance(norms["fin"])
            diagonals(norms["fin"])
            modulate(norms["fin"])
            for l in range(2):
                u0 = U_B2 + l * B2_UNITS
                steps(p_a[l], 0, B2_FM1)
                steps(p_b[l], 0, 2)
                variance(norms[f"q{l}"])
                diagonals(norms[f"q{l}"])
                steps(p_b[l], 2, 4)
                modulate(norms[f"q{l}"])
                steps(p_b[l], 4, 5)
                variance(norms[f"kv{l}"])
                diagonals(norms[f"kv{l}"])
                steps(p_b[l], 5, 7)
                modulate(norms[f"kv{l}"])
                steps(p_b[l], 7, B2_FM2)
                for v in range(6):
                    ahead(u0 + 23 + v)
                    if v >= 2:
                        index_heads(l, v - 2)
                for i in range(KT):
                    ahead(u0 + 29 + i)
                    dve.wait_ge(sem("proj_out"), p_g[l].o0 + i + 1)
                    dve.scalar_tensor_tensor(GT[:, i, :], PQ[:, i, :], 1.0, GT[:, i, :], ALU.add, ALU.mult)
                    topk_round(l, i)
                steps(p_uq[l], 0, 6)
                ahead(u0 + 43)
                ahead(u0 + 44)
                if l == 0:
                    dve.wait_ge(sem("ali_landed"), 16)
                dve.wait_ge(sem("sb_done"), l + 1)
                attend(*J_B2[l])

                def add(i, bank, l=l):
                    x = X[:, i, 0:N]
                    link(dve.tensor_scalar(x, x, ALPHA, None, ALU.mult))
                    return dve.scalar_tensor_tensor(x, bank[:, 0:N], SC[:, 10 + l, i:i + 1], x, ALU.mult, ALU.add)
                add_out(u0 + 45, 16 + 8 * l, add)
                dve.wait_ge(sem("mean_sum"), l + 1)
                link(dve.tensor_scalar(RS[:, 0:N], ps[:, 7, 0:N], 1.0 / D, None, ALU.mult))
                for k in range(KT):
                    dve.tensor_tensor(X[:, k, 0:N], X[:, k, 0:N], RS[:, 0:N], ALU.subtract)\
                       .then_inc(sem("centred"), 1)
                variance(norms[f"ln{l}"])
                diagonals(norms[f"ln{l}"])
                modulate(norms[f"ln{l}"])

        @block.gpsimd
        def _(pool):
            def root(dst, src, T):
                return pool.tensor_tensor(dst, src, mhalf[:, 0:1].to_broadcast([P, T]), ALU.pow)

            def roots(n):
                pool.wait_ge(sem("var"), n.idx + 1)
                root(VR[:, 1, 0:n.T // P], VR[:, 0, 0:n.T // P], n.T // P).then_inc(sem("rstd"), 1)

            def sub_roots(j0, j1):
                for g in range(j0, j1):
                    st = small[:, g % 4, :]
                    pool.wait_ge(sem("sub_sq"), g - j0 + 1)
                    pool.tensor_scalar(st[:, 12:13], st[:, 11:12], 1.0 / P, 1e-6, ALU.mult, ALU.add)\
                        .then_inc(sem("sub_var"), 1)
                    pool.wait_ge(sem("sub_var"), g - j0 + 1)
                    root(st[:, 13:14], st[:, 12:13], 1).then_inc(sem("sub_rs"), 1)
                    pool.wait_ge(sem("sub_rs"), g - j0 + 1)
                    pool.tensor_scalar(DS[:, g % 2, :], ident, st[:, 13:14], None, ALU.mult)\
                        .then_inc(sem("sub_diag"), 1)

            def zeros(pairs, name):
                for ap in pairs:
                    for r in range(2):
                        ins = pool.memset(ap(r)[rows(1 - r)], 0.0)
                ins.then_inc(sem(name), 1)

            zeros([lambda r: K0[:, :, r, :]], "l0_zeros")
            pool.wait_ge(sem("l0_zeros"), 1)
            pool.wait_ge(sem("mhalf_set"), 1)
            roots(norms["l0a"])
            pool.wait_ge(sem("rpb_landed"), 16 * 4)
            pool.wait_ge(sem("cst_landed"), 16)
            for t in range(2):
                pool.tensor_scalar(BI[:, t, :, :], BI[:, t, :, :], 8.0, None, ALU.mult).then_inc(sem("rpb_x8"), 1)
            pool.wait_ge(sem("rpb_x8"), 2)
            for t in range(2):
                ins = pool.tensor_tensor(BI[:, t, :, :], BI[:, t, :, :],
                                         cst[:, None, C_NBR + N * t:C_NBR + N * t + N].to_broadcast([P, 8, N]), ALU.add)
            ins.then_inc(sem("rpb_done"), 1)
            roots(norms["l0b"])
            roots(norms["l1a"])
            pool.wait_ge(sem("nlo"), norms["l1a"].h0 + 8)
            zeros([lambda r: Q1[:, :, r, :]], "l1_zeros")
            pool.wait_ge(sem("l1_zeros"), 1)
            sub_roots(*J_L1)
            roots(norms["l1b"])
            roots(norms["fin"])
            pool.wait_ge(sem("nlo"), norms["fin"].h0 + 8)
            zeros([lambda r: QZ[:, :, r, :], lambda r: KI[:, r, :]], "b2_zeros")
            pool.wait_ge(sem("b2_zeros"), 1)
            for l in range(2):
                pool.wait_ge(sem("rope_out"), p_a[l].r0 + 1)
                pool.tensor_copy(KA[64:96, :, :], KK[64:96, None, :].to_broadcast([32, 6, N])).then_inc(sem("kr_done"), 1)
                pool.wait_ge(sem("kr_done"), l + 1)
                roots(norms[f"q{l}"])
                roots(norms[f"kv{l}"])
                pool.wait_ge(sem("sel_done"), l + 1)
                pool.wait_ge(sem("ali_landed"), 16 * (l + 1))
                pool.tensor_tensor(AL[:, 6:10, :], AL[:, 6:10, :], SEL[:, None, :].to_broadcast([P, 4, 384]), ALU.add)\
                    .then_inc(sem("sb_done"), 1)
                roots(norms[f"ln{l}"])

        @block.tensor
        def _(pe):
            def mm3(o, a, b, first, last):
                pe.matmul(o, a[0], b[0], start=first, stop=False)
                pe.matmul(o, a[0], b[1], start=False, stop=False)
                return pe.matmul(o, a[1], b[0], start=False, stop=last)

            def wtile(slot, c0, n):
                return whi[:, slot, c0:c0 + n], wlo[:, slot, c0:c0 + n]

            def ada_mm(a, kt, slot, lap, g):
                pe.wait_ge(sem(f"a_landed{slot}"), 16 * lap)
                if kt == 0 and (not isinstance(g, int) or g):
                    pe.wait_ge(sem("ar_ready"), g)
                for j in range(4):
                    ins = pe.matmul(ps[32 * j:32 * j + 32, 6, 0:ADA_N], scs[:, kt, :],
                                    aring[:, slot, ADA_N * j:ADA_N * j + ADA_N], start=(kt == 0), stop=(kt == KT - 1))
                ins.then_inc(sem("a_used"), 1)

            def ada_turn(g):
                pe.wait_ge(sem("ar_ready"), g + 1)
                if not isinstance(g, int) or g:
                    pe.wait_ge(sem("ada_ready"), g)
                for c in range(3):
                    ins = pe.transpose(ps[:, 7, P * c:P * c + P], AR[:, P * c:P * c + P], ident)
                ins.then_inc(sem("ada_tr"), 1)

            def sums(n):
                if n.idx:
                    pe.wait_ge(sem("modded"), n.t0)
                for k in range(n.n):
                    t = n.t0 + k
                    pe.wait_ge(sem("sq"), t + 1)
                    pe.matmul(ps[:, 7, 0:n.T], ones, SQ[:, t % 4, 0:n.T], start=(k == 0), stop=(k == n.n - 1))\
                      .then_inc(sem("ss"), 1)

            def spread(n):
                pe.wait_ge(sem("diag"), n.idx + 1)
                pe.matmul(ps[:, 7, 0:n.T], ones, RS[:, 0:n.T], start=True, stop=True).then_inc(sem("spread"), 1)

            def rot(pr, i):
                t = pr.tiles[i]
                if t.rope is None:
                    return
                r = pr.rope_index(i)
                n, c = (128, C_RQ) if t.rope == "q" else (96, C_RM)
                pe.wait_ge(sem("proj_out"), pr.o0 + i + 1)
                if r >= 2:
                    pe.wait_ge(sem("rope_out"), r - 1)
                pe.matmul(ps[0:n, 4 + r % 2, 0:N], cst[0:n, c:c + n], wk1[0:n, r % 2, 0:N], start=True, stop=True)\
                  .then_inc(sem("rope_rot"), 1)

            def project(pr, lo, hi, x, kts=KT, ready=None, after=None):
                for i in range(lo, hi):
                    u, o, t = pr.u0 + i, pr.o0 + i, pr.tiles[i]
                    pe.wait_ge(sem("w_lo"), u + 1)
                    if o >= 4:
                        pe.wait_ge(sem("proj_out"), o - 3)
                    for k in range(kts):
                        if i == 0 and ready is not None:
                            pe.wait_ge(sem("nlo"), ready + k + 1)
                        ins = mm3(ps[:, o % 4, 0:t.T], wtile(u % SLOTS, P * k, P),
                                  (x[0](k)[:, 0:t.T], x[1](k)[:, 0:t.T]), k == 0, k == kts - 1)
                    ins.then_inc(sem("w_used"), 1)
                    if i:
                        rot(pr, i - 1)
                    if after:
                        after(i)
                if hi == len(pr.tiles):
                    rot(pr, hi - 1)

            def values(u, o0, toks, x, after=None):
                for half in range(2):
                    pe.wait_ge(sem("w_lo"), u + half + 1)
                    for t in range(toks):
                        o = o0 + t
                        if half == 0:
                            pe.wait_ge(sem("proj_out"), o - 3)
                        for k in range(4):
                            kk = 4 * half + k
                            ins = mm3(ps[:, o % 4, 0:N],
                                      (x[0](kk)[:, P * t:P * t + P], x[1](kk)[:, P * t:P * t + P]),
                                      wtile((u + half) % SLOTS, N * k, N), kk == 0, kk == KT - 1)
                    ins.then_inc(sem("w_used"), 1)
                    if after:
                        after(half)

            def attend(j0, j1):
                for s in range(j0, j1 + (5 if jobs[j0].diff else 3)):
                    if s < j1:
                        j = jobs[s]
                        if s - j0 >= 2:
                            pe.wait_ge(sem("x_done"), s - 1)
                        for r in range(2):
                            ins = pe.matmul(ps[:, 2 * (s % 2) + r, 0:j.nk], j.q[r], j.k[r], start=True, stop=True)
                        ins.then_inc(sem("s_done"), 1)
                    if j0 <= s - 2 < j1:
                        g = s - 2
                        j = jobs[g]
                        pe.wait_ge(sem("n_v"), g + 1)
                        if g > j0:
                            pe.wait_ge(sem("ev_a"), g)
                            if not j.diff:
                                pe.wait_ge(sem("ev_v"), HL[g - 1])
                        for r in range(1 if j.diff else 2):
                            for kt in range(j.nk // P):
                                o, e = ps[:, 4 + r, P * kt:P * kt + P], E[:, g % 2, r, P * kt:P * kt + P]
                                if j.diff:
                                    ins = pe.transpose(o, e, ident)
                                else:
                                    ins = pe.matmul(o, e, DG[:, g % 2, r, :], start=True, stop=True)
                        ins.then_inc(sem("t_done"), 1)
                    if j0 <= s - 3 < j1:
                        g = s - 3
                        j = jobs[g]
                        pe.wait_ge(sem("ev_a"), g + 1)
                        if not j.diff:
                            pe.wait_ge(sem("ev_v"), HL[g])
                        if g - 2 >= j0:
                            if j.diff:
                                pe.wait_ge(sem("sub_sq"), g - 2 - J_L1[0] + 1)
                            elif j.gate is None:
                                pe.wait_ge(sem("o_lo"), HL[g - 2])
                            else:
                                pe.wait_ge(sem("o_m"), GJOB[g - 2] + 1)
                        nkt = j.nk // P
                        if j.diff:
                            for kt in range(nkt):
                                ins = pe.matmul(ps[:, 6 + g % 2, 0:P], PT[:, g % 2, 0, P * kt:P * kt + P], j.v(kt, 0),
                                                start=(kt == 0), stop=(kt == nkt - 1))
                        else:
                            for r in range(2):
                                for kt in range(nkt):
                                    ins = pe.matmul(ps[64 * r:64 * r + 64, 6 + g % 2, 0:P], j.v(kt, r),
                                                    PT[:, g % 2, r, P * kt:P * kt + P],
                                                    start=(kt == 0), stop=(kt == nkt - 1))
                        ins.then_inc(sem("pv_done"), 1)
                    if j0 <= s - 5 < j1 and jobs[s - 5].diff:
                        g = s - 5
                        pe.wait_ge(sem("sub_diag"), g - j0 + 1)
                        if g > j0:
                            pe.wait_ge(sem("sub_lo"), g - j0)
                        pe.matmul(ps[:, 5, 0:P], OS[:, g % 2, :], DS[:, g % 2, :], start=True, stop=True)\
                          .then_inc(sem("sub_tr"), 1)

            def project_out(u0, o0, T, x):
                for i in range(KT):
                    u = u0 + i
                    pe.wait_ge(sem("w_lo"), u + 1)
                    if i >= 4:
                        pe.wait_ge(sem("out_added"), o0 + i - 3)
                    for k in range(KT):
                        ins = mm3(ps[:, i % 4, 0:T], wtile(u % SLOTS, P * k, P), (x[0](k)[:, 0:T], x[1](k)[:, 0:T]),
                                  k == 0, k == KT - 1)
                    ins.then_inc(sem("w_used"), 1)

            def mlp(u0, h0, T, ready, a0, g0):
                for k in range(KT):
                    pe.wait_ge(sem("nlo"), ready + k + 1)
                with pe.Fori(0, QUARTERS) as it:
                    for j in range(16):
                        pe.wait_ge(sem("w_lo"), 16 * it + (u0 + j + 1))
                        i = j % 8
                        if j < 8:
                            if j >= 2:
                                pe.wait_ge(sem("hid"), 8 * it + (2 + h0 + j - 1))
                        elif i >= 2:
                            pe.wait_ge(sem("mlp_added"), 8 * it + (1 + h0 + i - 1))
                        else:
                            pe.wait_ge(sem("mlp_added"), 8 * it + (1 + h0))
                        for k in range(KT):
                            if j == 8:
                                pe.wait_ge(sem("hid"), 8 * it + (2 + h0 + k + 1))
                            b = ((Hh, Hl) if j < 8 else (HIDh, HIDl))
                            ins = mm3(ps[:, 2 * (j // 8) + j % 2, 0:T], wtile((u0 + j) % SLOTS, P * k, P),
                                      (b[0][:, k, 0:T], b[1][:, k, 0:T]), k == 0, k == KT - 1)
                        ins.then_inc(sem("w_used"), 1)
                        if j % 2:
                            a = a0 + j // 2
                            ada_mm(None, j // 2, a % ADA_SLOTS, 2 * it + (a // ADA_SLOTS + 1), 1 * it + g0)
                    ada_turn(1 * it + g0)

            Hx = (lambda k: Hh[:, k, :], lambda k: Hl[:, k, :])
            Gx = (lambda k: Gh[:, k, :], lambda k: Gl[:, k, :])
            Cx = (lambda k: CQh[:, k, :], lambda k: CQl[:, k, :])

            def ada_static(a):
                ada_mm(a, a % KT, a % ADA_SLOTS, a // ADA_SLOTS + 1, a // KT)

            pe.wait_ge(sem("cst_landed"), 16)
            pe.wait_ge(sem("lam_prod"), 1)
            pe.matmul(ps[:, 5, 0:2], ones, lam[:, 0:2], start=True, stop=True).then_inc(sem("lam_sum"), 1)
            sums(norms["l0a"])
            pe.wait_ge(sem("scs_ready"), 1)
            pe.wait_ge(sem("var"), 1)
            for a in range(2 * KT):
                ada_static(a)
                if a % KT == KT - 1:
                    ada_turn(a // KT)
            pe.wait_ge(sem("ada_ready"), 2)
            spread(norms["l0a"])

            def ada_between(i):
                if i == 6:
                    ada_turn(2)
                for a in range(2 * KT * i // 12, 2 * KT * (i + 1) // 12):
                    ada_static(2 * KT + a)

            project(p_l0, 0, L0_FM, Hx, ready=norms["l0a"].h0, after=ada_between)
            values(U_L0 + L0_FM, V_L0, 4, Hx, after=lambda h: ada_between(L0_FM + h))
            ada_turn(3)
            pe.wait_ge(sem("proj_out"), V_L0 + 4)
            pe.wait_ge(sem("rope_out"), 5)
            pe.wait_ge(sem("ada_ready"), 4)
            pe.wait_ge(sem("l0_zeros"), 1)
            attend(*J_L0)
            pe.wait_ge(sem("o_lo"), HL[J_L0[1] - 1])
            project_out(U_L0_OUT, 0, 512, Hx)
            sums(norms["l0b"])
            spread(norms["l0b"])
            mlp(U_L0_MLP, 0, 512, norms["l0b"].h0, 4 * KT, 4)
            pe.wait_ge(sem("ada_ready"), 8)
            sums(norms["l1a"])
            spread(norms["l1a"])
            project(p_l1, 0, L1_FM, Hx, ready=norms["l1a"].h0)
            for c in range(4):
                values(U_L1 + L1_FM + 2 * c, V_L1 + 4 * c, 4, Hx)
            pe.wait_ge(sem("proj_out"), V_L1 + 16)
            pe.wait_ge(sem("rope_out"), p_l1.r0 + 16)
            pe.wait_ge(sem("l1_zeros"), 1)
            attend(*J_L1)
            pe.wait_ge(sem("sub_lo"), 16)
            project_out(U_L1_OUT, 8, 256, Hx)
            sums(norms["l1b"])
            spread(norms["l1b"])
            mlp(U_L1_MLP, 32, 256, norms["l1b"].h0, 8 * KT, 8)
            pe.wait_ge(sem("ada_ready"), 12)
            sums(norms["fin"])
            spread(norms["fin"])
            for l in range(2):
                u0 = U_B2 + l * B2_UNITS
                project(p_a[l], 0, B2_FM1, Gx, ready=norms["fin" if l == 0 else "ln0"].h0)
                project(p_b[l], 0, 2, Gx)
                sums(norms[f"q{l}"])
                project(p_b[l], 2, 4, Gx)
                spread(norms[f"q{l}"])
                project(p_b[l], 4, 5, Gx)
                sums(norms[f"kv{l}"])
                project(p_b[l], 5, 7, Gx)
                spread(norms[f"kv{l}"])
                project(p_b[l], 7, B2_FM2, Gx)
                values(u0 + 23, V_B2[l], 2, Gx)
                pe.wait_ge(sem("ki_shift"), l + 1)
                for h in range(8):
                    o = O_IX[l] + h
                    pe.wait_ge(sem("proj_out"), o - 3)
                    q, ki = KQ[:, 5 + h // 2, :], KI[:, h % 2, :]
                    pe.matmul(ps[:, o % 4, 0:P], q[:, 0:P], ki[:, 0:P], start=True, stop=True)
                    pe.matmul(ps[:, o % 4, P:3 * P], q[:, P:2 * P], ki, start=True, stop=True).then_inc(sem("ix_ps"), 1)
                for c in range(1, 3):
                    values(u0 + 23 + 2 * c, V_B2[l] + 8 + 2 * c, 2, Gx)
                project(p_g[l], 0, KT, Gx)
                project(p_uq[l], 0, 6, Cx, kts=6, ready=norms[f"q{l}"].h0)
                pe.wait_ge(sem("nlo"), norms[f"kv{l}"].h0 + 2)
                u = u0 + 43
                pe.wait_ge(sem("w_lo"), u + 1)
                for m in range(3):
                    o = p_uk[l] + m
                    pe.wait_ge(sem("proj_out"), o - 3)
                    for k in range(2):
                        ins = mm3(ps[:, o % 4, 0:N], wtile(u % SLOTS, P * (2 * m + k), P),
                                  (Cx[0](6 + k), Cx[1](6 + k)), k == 0, k == 1)
                ins.then_inc(sem("w_used"), 1)
                u = u0 + 44
                pe.wait_ge(sem("w_lo"), u + 1)
                for t in range(2):
                    o = V_UV[l] + t
                    pe.wait_ge(sem("proj_out"), o - 3)
                    for k in range(2):
                        ins = mm3(ps[:, o % 4, 0:384], (Cx[0](6 + k)[:, P * t:P * t + P], Cx[1](6 + k)[:, P * t:P * t + P]),
                                  wtile(u % SLOTS, 384 * k, 384), k == 0, k == 1)
                ins.then_inc(sem("w_used"), 1)
                pe.wait_ge(sem("proj_out"), V_UV[l] + 2)
                pe.wait_ge(sem("rope_out"), p_uq[l].r0 + 6)
                pe.wait_ge(sem("kr_done"), l + 1)
                attend(*J_B2[l])
                pe.wait_ge(sem("o_lo"), HL[J_B2[l][1] - 1])
                project_out(u0 + 45, 16 + 8 * l, 256, Gx)
                for k in range(KT):
                    pe.wait_ge(sem("out_added"), 16 + 8 * l + k + 1)
                    ins = pe.matmul(ps[:, 7, 0:N], ones, X[:, k, 0:N], start=(k == 0), stop=(k == KT - 1))
                ins.then_inc(sem("mean_sum"), 1)
                sums(norms[f"ln{l}"])
                spread(norms[f"ln{l}"])


def feature_units(w):
    k, n = w.shape
    u = w.reshape(k // P, P, n // P, P).transpose(2, 1, 0, 3).reshape(n // P, P, k)
    return np.concatenate([u, np.zeros((n // P, P, 1024 - k), w.dtype)], axis=2) if k < 1024 else u


def value_units(w):
    c = w.shape[1] // N
    return w.reshape(2, 4, P, c, N).transpose(3, 0, 2, 1, 4).reshape(2 * c, P, 1024)


def mlp_units(w1, w2):
    parts = []
    for q in range(QUARTERS):
        parts += [feature_units(w1[:, 1024 * q:1024 * q + 1024]), feature_units(w2[1024 * q:1024 * q + 1024, :])]
    return np.concatenate(parts)


def one_unit(parts):
    row = np.concatenate(parts, axis=1)
    return np.concatenate([row, np.zeros((P, 1024 - row.shape[1]), row.dtype)], axis=1)[None]


def cols(v):
    return v.reshape(-1, P).T


PAIRS = [0, 4, 1, 5, 2, 6, 3, 7]


def weight_stream(a):
    we, wo = a["even_w_in"][0], a["odd_w_in"][0]
    aq, ak, av, bq, bk, bv = (we[:, x:y] for x, y in ((0, 512), (512, 640), (640, 768), (768, 1280), (1280, 1408),
                                                      (1408, 1536)))

    def pair(w):
        return w.reshape(1024, 8, 64)[:, PAIRS].reshape(1024, 512)

    w_out = a["even_w_out"][0].reshape(2, 8, 64, 1024)[:, PAIRS].reshape(1024, 1024)
    parts = [feature_units(np.concatenate([pair(aq), ak, pair(bq), bk], axis=1)),
             value_units(np.concatenate([av, bv], axis=1)), feature_units(w_out),
             mlp_units(a["mlp_w1"][0], a["mlp_w2"][0]),
             feature_units(wo[:, 0:2048]), value_units(wo[:, 2048:3072]), feature_units(a["odd_w_out"][0]),
             mlp_units(a["mlp_w1"][1], a["mlp_w2"][1])]
    for l in range(2):
        w = a["w_in_2"][l]
        s = np.cumsum([0, 768, 256, 32, 384, 384, 384, 256, 256, 256, 512, 64, 8, 1024])
        cq, ckv, kr, qb, kb, vb, qc, kc, vc, qi, ki, wi, gate = (w[:, s[i]:s[i + 1]] for i in range(13))
        z = np.zeros((1024, 120), w.dtype)
        uq = a["w_uq_2"][l].reshape(768, 6, 96)
        uq = np.concatenate([uq, np.zeros((768, 6, 32), w.dtype)], axis=2).reshape(768, 768)
        uk, uv = a["w_uk_2"][l], a["w_uv_2"][l]
        parts += [feature_units(np.concatenate([cq, ckv, ki, kr, z[:, 0:32], qb, kb, qc, kc, qi], axis=1)),
                  value_units(np.concatenate([vc[:, P:], wi, z, vb, vc[:, :P]], axis=1)), feature_units(gate), feature_units(uq),
                  one_unit([uk[P * k:P * k + P, P * m:P * m + P] for m in range(3) for k in range(2)]),
                  one_unit([uv[0:P], uv[P:2 * P]]), feature_units(a["w_out_2"][l])]
    return np.concatenate(parts)


def ada_stream(a):
    w = np.concatenate([a["ada_w"][0], a["ada_w"][1], a["w_ada_2"][0], a["w_ada_2"][1]], axis=1)
    return w.reshape(KT, P, 12, GROUP).transpose(2, 0, 1, 3).reshape(12 * KT, P, GROUP)


def constants():
    c = np.zeros((P, C_END), np.float32)
    c[:, C_ID:C_ID + P] = np.eye(P)
    c[:, C_ONE:C_ONE + P] = 1.0
    for m in range(P):
        k, v = (m + 16, -1.0) if m % 32 < 16 else (m - 16, 1.0)
        c[k, C_RQ + m] = v
        if 64 <= m < 96:
            c[k, C_RM + m] = v
    t = np.arange(N)
    inv = (10000.0 ** (-np.arange(16) / 16.0)).astype(np.float32)
    row, col = (t // 64).astype(np.float32), (t % 64).astype(np.float32)
    ang = np.concatenate([np.outer(inv, row)] * 2 + [np.outer(inv, col)] * 2).astype(np.float32)
    c[:, C_COS:C_COS + N] = np.cos(np.concatenate([ang, ang]))
    c[:, C_SIN:C_SIN + N] = np.sin(np.concatenate([ang, ang]))
    angm = np.outer(inv, t.astype(np.float32)).astype(np.float32)
    c[:, C_COSM:C_COSM + N] = 1.0
    c[64:96, C_COSM:C_COSM + N] = np.cos(np.concatenate([angm, angm]))
    c[64:96, C_SINM:C_SINM + N] = np.sin(np.concatenate([angm, angm]))
    q, k = np.arange(N)[:, None], np.arange(N)[None, :]
    win = np.where(np.abs(q - k) <= 128, 0.0, NEG)
    start = np.clip(q % 64 - 8, 0, 48)
    nbr = np.where((k % 64 >= start) & (k % 64 < start + 16), 0.0, NEG)
    cau = np.where(k <= q, 0.0, NEG)
    for x, c0 in ((win, C_WIN), (nbr, C_NBR)):
        c[:, c0:c0 + 2 * N] = x.reshape(2, P, N).transpose(1, 0, 2).reshape(P, 2 * N)
    c[:, C_CAU:C_CAU + P] = cau[0:P, 0:P]
    c[:, C_CAU + P:C_CAU + 3 * P] = cau[P:]
    d = q - k
    count = ((d >= 0) & (d <= 128)) * 1.0 + ((d >= 0) & (d % 4 == 0)) + ((d >= 0) & (d % 16 == 0))
    ali = np.zeros((P, 10, 384), np.float32)
    for h in range(10):
        slope = 2.0 ** (-8.0 * (h + 1) / 10)
        x = -slope * d + (np.where(count > 0, np.log(np.maximum(count, 1.0)), NEG) if h < 6
                          else np.where(d >= 0, 0.0, NEG))
        ali[:, h, 0:P] = x[0:P, 0:P]
        ali[:, h, P:] = x[P:]
    return c, ali


def parameters(a):
    p = np.zeros((P, P_END), np.float32)
    p[:, P_CV:P_CV + 24] = np.stack([cols(a["c"][0]), cols(a["c_ctx"]), cols(a["c_2"][0])], axis=2).reshape(P, 24)
    p[:, P_AB:P_AB + 144] = cols(np.concatenate([a["ada_b"][0], a["ada_b"][1], a["b_ada_2"][0], a["b_ada_2"][1]]))
    p[:, P_N1:P_N1 + 16] = cols(a["norm1_g"].reshape(-1))
    p[:, P_N2:P_N2 + 16] = cols(a["norm2_g"].reshape(-1))
    p[:, P_FIN:P_FIN + 8] = cols(a["final_g"])
    p[:, P_LNG:P_LNG + 16] = cols(a["ln_g_2"].reshape(-1))
    p[:, P_LNB:P_LNB + 16] = cols(a["ln_b_2"].reshape(-1))
    p[:, P_QN:P_QN + 12] = cols(a["q_norm_g_2"].reshape(-1))
    p[:, P_KVN:P_KVN + 4] = cols(a["kv_norm_g_2"].reshape(-1))
    p[:, P_SUB:P_SUB + 1] = cols(a["subln_g"].reshape(-1))
    p[:, P_SINK:P_SINK + 8] = np.broadcast_to(a["a_sink"][0][PAIRS], (P, 8))
    for i, name in enumerate(("lam_q1", "lam_q2", "lam_k1", "lam_k2")):
        p[0:64, P_LAM + i] = a[name][0]
    return p


def tokens(x):
    return x.reshape(N, KT, P).transpose(2, 1, 0)


def kernel(**inputs):
    import concourse.bacc as bacc
    from concourse.bass_utils import run_bass_kernel_spmd

    a = {k: np.asarray(v) for k, v in inputs.items()}
    const, ali = constants()
    pad = np.zeros((8, 7, 127), np.float32)
    pad[:, :, 48:79] = a["b_rpb"][0][PAIRS][:, 4:11]
    rpb = np.stack([pad[:, :, 63 - q:127 - q] for q in range(64)]).reshape(64, 8, 7 * 64)
    arrays = {
        "wall": weight_stream(a), "aall": ada_stream(a), "const": const, "prm": parameters(a),
        "xin": np.concatenate([tokens(a["x"][0]), tokens(a["ctx"][0])], axis=2), "rpb": rpb, "ali": ali,
    }
    arrays = {k: np.ascontiguousarray(v) for k, v in arrays.items()}
    assert arrays["wall"].shape == (UNITS, P, 1024) and arrays["aall"].shape == (ADA_UNITS, P, GROUP)
    nc = bacc.Bacc("TRN2", target_bir_lowering=False, num_devices=1)
    args = [nc.dram_tensor(k, v.shape, mybir.dt.from_np(v.dtype), kind="ExternalInput").ap() for k, v in arrays.items()]
    out = nc.dram_tensor("out", (P, KT, N), F32, kind="ExternalOutput").ap()
    program(nc, *args, out)
    r = run_bass_kernel_spmd(nc, [arrays], core_ids=[0])
    return r.results[0]["out"].transpose(2, 1, 0).reshape(1, N, D)
```

```python
import math
from contextlib import ExitStack

import concourse.bass as bass
import numpy as np
from concourse import mybir

F32 = mybir.dt.float32
F32R = mybir.dt.float32r
ALU = mybir.AluOpType
ACT = mybir.ActivationFunctionType
AX = mybir.AxisListType

P = 128
D = 1024
KT = D // P
N = 256
SLOTS = 4
TOGETHER = 3
AHEAD = 3
ADA_SLOTS = 4
ADA_N = 384
GROUP = 4 * ADA_N
HID_BANKS = (0, 1, 4, 5)
QUARTERS = 4
NEG = -1.0e30
TAKEN = -3.0e38
TOPK = 64
LAM_INIT = 0.8 - 0.6 * math.exp(-0.3)
ALPHA = 4 ** 0.25

C_ID, C_ONE, C_RQ, C_RM = 0, 128, 256, 384
C_COS, C_SIN, C_COSM, C_SINM = 512, 768, 1024, 1280
C_WIN, C_NBR, C_CAU = 1536, 2048, 2560
C_END = 2944
P_CV, P_AB, P_N1, P_N2, P_FIN, P_LNG, P_LNB, P_QN, P_KVN, P_SUB, P_SINK, P_LAM = (
    0, 24, 168, 184, 200, 208, 224, 240, 252, 256, 257, 265)
P_END = 269

U_L0 = 0
L0_FM = 10
U_L0_OUT = L0_FM + 2
U_L0_MLP = U_L0_OUT + KT
MLP_UNITS = QUARTERS * 16
U_L1 = U_L0_MLP + MLP_UNITS
L1_FM = 16
U_L1_OUT = U_L1 + L1_FM + 8
U_L1_MLP = U_L1_OUT + KT
U_B2 = U_L1_MLP + MLP_UNITS
B2_FM1 = 9
B2_FM2 = 14
B2_UNITS = B2_FM1 + B2_FM2 + 6 + KT + 6 + 1 + 1 + KT
UNITS = U_B2 + 2 * B2_UNITS
FIRST = 5
NARROW = 3
ADA_GROUPS = FIRST + 8
ADA_UNITS = ADA_GROUPS * KT


def ada_width(g):
    return 256 if isinstance(g, int) and g < NARROW else ADA_N


def program(nc, wall, aall, const, prm, xin, rpb, ali, out):
    with ExitStack() as top:
        def sb(name, shape, dt=F32, scope=top):
            return scope.enter_context(nc.sbuf_tensor(name, shape, dt))

        sems = {}

        def sem(name):
            if name not in sems:
                sems[name] = top.enter_context(nc.semaphore(name))
            return sems[name]

        ps = top.enter_context(nc.psum_tensor("ps", [P, 8, 512], F32))

        X = sb("X", [P, KT, 2 * N])
        raw = sb("raw", [P, SLOTS, 1024])
        whi = sb("whi", [P, SLOTS, 1024], F32R)
        wlo = sb("wlo", [P, SLOTS, 1024], F32R)
        wk1 = sb("wk1", [P, 4, 512])
        wk2 = sb("wk2", [P, 4, 512])
        RS = sb("RS", [P, 512])
        VR = sb("VR", [P, 2, 4])
        cst = sb("cst", [P, C_END])
        par = sb("par", [P, P_END])
        ada = sb("ada", [P, 3, 3 * 48])
        SC = sb("SC", [P, 24, 8])
        small = sb("small", [P, 4, 16])
        lam = sb("lam", [P, 8])
        nsink = sb("nsink", [P, 8])
        mhalf = sb("mhalf", [P, 1])

        ident = cst[:, C_ID:C_ID + P]
        ones = cst[:, C_ONE:C_ONE + P]
        E = wk1[:, :, :].rearrange("p (g r) n -> p g r n", g=2)
        PT = wk2[:, :, :].rearrange("p (g r) n -> p g r n", g=2)
        SQ = wk1
        Y = wk2[:, 0:2, :]
        DG = RS[:, :].rearrange("p (g r n) -> p g r n", g=2, r=2)
        OS = RS[:, 0:N].rearrange("p (g n) -> p g n", g=2)
        DS = RS[:, N:2 * N].rearrange("p (g n) -> p g n", g=2)
        M = wk2[:, 2:4, :]
        SEL = wk2[:, 0, 0:384]

        def RI(h):
            return (wk2 if h < 4 else wk1)[:, h % 4, 0:384]


        b1 = ExitStack()
        Hh = sb("Hh", [P, KT, 2 * N], F32R, b1)
        Hl = sb("Hl", [P, KT, 2 * N], F32R, b1)
        aring = sb("aring", [P, ADA_SLOTS, GROUP], F32, b1)
        AR = sb("AR", [P, ADA_N], F32, b1)
        scs = sb("scs", [P, KT, 32], F32, b1)
        stp = sb("stp", [P, 2, KT, 3], F32, b1)
        s0 = ExitStack()
        Q0 = sb("Q0", [P, 8, 2 * N], F32, s0)
        K0 = sb("K0", [P, 2, 2, 2 * N], F32, s0)
        V0 = sb("V0", [P, 4, N], F32, s0)
        BI = sb("BI", [P, 2, 8, N], F32, s0)
        s0.close()
        s1 = ExitStack()
        Q1 = sb("Q1", [P, 8, 2, N], F32, s1)
        K1 = sb("K1", [P, 8, 2 * N], F32, s1)
        V1 = sb("V1", [P, 4, D], F32, s1)
        s1.close()

        sm = ExitStack()
        HIDh = sb("HIDh", [P, KT, 2 * N], F32R, sm)
        HIDl = sb("HIDl", [P, KT, 2 * N], F32R, sm)
        sm.close()
        b1.close()
        b2 = ExitStack()
        Gh = sb("Gh", [P, KT, N], F32R, b2)
        Gl = sb("Gl", [P, KT, N], F32R, b2)
        QZ = sb("QZ", [P, 5, 2, N], F32, b2)
        KQ = sb("KQ", [P, 9, N], F32, b2)
        V2 = sb("V2", [P, 2, 3 * N], F32, b2)
        GT = sb("GT", [P, KT, N], F32, b2)
        QA = sb("QA", [P, 6, N], F32, b2)
        KA = sb("KA", [P, 6, N], F32, b2)
        VA = sb("VA", [P, 2, 384], F32, b2)
        KK = sb("KK", [P, N], F32, b2)
        KI = sb("KI", [P, 2, N], F32, b2)
        AL = sb("AL", [P, 10, 384], F32, b2)
        MO = sb("MO", [P, 2, P], F32, b2)
        WI = sb("WI", [P, 2, 8], F32, b2)
        IX = sb("IX", [P, 384], F32, b2)
        M8 = sb("M8", [P, 16], F32, b2)
        PQ = sb("PQ", [P, 8, N], F32, b2)
        CQh = sb("CQh", [P, 8, N], F32R, b2)
        CQl = sb("CQl", [P, 8, N], F32R, b2)
        b2.close()

        KOFF, KLEN = (0, P), (P, 2 * P)

        class Norm:

            def __init__(self, src, n, T, width, streams, dst, eps=1e-6, keep=None, ready=None,
                         direct=False):
                self.src, self.n, self.T, self.width, self.eps = src, n, T, width, eps
                self.streams = streams
                self.dst = dst
                self.keep = keep
                self.ready = ready
                self.direct = direct

        def adacol(s, v, t):
            return ada[:, v, 48 * s + t:48 * s + t + 1]

        def xt(k, T):
            return X[:, k, 0:T]

        def mod(scale_row, s, v, t0):
            return lambda k: SC[:, scale_row, k:k + 1], lambda k: adacol(s, v, t0 + k)

        Hd = (lambda k: Hh[:, k, :], lambda k: Hl[:, k, :])
        Hdx = (lambda k: Hh[:, k, 0:N], lambda k: Hl[:, k, 0:N])
        Gd = (lambda k: Gh[:, k, :], lambda k: Gl[:, k, :])

        def counted(name, base):
            return lambda k: [(name, base + k + 1)]

        norms = {}
        norms["l0a"] = Norm(xt, 8, 512, D, [(0, *mod(0, 0, 0, 0)), (N, *mod(1, 0, 1, 0))], Hd,
                            ready=lambda k: [("x_landed", 16)])
        norms["l0b"] = Norm(xt, 8, 512, D, [(0, *mod(2, 0, 0, 24)), (N, *mod(3, 0, 1, 24))], Hd,
                            ready=counted("out_added", 0))
        norms["l1a"] = Norm(xt, 8, 512, D, [(0, *mod(4, 1, 0, 0)), (N, *mod(5, 1, 1, 0))], Hd,
                            ready=counted("mlp_added", 25))
        norms["l1b"] = Norm(xt, 8, 256, D, [(0, *mod(6, 1, 0, 24))], Hdx, ready=counted("out_added", 8))
        norms["fin"] = Norm(xt, 8, 256, D, [(0, *mod(8, 2, 2, 0))], Gd, ready=counted("mlp_added", 57),
                            keep=(lambda k: X[:, k, 0:N], lambda k: par[:, P_FIN + k:P_FIN + k + 1], None))
        for l in range(2):
            norms[f"q{l}"] = Norm(lambda k, T: PQ[:, k, 0:T], 6, 256, 768,
                                  [(0, lambda k, l=l: par[:, P_QN + 6 * l + k:P_QN + 6 * l + k + 1], None)],
                                  (lambda k: CQh[:, k, :], lambda k: CQl[:, k, :]),
                                  ready=lambda k: [])
            norms[f"kv{l}"] = Norm(lambda k, T: PQ[:, 6 + k, 0:T], 2, 256, 256,
                                   [(0, lambda k, l=l: par[:, P_KVN + 2 * l + k:P_KVN + 2 * l + k + 1], None)],
                                   (lambda k: CQh[:, 6 + k, :], lambda k: CQl[:, 6 + k, :]),
                                   ready=lambda k: [], direct=True)
            norms[f"ln{l}"] = Norm(xt, 8, 256, D, [(0, *mod(9, 2, 2, 24))] if l == 0 else [],
                                   Gd if l == 0 else None, eps=1e-5, ready=counted("centred", 8 * l), direct=True,
                                   keep=(lambda k: X[:, k, 0:N],
                                         lambda k, l=l: par[:, P_LNG + 8 * l + k:P_LNG + 8 * l + k + 1],
                                         lambda k, l=l: par[:, P_LNB + 8 * l + k:P_LNB + 8 * l + k + 1]))

        order = ["l0a", "l0b", "l1a", "l1b", "fin", "q0", "kv0", "ln0", "q1", "kv1", "ln1"]
        tiles = split_tiles = 0
        for idx, name in enumerate(order):
            n = norms[name]
            n.t0, n.h0, n.idx = tiles, split_tiles, idx
            tiles += n.n
            split_tiles += n.n if n.dst else 0

        class Tile:

            def __init__(self, T, rope, dst, rest=()):
                self.T, self.rope = T, rope
                self.dst = dst if isinstance(dst, list) else [(slice(0, dst.shape[0]), dst)]
                self.rest = rest

        class Proj:
            outs = 0
            ropes = 0

            def __init__(self, u0, tiles):
                self.u0, self.tiles = u0, tiles
                self.o0, self.r0 = Proj.outs, Proj.ropes
                Proj.outs += len(tiles)
                Proj.ropes += sum(t.rope is not None for t in tiles)

            def rope_index(self, i):
                return self.r0 + sum(t.rope is not None for t in self.tiles[:i])

        def rows(r):
            return slice(64 * r, 64 * r + 64)

        def halves(ap):
            return [(rows(r), ap(r)[rows(r)]) for r in range(2)]

        def l0_tile(i):
            if i < 4:
                return Tile(512, "q", Q0[:, i, 0:N], [(slice(0, P), Q0[:, i, N:2 * N])])
            if i == 4:
                return Tile(512, "q", halves(lambda r: K0[:, 0, r, 0:N]), halves(lambda r: K0[:, 0, r, N:2 * N]))
            if i < 9:
                return Tile(512, None, Q0[:, i - 1, :])
            return Tile(512, None, halves(lambda r: K0[:, 1, r, :]))

        p_l0 = Proj(U_L0, [l0_tile(i) for i in range(L0_FM)])
        V_L0 = Proj.outs
        Proj.outs += 4
        p_l1 = Proj(U_L1, [Tile(256, "q", halves(lambda r, i=i: Q1[:, i, r, :])) for i in range(8)]
                    + [Tile(512, "q", K1[:, i, 0:N], [(slice(0, P), K1[:, i, N:2 * N])]) for i in range(8)])

        def b2_tile(i):
            if i < 3 or 6 <= i < 8:
                n = i if i < 3 else i - 3
                return Tile(256, None, halves(lambda r: QZ[:, n, r, :]))
            return Tile(256, None, KQ[:, i - 3 if i < 6 else i - 5, :])

        V_L1 = Proj.outs
        Proj.outs += 16
        O_IX = []
        p_a, p_b, V_B2, p_g, p_uq, p_uk, V_UV = [], [], [], [], [], [], []
        for l in range(2):
            u = U_B2 + l * B2_UNITS
            p_a.append(Proj(u, [Tile(256, None, PQ[:, i, :]) for i in range(8)] + [Tile(256, "m", KK[0:96, :])]))
            p_b.append(Proj(u + 9, [b2_tile(i) for i in range(B2_FM2)]))
            V_B2.append(Proj.outs)
            Proj.outs += 2
            O_IX.append(Proj.outs)
            Proj.outs += 8
            Proj.outs += 4
            p_g.append(Proj(u + 29, [Tile(256, None, GT[:, i, :]) for i in range(KT)]))
            p_uq.append(Proj(u + 37, [Tile(256, "m", QA[0:96, i, :]) for i in range(6)]))
            p_uk.append(Proj.outs)
            Proj.outs += 3
            V_UV.append(Proj.outs)
            Proj.outs += 2

        class Job:

            def __init__(self, q, k, nk, bias, pre, post, v, dst, sink=None, diff=False, gate=None):
                self.q, self.k, self.nk, self.bias, self.pre, self.post = q, k, nk, bias, pre, post
                self.v, self.dst, self.sink, self.diff, self.gate = v, dst, sink, diff, gate

        def two(ap, n):
            return ap[:, None, :].to_broadcast([P, 2, n])

        jobs = []
        for kind in range(2):
            for i in range(4):
                for t in range(4):
                    ctx_q = t >= 2
                    t2 = t % 2
                    bias = None
                    if not ctx_q:
                        bias = (two(cst[:, C_WIN + N * t2:C_WIN + N * t2 + N], N) if kind == 0
                                else BI[:, t2, 2 * i:2 * i + 2, :])
                    k0 = N if ctx_q else 0
                    jobs.append(Job(
                        q=[Q0[:, 4 * kind + i, P * t:P * t + P] for r in range(2)],
                        k=[K0[:, kind, r, k0:2 * N] for r in range(2)],
                        nk=2 * N - k0, bias=bias, pre=1.0, post=0.125,
                        v=(lambda kt, r, kind=kind, k0=k0: V0[:, k0 // P + kt, P * kind + 64 * r:P * kind + 64 * r + 64]),
                        dst=(Hh[:, 4 * kind + i, P * t:P * t + P], Hl[:, 4 * kind + i, P * t:P * t + P]),
                        sink=(2 * i if kind == 0 else None)))
        J_L0 = (0, len(jobs))
        for h in range(8):
            for t in range(2):
                jobs.append(Job(
                    q=[Q1[:, h, r, P * t:P * t + P] for r in range(2)],
                    k=[K1[:, h, :] for r in range(2)], nk=2 * N, bias=None, pre=1.0, post=0.125,
                    v=(lambda kt, r, h=h: V1[:, kt, P * h:P * h + P]),
                    dst=(Hh[:, h, P * t:P * t + P], Hl[:, h, P * t:P * t + P]), diff=True))
        J_L1 = (J_L0[1], len(jobs))
        J_B2 = []
        for l in range(2):
            j0 = len(jobs)
            for i in range(3):
                for t in range(2):
                    jobs.append(Job(
                        q=[QA[0:96, 2 * i + r, P * t:P * t + P] for r in range(2)],
                        k=[KA[0:96, 2 * i + r, 0:KLEN[t]] for r in range(2)], nk=KLEN[t],
                        bias=two(cst[:, C_CAU + KOFF[t]:C_CAU + KOFF[t] + KLEN[t]], KLEN[t]),
                        pre=96 ** -0.5, post=1.0,
                        v=(lambda kt, r, i=i: VA[:, kt, 64 * (2 * i + r):64 * (2 * i + r) + 64]),
                        dst=(Gh[:, i, P * t:P * t + P], Gl[:, i, P * t:P * t + P]), gate=GT[:, i, P * t:P * t + P]))
            for i in range(3):
                for t in range(2):
                    jobs.append(Job(
                        q=[QZ[:, i, r, P * t:P * t + P] for r in range(2)],
                        k=[KQ[:, i, 0:KLEN[t]] for r in range(2)], nk=KLEN[t],
                        bias=AL[:, 2 * i:2 * i + 2, KOFF[t]:KOFF[t] + KLEN[t]], pre=0.125, post=1.0,
                        v=(lambda kt, r, i=i: V2[:, kt, N + 64 * (2 * i + r):N + 64 * (2 * i + r) + 64]),
                        dst=(Gh[:, 3 + i, P * t:P * t + P], Gl[:, 3 + i, P * t:P * t + P]),
                        gate=GT[:, 3 + i, P * t:P * t + P]))
            for i in range(2):
                for t in range(2):
                    jobs.append(Job(
                        q=[QZ[:, 3 + i, r, P * t:P * t + P] for r in range(2)],
                        k=[KQ[:, 3 + i, 0:KLEN[t]] for r in range(2)], nk=KLEN[t],
                        bias=AL[:, 6 + 2 * i:8 + 2 * i, KOFF[t]:KOFF[t] + KLEN[t]], pre=0.125, post=1.0,
                        v=(lambda kt, r, i=i: V2[:, kt, 640 * (1 - i) + 64 * r:640 * (1 - i) + 64 * r + 64]),
                        dst=(Gh[:, 6 + i, P * t:P * t + P], Gl[:, 6 + i, P * t:P * t + P]),
                        gate=GT[:, 6 + i, P * t:P * t + P]))
            J_B2.append((j0, len(jobs)))
        GJOB = {g: n for n, g in enumerate(g for g in range(len(jobs)) if jobs[g].gate is not None)}
        HL = {}
        for g in range(len(jobs)):
            HL[g] = sum(1 for j in jobs[:g + 1] if not j.diff)

        block = top.enter_context(nc.Block())


        for l in range(2):
            norms[f"q{l}"].ready = lambda k, l=l: [("proj_out", p_a[l].o0 + 9), ("rope_out", p_a[l].r0 + 1)]

        @block.sync
        def _(sp):
            def weight(u, slot):
                if not isinstance(u, int) or u >= SLOTS:
                    sp.wait_ge(sem("w_lo"), u - (SLOTS - 1))
                src = wall[u] if isinstance(u, int) else wall[bass.ds(u, 1), :, :].rearrange("a p n -> p (a n)")
                sp.dma_start(raw[:, slot, :], src).then_inc(sem(f"w_landed{slot}"), 16)

            def ada_unit(a, slot):
                if not isinstance(a, int) or a >= ADA_SLOTS:
                    sp.wait_ge(sem("a_used"), a - (ADA_SLOTS - 1))
                n = 4 * ada_width(a // KT if isinstance(a, int) else a)
                src = aall[a, :, 0:n] if isinstance(a, int) else aall[bass.ds(a, 1), :, :].rearrange("a p n -> p (a n)")
                sp.dma_start(aring[:, slot, 0:n], src).then_inc(sem(f"a_landed{slot}"), 16)

            def mlp_loads(u0, a0=None):
                with sp.Fori(0, QUARTERS) as it:
                    for j in range(16):
                        weight(16 * it + (u0 + j), (u0 + j) % SLOTS)
                        if a0 is not None:
                            ada_unit(16 * it + (a0 + j), (a0 + j) % ADA_SLOTS)

            sp.dma_start(par[:, :], prm).then_inc(sem("par_landed"), 16)
            sp.dma_start(cst[:, 0:C_COS], const[:, 0:C_COS]).then_inc(sem("cst_landed"), 16)
            for a in range(ADA_SLOTS):
                ada_unit(a, a)
            sp.dma_start(X[:, :, :], xin).then_inc(sem("x_landed"), 16)
            for a in range(ADA_SLOTS, 2 * KT):
                ada_unit(a, a % ADA_SLOTS)
            for u in range(SLOTS):
                weight(u, u)
            sp.dma_start(cst[:, C_COS:], const[:, C_COS:]).then_inc(sem("tables_landed"), 16)
            for u in range(SLOTS, U_L0_MLP):
                weight(u, u % SLOTS)
                i = u - SLOTS
                if i < 12:
                    for a in range(2 * KT + 2 * i, 2 * KT + 2 * i + 2):
                        ada_unit(a, a % ADA_SLOTS)
                if i == 2:
                    for qr in range(4):
                        sp.dma_start(BI[64 * (qr % 2):64 * (qr % 2) + 64, qr // 2, :, :],
                                     rpb[:, :, 64 * (3 - qr):64 * (3 - qr) + N]).then_inc(sem("rpb_landed"), 16)
            mlp_loads(U_L0_MLP, FIRST * KT)
            for u in range(U_L1, U_L1_MLP):
                weight(u, u % SLOTS)
            mlp_loads(U_L1_MLP)
            for u in range(U_B2, UNITS):
                weight(u, u % SLOTS)
                if u == U_B2 + 8:
                    sp.wait_ge(sem("mlp_added"), 65)
                if 0 <= u - (U_B2 + 8) < 10:
                    h = u - (U_B2 + 8)
                    sp.dma_start(AL[:, h, :], ali[:, h, :]).then_inc(sem("ali_landed"), 16)
                if u == U_B2 + B2_UNITS + 8:
                    sp.wait_ge(sem("m_done"), J_B2[0][1])
                if 0 <= u - (U_B2 + B2_UNITS + 8) < 4:
                    h = 6 + u - (U_B2 + B2_UNITS + 8)
                    sp.dma_start(AL[:, h, :], ali[:, h, :]).then_inc(sem("ali_landed"), 16)
            for k in range(0, KT, 2):
                sp.wait_ge(sem("finished"), k + 2)
                sp.dma_start(out[:, k:k + 2, :], X[:, k:k + 2, 0:N]).then_inc(sem("stored"), 16)
            sp.wait_ge(sem("stored"), 16 * KT // 2)

        @block.scalar
        def _(act):
            def split_hi(u, slot, lap):
                act.wait_ge(sem(f"w_landed{slot}"), 16 * lap)
                if not isinstance(u, int) or u >= SLOTS:
                    act.wait_ge(sem("w_used"), u - (SLOTS - 1))
                act.activation(whi[:, slot, :], raw[:, slot, :], ACT.Copy).then_inc(sem("w_hi"), 1)

            def ahead(u):
                if u + AHEAD < UNITS:
                    v = u + AHEAD
                    split_hi(v, v % SLOTS, v // SLOTS + 1)

            def ada_rows(g):
                act.wait_ge(sem("a_used"), 8 * g + 8)
                if not isinstance(g, int) or g:
                    act.wait_ge(sem("ada_tr"), g)
                n = ada_width(g)
                act.activation(AR[:, 0:n], ps[:, 6, 0:n], ACT.Copy).then_inc(sem("ar_ready"), 1)

            def square(n, k):
                for name, value in n.ready(k):
                    act.wait_ge(sem(name), value)
                t = n.t0 + k
                if t >= 4:
                    act.wait_ge(sem("sq_used"), t - 3)
                act.activation(SQ[:, t % 4, 0:n.T], n.src(k, n.T), ACT.Square).then_inc(sem("sq"), 1)

            def squares(n):
                for k in range(n.n):
                    square(n, k)

            def his(n):
                for k in range(n.n):
                    act.wait_ge(sem("modded"), n.t0 + k + 1)
                    for c0, _, shift in n.streams:
                        c1 = min(c0 + N, n.T)
                        o, m = n.dst[0](k)[:, c0:c1], M[:, (n.t0 + k) % 2, c0:c1]
                        if n.keep or shift is None:
                            ins = act.activation(o, m, ACT.Copy)
                        else:
                            ins = act.activation(o, m, ACT.Identity, bias=shift(k))
                    ins.then_inc(sem("nhi"), 1)

            def evac(pr, i):
                t, o = pr.tiles[i], pr.o0 + i
                act.wait_ge(sem("w_used"), pr.u0 + i + 1)
                bank = ps[:, o % 4, :]
                if t.rope is None:
                    for p, dst in t.dst:
                        ins = act.activation(dst, bank[p, 0:t.T], ACT.Copy)
                    ins.then_inc(sem("proj_out"), 1)
                    return
                r = pr.rope_index(i)
                n = 128 if t.rope == "q" else 96
                if r >= 2:
                    act.wait_ge(sem("rope_out"), r - 1)
                ins = act.activation(wk1[0:n, r % 2, 0:N], bank[0:n, 0:N], ACT.Copy)
                for p, dst in t.rest:
                    ins = act.activation(dst, bank[p, N:2 * N], ACT.Copy)
                ins.then_inc(sem("proj_out"), 1)

            def evac_v(u, o0, dsts):
                act.wait_ge(sem("w_used"), u + 1)
                for t, dst in enumerate(dsts):
                    act.activation(dst, ps[:, (o0 + t) % 4, 0:dst.shape[1]], ACT.Copy).then_inc(sem("proj_out"), 1)

            def attend(j0, j1):
                for s in range(j0, j1 + (6 if jobs[j0].diff else 4)):
                    if j0 <= s - 6 < j1 and jobs[s - 6].diff:
                        g = s - 6
                        act.wait_ge(sem("sub_tr"), g - j0 + 1)
                        act.activation(jobs[g].dst[0], ps[:, 5, 0:P], ACT.Identity, scale=SC[:, 12, 0:1])\
                           .then_inc(sem("sub_hi"), 1)
                    if j0 <= s - 2 < j1:
                        g = s - 2
                        act.wait_ge(sem("t_done"), g + 1)
                        if g >= 2:
                            act.wait_ge(sem("pv_done"), g - 1)
                        act.activation(PT[:, g % 2, 0, 0:jobs[g].nk], ps[:, 4, 0:jobs[g].nk], ACT.Copy)\
                           .then_inc(sem("ev_a"), 1)
                    if j0 <= s - 4 < j1:
                        g = s - 4
                        j = jobs[g]
                        if j.diff:
                            act.wait_ge(sem("pv_done"), g + 1)
                            if g - 2 >= j0:
                                act.wait_ge(sem("sub_tr"), g - 2 - j0 + 1)
                            st = small[:, g % 4, :]
                            act.activation(OS[:, g % 2, :], ps[:, 6 + g % 2, 0:P], ACT.Identity, scale=st[:, 6:7])\
                               .then_inc(sem("sub_o"), 1)
                            act.wait_ge(sem("sub_o"), g - j0 + 1)
                            act.activation(DS[:, g % 2, :], OS[:, g % 2, :], ACT.Square, accum_out=st[:, 11:12])\
                               .then_inc(sem("sub_sq"), 1)
                        elif j.gate is None:
                            act.wait_ge(sem("pv_done"), g + 1)
                            act.activation(j.dst[0], ps[:, 6 + g % 2, 0:P], ACT.Copy).then_inc(sem("o_hi"), 1)
                        else:
                            act.wait_ge(sem("o_m"), GJOB[g] + 1)
                            act.activation(j.dst[0], MO[:, g % 2, :], ACT.Copy).then_inc(sem("o_hi"), 1)
                    if s < j1:
                        j = jobs[s]
                        act.wait_ge(sem("m_done"), s + 1)
                        if s >= 2:
                            act.wait_ge(sem("t_done"), s - 1)
                        st = small[:, s % 4, :]
                        if j.sink is not None:
                            act.activation(st[:, 8:10], st[:, 8:10], ACT.Exp)
                        for r in range(2):
                            ins = act.activation(E[:, s % 2, r, 0:j.nk], ps[:, 2 * (s % 2) + r, 0:j.nk], ACT.Exp,
                                                 bias=st[:, 2 + r:3 + r], scale=j.post,
                                                 accum_out=st[:, 4 + r:5 + r])
                        ins.then_inc(sem("x_done"), 1)

            def mlp(u0, h0, T, n, g0=None):
                def quarter(it, last=None):
                    for j in range(16):
                        v = u0 + j + AHEAD
                        split_hi(16 * it + v, v % SLOTS, 4 * it + (v // SLOTS + 1))
                        if j < 8:
                            act.wait_ge(sem("w_used"), 16 * it + (u0 + j + 1))
                            act.wait_ge(sem("hid"), 8 * it + (h0 + j + 1))
                            act.activation(Y[:, j % 2, 0:T], ps[:, HID_BANKS[j % 4], 0:T], ACT.Relu).then_inc(sem("hid_r"), 1)
                            act.wait_ge(sem("hid_r"), 8 * it + (h0 + j + 1))
                            act.activation(HIDh[:, j, 0:T], Y[:, j % 2, 0:T], ACT.Square).then_inc(sem("hid_h"), 1)
                        elif last and j > 8:
                            square(last, j - 9)
                        if j == 8 and g0:
                            ada_rows(2 * it + g0)
                    if last:
                        square(last, 7)
                    if g0:
                        ada_rows(2 * it + (g0 + 1))

                with act.Fori(0, QUARTERS - 1) as it:
                    quarter(it)
                quarter(QUARTERS - 1, n)

            def out_proj(u0, n):
                for i in range(KT):
                    ahead(u0 + i)
                    if i:
                        square(n, i - 1)
                square(n, KT - 1)

            act.wait_ge(sem("par_landed"), 16)
            act.activation(stp[:, 0, :, :], par[:, P_CV:P_CV + 24].rearrange("p (k v) -> p k v", v=3), ACT.Exp,
                           scale=-1.0).then_inc(sem("silu_e"), 1)
            act.wait_ge(sem("lam_sum"), 1)
            act.activation(lam[:, 2:4], ps[:, 5, 0:2], ACT.Exp).then_inc(sem("lam_e"), 1)
            squares(norms["l0a"])
            ada_rows(0)
            ada_rows(1)
            for v in range(AHEAD):
                split_hi(v, v, 1)
            his(norms["l0a"])
            for i in range(L0_FM):
                ahead(U_L0 + i)
                evac(p_l0, i)
                if i == 3:
                    ada_rows(2)
                if i == 7:
                    ada_rows(3)
            for h in range(2):
                ahead(U_L0 + L0_FM + h)
            evac_v(U_L0 + L0_FM + 1, V_L0, [V0[:, t, :] for t in range(4)])
            ada_rows(4)
            attend(*J_L0)
            out_proj(U_L0_OUT, norms["l0b"])
            his(norms["l0b"])
            mlp(U_L0_MLP, 0, 512, norms["l1a"], FIRST)
            his(norms["l1a"])
            for i in range(L1_FM):
                ahead(U_L1 + i)
                evac(p_l1, i)
            for c in range(4):
                u = U_L1 + L1_FM + 2 * c
                ahead(u)
                ahead(u + 1)
                evac_v(u + 1, V_L1 + 4 * c, [V1[:, t, N * c:N * c + N] for t in range(4)])
            attend(*J_L1)
            out_proj(U_L1_OUT, norms["l1b"])
            his(norms["l1b"])
            mlp(U_L1_MLP, 32, 256, norms["fin"])
            his(norms["fin"])
            for l in range(2):
                u0 = U_B2 + l * B2_UNITS
                for i in range(B2_FM1):
                    ahead(u0 + i)
                    evac(p_a[l], i)
                act.wait_ge(sem("rope_out"), p_a[l].r0 + 1)
                if l == 0:
                    act.wait_ge(sem("b2_zeros"), 1)
                for r in range(2):
                    ins = act.activation(KI[rows(r), r, :], KK[0:64, :], ACT.Copy)
                ins.then_inc(sem("ki_shift"), 1)
                squares(norms[f"q{l}"])
                squares(norms[f"kv{l}"])
                for i in range(6):
                    ahead(u0 + 9 + i)
                    evac(p_b[l], i)
                his(norms[f"q{l}"])
                for i in range(6, 9):
                    ahead(u0 + 9 + i)
                    evac(p_b[l], i)
                his(norms[f"kv{l}"])
                for i in range(9, B2_FM2):
                    ahead(u0 + 9 + i)
                    evac(p_b[l], i)
                for c in range(3):
                    u = u0 + 23 + 2 * c
                    ahead(u)
                    ahead(u + 1)
                    evac_v(u + 1, V_B2[l] + 2 * c + (8 if c else 0), [V2[:, t, N * c:N * c + N] for t in range(2)])
                    if c == 0:
                        act.wait_ge(sem("nlo"), norms[f"kv{l}"].h0 + 2)
                        for h in range(8):
                            act.wait_ge(sem("ix_ps"), 8 * l + h + 1)
                            act.activation(RI(h), ps[:, (O_IX[l] + h) % 4, 0:384], ACT.Relu, scale=0.125)\
                               .then_inc(sem("proj_out"), 1)
                for i in range(KT):
                    u = u0 + 29 + i
                    ahead(u)
                    act.wait_ge(sem("w_used"), u + 1)
                    bank = ps[:, (p_g[l].o0 + i) % 4, 0:N]
                    act.activation(PQ[:, i, :], bank, ACT.Tanh, scale=0.5)
                    act.activation(GT[:, i, :], bank, ACT.Copy, scale=0.5).then_inc(sem("proj_out"), 1)
                act.wait_ge(sem("ix_used"), 4 * (l + 1))
                for i in range(6):
                    ahead(u0 + 37 + i)
                    evac(p_uq[l], i)
                ahead(u0 + 43)
                act.wait_ge(sem("w_used"), u0 + 44)
                for i in range(3):
                    bank = ps[:, (p_uk[l] + i) % 4, 0:N]
                    act.activation(KA[0:64, 2 * i, :], bank[0:64, :], ACT.Copy)
                    act.activation(KA[0:64, 2 * i + 1, :], bank[64:128, :], ACT.Copy).then_inc(sem("proj_out"), 1)
                ahead(u0 + 44)
                evac_v(u0 + 44, V_UV[l], [VA[:, t, :] for t in range(2)])
                act.wait_ge(sem("sb_done"), l + 1)
                attend(*J_B2[l])
                for i in range(KT):
                    ahead(u0 + 45 + i)
                squares(norms[f"ln{l}"])
                if l == 0:
                    his(norms["ln0"])
            n = norms["ln1"]
            for k in range(KT):
                act.wait_ge(sem("modded"), n.t0 + k + 1)
                act.activation(n.keep[0](k), n.keep[0](k), ACT.Identity, bias=n.keep[2](k)).then_inc(sem("finished"), 1)

        @block.vector
        def _(dve):
            linked = [0]

            def link(ins):
                linked[0] += 1
                ins.then_inc(sem("dve_link"), 1)
                dve.wait_ge(sem("dve_link"), linked[0])

            def split_lo(u, slot):
                dve.wait_ge(sem("w_hi"), u + 1)
                dve.tensor_tensor(wlo[:, slot, :], raw[:, slot, :], whi[:, slot, :].bitcast(F32), ALU.subtract)\
                   .then_inc(sem("w_lo"), 1)

            def ahead(u):
                if u + AHEAD < UNITS:
                    split_lo(u + AHEAD, (u + AHEAD) % SLOTS)

            def ada_cols(g):
                dve.wait_ge(sem("ada_tr"), g + 1)
                c = ada_width(g) // P
                src = ps[:, 7, 0:ada_width(g)].rearrange("p (c j r) -> p r j c", c=c, j=4)
                for v in range(3):
                    if isinstance(g, int):
                        t = 8 * min(g, NARROW) + 12 * max(g - NARROW, 0)
                        dst, bias = ada[:, v, t:t + 4 * c], par[:, P_AB + t:P_AB + t + 4 * c]
                    else:
                        t = 12 * g - 4 * NARROW
                        dst, bias = ada[:, v, bass.ds(t, 12)], par[:, bass.ds(t + P_AB, 12)]
                    ins = dve.tensor_tensor(dst.rearrange("p (j c) -> p j c", j=4), src[:, v, :, :],
                                            bias.rearrange("p (j c) -> p j c", j=4), ALU.add)
                ins.then_inc(sem("ada_ready"), 1)

            def scale_row(row, s, v, t0, gain):
                src = ada[:, v, 48 * s + t0:48 * s + t0 + 8]
                if gain is None:
                    link(dve.tensor_scalar(SC[:, row, :], src, 1.0, None, ALU.add))
                else:
                    link(dve.scalar_tensor_tensor(SC[:, row, :], src, 1.0, par[:, gain:gain + 8], ALU.add, ALU.mult))

            def variance(n):
                dve.wait_ge(sem("sq_used"), n.t0 + n.n)
                tt = n.T // P
                dve.tensor_scalar(VR[:, 0, 0:tt], ps[:, 7, 0:2 * tt:2], 1.0 / n.width, n.eps, ALU.mult, ALU.add)\
                   .then_inc(sem("var"), 1)

            def modulate(n):
                root = ps[:, 7, :]

                def lo(k):
                    dve.wait_ge(sem("nhi"), n.h0 + k + 1)
                    m = M[:, (n.t0 + k) % 2, :]
                    for c0, _, shift in n.streams:
                        c1 = min(c0 + N, n.T)
                        h, o = n.dst[0](k)[:, c0:c1].bitcast(F32), n.dst[1](k)[:, c0:c1]
                        if n.keep or shift is None:
                            ins = dve.tensor_tensor(o, m[:, c0:c1], h, ALU.subtract)
                        else:
                            ins = dve.scalar_tensor_tensor(o, m[:, c0:c1], shift(k), h, ALU.add, ALU.subtract)
                    ins.then_inc(sem("nlo"), 1)

                dve.wait_ge(sem("spread"), n.idx + 1)
                for k in range(n.n):
                    t = n.t0 + k
                    if n.dst and n.h0 + k > 1:
                        dve.wait_ge(sem("nlo"), n.h0 + max(k - 1, 0))
                    src = n.src(k, n.T)
                    if n.keep:
                        x, g, b = n.keep[0](k), n.keep[1](k), n.keep[2]
                        ins = dve.scalar_tensor_tensor(x, src, g, root[:, 0:n.T], ALU.mult, ALU.mult)
                        if b is not None and n.streams:
                            link(ins)
                            ins = dve.tensor_scalar(x, x, b(k), None, ALU.add)
                        if n.streams:
                            link(ins)
                            ins = dve.tensor_scalar(M[:, t % 2, 0:n.T], x, n.streams[0][1](k), n.streams[0][2](k),
                                                    ALU.mult, ALU.add)
                    else:
                        for c0, scale, _ in n.streams:
                            c1 = min(c0 + N, n.T)
                            ins = dve.scalar_tensor_tensor(M[:, t % 2, c0:c1], src[:, c0:c1], scale(k), root[:, c0:c1],
                                                           ALU.mult, ALU.mult)
                    ins.then_inc(sem("modded"), 1)
                    if n.dst and k:
                        lo(k - 1)
                if n.dst:
                    lo(n.n - 1)

            def rope(pr, i):
                t = pr.tiles[i]
                r = pr.rope_index(i)
                n, c, s = (128, C_COS, C_SIN) if t.rope == "q" else (96, C_COSM, C_SINM)
                dve.wait_ge(sem("rope_rot"), r + 1)
                if r >= 2:
                    dve.wait_ge(sem("rope_out"), r - 1)
                link(dve.tensor_tensor(wk1[0:n, 2 + r % 2, 0:N], wk1[0:n, r % 2, 0:N], cst[0:n, c:c + N], ALU.mult))
                link(dve.tensor_tensor(wk1[0:n, r % 2, 0:N], ps[0:n, 4 + r % 2, 0:N], cst[0:n, s:s + N], ALU.mult))
                for p, dst in t.dst:
                    ins = dve.tensor_tensor(dst, wk1[p, 2 + r % 2, 0:N], wk1[p, r % 2, 0:N], ALU.add)
                ins.then_inc(sem("rope_out"), 1)

            def steps(pr, lo, hi):
                for i in range(lo, hi):
                    ahead(pr.u0 + i)
                    if i and pr.tiles[i - 1].rope:
                        rope(pr, i - 1)
                if hi == len(pr.tiles) and pr.tiles[-1].rope:
                    rope(pr, hi - 1)

            def attend(j0, j1):
                for s in range(j0, j1 + (6 if jobs[j0].diff else 5)):
                    if j0 <= s - 6 < j1 and jobs[s - 6].diff:
                        g = s - 6
                        dve.wait_ge(sem("sub_hi"), g - j0 + 1)
                        dve.scalar_tensor_tensor(jobs[g].dst[1], ps[:, 5, 0:P], SC[:, 12, 0:1],
                                                 jobs[g].dst[0].bitcast(F32), ALU.mult, ALU.subtract)\
                           .then_inc(sem("sub_lo"), 1)
                    if j0 <= s - 5 < j1:
                        g = s - 5
                        j = jobs[g]
                        if not j.diff:
                            dve.wait_ge(sem("o_hi"), HL[g])
                            src = MO[:, g % 2, :] if j.gate is not None else ps[:, 6 + g % 2, 0:P]
                            dve.tensor_tensor(j.dst[1], src, j.dst[0].bitcast(F32), ALU.subtract)\
                               .then_inc(sem("o_lo"), 1)
                    if j0 <= s - 4 < j1 and jobs[s - 4].gate is not None:
                        g = s - 4
                        dve.wait_ge(sem("pv_done"), g + 1)
                        if g - 2 >= j0:
                            dve.wait_ge(sem("o_lo"), HL[g - 2])
                        dve.tensor_tensor(MO[:, g % 2, :], ps[:, 6 + g % 2, 0:P], jobs[g].gate, ALU.mult)\
                           .then_inc(sem("o_m"), 1)
                    if s < j1:
                        j = jobs[s]
                        st = small[:, s % 4, :]
                        dve.wait_ge(sem("s_done"), s + 1)
                        b0 = 2 * (s % 2)
                        if j.bias is not None:
                            nb = j.bias.shape[2]
                            w = ps[:, b0:b0 + 2, 0:nb]
                            if j.pre == 1.0:
                                link(dve.tensor_tensor(w, w, j.bias, ALU.add))
                            else:
                                link(dve.scalar_tensor_tensor(w, w, j.pre, j.bias, ALU.mult, ALU.add))
                        link(dve.tensor_reduce(st[:, 0:2], ps[:, b0:b0 + 2, 0:j.nk], AX.X, ALU.max))
                        if j.sink is None:
                            dve.tensor_scalar(st[:, 2:4], st[:, 0:2], -j.post, None, ALU.mult)\
                               .then_inc(sem("m_done"), 1)
                        else:
                            link(dve.scalar_tensor_tensor(st[:, 2:4], st[:, 0:2], -j.post,
                                                          nsink[:, j.sink:j.sink + 2], ALU.mult, ALU.min))
                            dve.tensor_tensor(st[:, 8:10], st[:, 2:4], nsink[:, j.sink:j.sink + 2], ALU.subtract)\
                               .then_inc(sem("m_done"), 1)
                    if j0 <= s - 1 < j1:
                        g = s - 1
                        j = jobs[g]
                        st = small[:, g % 4, :]
                        dve.wait_ge(sem("x_done"), g + 1)
                        if j.sink is not None:
                            link(dve.tensor_tensor(st[:, 4:6], st[:, 4:6], st[:, 8:10], ALU.add))
                        ins = dve.reciprocal(st[:, 6:8], st[:, 4:6])
                        if not j.diff:
                            ins.then_inc(sem("rc_done"), 1)
                        else:
                            link(ins)
                            link(dve.scalar_tensor_tensor(st[:, 10:11], st[:, 4:5], st[:, 7:8], lam[:, 4:5],
                                                          ALU.mult, ALU.mult))
                            e0, e1 = E[:, g % 2, 0, 0:j.nk], E[:, g % 2, 1, 0:j.nk]
                            dve.scalar_tensor_tensor(e0, e1, st[:, 10:11], e0, ALU.mult, ALU.add)\
                               .then_inc(sem("normed"), 1)
                    if j0 <= s - 2 < j1 and not jobs[s - 2].diff:
                        g = s - 2
                        dve.wait_ge(sem("t_done"), g + 1)
                        if g >= 2:
                            dve.wait_ge(sem("pv_done"), g - 1)
                        dve.tensor_copy(PT[:, g % 2, 1, 0:jobs[g].nk], ps[:, 5, 0:jobs[g].nk]).then_inc(sem("ev_v"), 1)

            def index_heads(l, p):
                if p == 0:
                    dve.wait_ge(sem("proj_out"), O_IX[l])
                    link(dve.tensor_scalar(WI[:, :, :], V2[:, :, P:P + 8], 8 ** -0.5, None, ALU.mult))
                for h in (2 * p, 2 * p + 1):
                    dve.wait_ge(sem("proj_out"), O_IX[l] + h + 1)
                    for t in range(2):
                        sl = slice(KOFF[t], KOFF[t] + KLEN[t])
                        base = IX[:, sl] if h else cst[:, C_CAU + KOFF[t]:C_CAU + KOFF[t] + KLEN[t]]
                        ins = dve.scalar_tensor_tensor(IX[:, sl], RI(h)[:, sl], WI[:, t, h:h + 1], base,
                                                       ALU.mult, ALU.add)
                    if h % 2 == 0:
                        link(ins)
                ins.then_inc(sem("ix_used"), 1)
                dve.wait_ge(sem("ix_used"), 4 * l + p + 1)

            def topk_round(l, p):
                ws = [IX[:, KOFF[t]:KOFF[t] + KLEN[t]] for t in range(2)]
                for t in range(2):
                    ins = dve.max(M8[:, 8 * t:8 * t + 8], ws[t])
                link(ins)
                for t in range(2):
                    ins = dve.match_replace(ws[t], M8[:, 8 * t:8 * t + 8], ws[t], TAKEN)
                link(ins)
                if p == TOPK // 8 - 1:
                    dve.tensor_scalar(SEL, IX[:, :], -2.0e38, NEG, ALU.is_gt, ALU.mult).then_inc(sem("sel_done"), 1)

            def add_out(u0, o0, add):
                for i in range(KT):
                    ahead(u0 + i)
                    dve.wait_ge(sem("w_used"), u0 + i + 1)
                    add(i, ps[:, i % 4, :]).then_inc(sem("out_added"), 1)

            def gated(s, t0, T):
                def add(i, bank):
                    for v in range(T // N):
                        x = X[:, i, N * v:N * v + N]
                        ins = dve.scalar_tensor_tensor(x, bank[:, N * v:N * v + N], adacol(s, v, t0 + i), x,
                                                       ALU.mult, ALU.add)
                    return ins
                return add

            def mlp(u0, h0, T, s, g0=None):
                with dve.Fori(0, QUARTERS) as it:
                    def lo(j):
                        dve.wait_ge(sem("hid_h"), 8 * it + (h0 + j + 1))
                        dve.tensor_tensor(HIDl[:, j, 0:T], M[:, j % 2, 0:T], HIDh[:, j, 0:T].bitcast(F32),
                                          ALU.subtract).then_inc(sem("hid"), 1)
                    for j in range(16):
                        v = u0 + j + AHEAD
                        split_lo(16 * it + v, v % SLOTS)
                        if j < 8:
                            dve.wait_ge(sem("hid_r"), 8 * it + (h0 + j + 1))
                            dve.wait_ge(sem("hid"), 8 * it + (h0 + j + 1))
                            dve.tensor_tensor(M[:, j % 2, 0:T], Y[:, j % 2, 0:T], Y[:, j % 2, 0:T], ALU.mult)\
                               .then_inc(sem("hid_a"), 1)
                            dve.wait_ge(sem("hid_a"), 8 * it + (h0 + j + 1))
                            lo(j)
                        else:
                            i = j - 8
                            dve.wait_ge(sem("w_used"), 16 * it + (u0 + j + 1))
                            gated(s, 40, T)(i, ps[:, 2 + i % 2, :]).then_inc(sem("mlp_added"), 1)
                        if j == 10 and g0:
                            ada_cols(2 * it + g0)
                    if g0:
                        ada_cols(2 * it + (g0 + 1))

            dve.memset(scs[:, :, :], 0.0).then_inc(sem("dve_link"), 1)
            linked[0] += 1
            dve.memset(mhalf[:, :], -0.5).then_inc(sem("mhalf_set"), 1)
            dve.memset(lam[:, 5:6], 0.0).then_inc(sem("hid"), 1)
            dve.memset(lam[:, 6:7], 0.0).then_inc(sem("hid"), 1)
            dve.memset(lam[:, 7:8], 0.0).then_inc(sem("mlp_added"), 1)
            dve.wait_ge(sem("silu_e"), 1)
            link(dve.tensor_scalar(stp[:, 1, :, :], stp[:, 0, :, :], 1.0, None, ALU.add))
            link(dve.reciprocal(stp[:, 0, :, :], stp[:, 1, :, :]))
            dve.tensor_tensor(scs[:, :, 0:3], par[:, P_CV:P_CV + 24].rearrange("p (k v) -> p k v", v=3),
                              stp[:, 0, :, :], ALU.mult).then_inc(sem("scs_ready"), 1)
            link(dve.tensor_scalar(nsink[:, :], par[:, P_SINK:P_SINK + 8], -1.0, None, ALU.mult))
            dve.tensor_tensor(lam[:, 0:2], par[:, P_LAM:P_LAM + 2], par[:, P_LAM + 2:P_LAM + 4], ALU.mult)\
               .then_inc(sem("lam_prod"), 1)
            link(dve.tensor_scalar(SC[:, 12, 0:1], par[:, P_SUB:P_SUB + 1], 1.0 - LAM_INIT, None, ALU.mult))
            dve.wait_ge(sem("lam_e"), 1)
            link(dve.tensor_tensor(lam[:, 4:5], lam[:, 3:4], lam[:, 2:3], ALU.subtract))
            link(dve.tensor_scalar(lam[:, 4:5], lam[:, 4:5], -LAM_INIT, None, ALU.add))
            variance(norms["l0a"])
            ada_cols(0)
            ada_cols(1)
            dve.wait_ge(sem("ada_ready"), 2)
            scale_row(0, 0, 0, 8, P_N1)
            scale_row(1, 0, 1, 8, P_N1)
            for u in range(AHEAD):
                split_lo(u, u)
            modulate(norms["l0a"])
            dve.wait_ge(sem("tables_landed"), 16)
            steps(p_l0, 0, 6)
            ada_cols(2)
            steps(p_l0, 6, L0_FM)
            ada_cols(3)
            for h in range(2):
                ahead(U_L0 + L0_FM + h)
            ada_cols(4)
            dve.wait_ge(sem("rpb_done"), 1)
            attend(*J_L0)
            dve.wait_ge(sem("ada_ready"), FIRST)
            add_out(U_L0_OUT, 0, gated(0, 16, 512))
            scale_row(2, 0, 0, 32, P_N2)
            scale_row(3, 0, 1, 32, P_N2)
            variance(norms["l0b"])
            modulate(norms["l0b"])
            mlp(U_L0_MLP, 0, 512, 0, FIRST)
            dve.wait_ge(sem("ada_ready"), ADA_GROUPS)
            scale_row(4, 1, 0, 8, P_N1 + 8)
            scale_row(5, 1, 1, 8, P_N1 + 8)
            scale_row(6, 1, 0, 32, P_N2 + 8)
            variance(norms["l1a"])
            modulate(norms["l1a"])
            steps(p_l1, 0, L1_FM)
            for v in range(8):
                ahead(U_L1 + L1_FM + v)
            attend(*J_L1)
            add_out(U_L1_OUT, 8, gated(1, 16, 256))
            variance(norms["l1b"])
            modulate(norms["l1b"])
            mlp(U_L1_MLP, 32, 256, 1)
            scale_row(8, 2, 2, 8, None)
            scale_row(9, 2, 2, 32, None)
            scale_row(10, 2, 2, 16, None)
            scale_row(11, 2, 2, 40, None)
            variance(norms["fin"])
            modulate(norms["fin"])
            for l in range(2):
                u0 = U_B2 + l * B2_UNITS
                steps(p_a[l], 0, B2_FM1)
                steps(p_b[l], 0, 4)
                variance(norms[f"q{l}"])
                steps(p_b[l], 4, 6)
                modulate(norms[f"q{l}"])
                steps(p_b[l], 6, 7)
                variance(norms[f"kv{l}"])
                steps(p_b[l], 7, 9)
                modulate(norms[f"kv{l}"])
                steps(p_b[l], 9, B2_FM2)
                for v in range(6):
                    ahead(u0 + 23 + v)
                    if v >= 2:
                        index_heads(l, v - 2)
                for i in range(KT):
                    ahead(u0 + 29 + i)
                    dve.wait_ge(sem("proj_out"), p_g[l].o0 + i + 1)
                    dve.scalar_tensor_tensor(GT[:, i, :], PQ[:, i, :], 1.0, GT[:, i, :], ALU.add, ALU.mult)
                    topk_round(l, i)
                steps(p_uq[l], 0, 6)
                ahead(u0 + 43)
                ahead(u0 + 44)
                if l == 0:
                    dve.wait_ge(sem("ali_landed"), 160)
                dve.wait_ge(sem("sb_done"), l + 1)
                attend(*J_B2[l])

                def add(i, bank, l=l):
                    x = X[:, i, 0:N]
                    link(dve.tensor_scalar(x, x, ALPHA, None, ALU.mult))
                    return dve.scalar_tensor_tensor(x, bank[:, 0:N], SC[:, 10 + l, i:i + 1], x, ALU.mult, ALU.add)
                add_out(u0 + 45, 16 + 8 * l, add)
                dve.wait_ge(sem("mean_sum"), l + 1)
                link(dve.tensor_scalar(RS[:, 0:N], ps[:, 7, 0:N], 1.0 / D, None, ALU.mult))
                for k in range(KT):
                    dve.tensor_tensor(X[:, k, 0:N], X[:, k, 0:N], RS[:, 0:N], ALU.subtract)\
                       .then_inc(sem("centred"), 1)
                variance(norms[f"ln{l}"])
                modulate(norms[f"ln{l}"])

        @block.gpsimd
        def _(pool):
            def root(dst, src, T):
                return pool.tensor_tensor(dst, src, mhalf[:, 0:1].to_broadcast([P, T]), ALU.pow)

            def roots(n):
                if not n.direct:
                    acc = RS[:, 0:n.T]
                    pool.wait_ge(sem("sq_used"), n.t0)
                    for k in range(1, n.n - 1):
                        t = n.t0 + k
                        pool.wait_ge(sem("sq"), t + 1)
                        prev = acc if k > 1 else SQ[:, n.t0 % 4, 0:n.T]
                        pool.tensor_tensor(acc, prev, SQ[:, t % 4, 0:n.T], ALU.add)\
                            .then_inc(sem("sq_used"), 2 if k == 1 else 1)
                        pool.wait_ge(sem("sq_used"), t + 1)
                pool.wait_ge(sem("var"), n.idx + 1)
                root(VR[:, 1, 0:n.T // P], VR[:, 0, 0:n.T // P], n.T // P).then_inc(sem("rstd"), 1)

            def attend(j0, j1):
                for g in range(j0, j1):
                    pool.wait_ge(sem("rc_done"), HL[g])
                    if g - 2 >= j0:
                        pool.wait_ge(sem("t_done"), g - 1)
                    pool.tensor_tensor(DG[:, g % 2, :, :], two(ident, P),
                                       small[:, g % 4, 6:8, None].to_broadcast([P, 2, P]), ALU.mult)\
                        .then_inc(sem("normed"), 1)

            def sub_roots(j0, j1):
                for g in range(j0, j1):
                    st = small[:, g % 4, :]
                    pool.wait_ge(sem("sub_sq"), g - j0 + 1)
                    pool.tensor_scalar(st[:, 12:13], st[:, 11:12], 1.0 / P, 1e-6, ALU.mult, ALU.add)\
                        .then_inc(sem("sub_var"), 1)
                    pool.wait_ge(sem("sub_var"), g - j0 + 1)
                    root(st[:, 13:14], st[:, 12:13], 1).then_inc(sem("sub_rs"), 1)
                    pool.wait_ge(sem("sub_rs"), g - j0 + 1)
                    pool.tensor_scalar(DS[:, g % 2, :], ident, st[:, 13:14], None, ALU.mult)\
                        .then_inc(sem("sub_diag"), 1)

            def zeros(pairs, name):
                for ap in pairs:
                    for r in range(2):
                        ins = pool.memset(ap(r)[rows(1 - r)], 0.0)
                ins.then_inc(sem(name), 1)

            zeros([lambda r: K0[:, :, r, :]], "l0_zeros")
            pool.wait_ge(sem("l0_zeros"), 1)
            pool.wait_ge(sem("mhalf_set"), 1)
            roots(norms["l0a"])
            pool.wait_ge(sem("rpb_landed"), 16 * 4)
            pool.wait_ge(sem("tables_landed"), 16)
            for t in range(2):
                pool.tensor_scalar(BI[:, t, :, :], BI[:, t, :, :], 8.0, None, ALU.mult).then_inc(sem("rpb_x8"), 1)
            pool.wait_ge(sem("rpb_x8"), 2)
            for t in range(2):
                ins = pool.tensor_tensor(BI[:, t, :, :], BI[:, t, :, :],
                                         cst[:, None, C_NBR + N * t:C_NBR + N * t + N].to_broadcast([P, 8, N]), ALU.add)
            ins.then_inc(sem("rpb_done"), 1)
            attend(*J_L0)
            roots(norms["l0b"])
            roots(norms["l1a"])
            pool.wait_ge(sem("nlo"), norms["l1a"].h0 + 8)
            zeros([lambda r: Q1[:, :, r, :]], "l1_zeros")
            pool.wait_ge(sem("l1_zeros"), 1)
            sub_roots(*J_L1)
            roots(norms["l1b"])
            roots(norms["fin"])
            pool.wait_ge(sem("nlo"), norms["fin"].h0 + 8)
            zeros([lambda r: QZ[:, :, r, :], lambda r: KI[:, r, :]], "b2_zeros")
            pool.wait_ge(sem("b2_zeros"), 1)
            for l in range(2):
                roots(norms[f"q{l}"])
                roots(norms[f"kv{l}"])
                pool.wait_ge(sem("rstd"), norms[f"kv{l}"].idx + 1)
                pool.wait_ge(sem("rope_out"), p_a[l].r0 + 1)
                pool.tensor_copy(KA[64:96, :, :], KK[64:96, None, :].to_broadcast([32, 6, N])).then_inc(sem("kr_done"), 1)
                pool.wait_ge(sem("kr_done"), l + 1)
                pool.wait_ge(sem("sel_done"), l + 1)
                pool.wait_ge(sem("ali_landed"), 16 * (10 + 4 * l))
                pool.tensor_tensor(AL[:, 6:10, :], AL[:, 6:10, :], SEL[:, None, :].to_broadcast([P, 4, 384]), ALU.add)\
                    .then_inc(sem("sb_done"), 1)
                attend(*J_B2[l])
                for k in range(1, KT):
                    pool.wait_ge(sem("out_added"), 16 + 8 * l + k + 1)
                    prev = RS[:, 0:N] if k > 1 else X[:, 0, 0:N]
                    pool.tensor_tensor(RS[:, 0:N], prev, X[:, k, 0:N], ALU.add).then_inc(sem("tile_summed"), 1)
                    pool.wait_ge(sem("tile_summed"), 7 * l + k)
                roots(norms[f"ln{l}"])

        @block.tensor
        def _(pe):
            def mm3(o, a, b, first, last):
                pe.matmul(o, a[0], b[0], start=first, stop=False)
                pe.matmul(o, a[0], b[1], start=False, stop=False)
                return pe.matmul(o, a[1], b[0], start=False, stop=last)

            def wtile(slot, c0, n):
                return whi[:, slot, c0:c0 + n], wlo[:, slot, c0:c0 + n]

            def ada_mm(a, kt, slot, lap, g):
                pe.wait_ge(sem(f"a_landed{slot}"), 16 * lap)
                if kt == 0 and (not isinstance(g, int) or g):
                    pe.wait_ge(sem("ar_ready"), g)
                n = ada_width(g)
                for j in range(4):
                    ins = pe.matmul(ps[32 * j:32 * j + 32, 6, 0:n], scs[:, kt, :],
                                    aring[:, slot, n * j:n * j + n], start=(kt == 0), stop=(kt == KT - 1))
                ins.then_inc(sem("a_used"), 1)

            def ada_turn(g):
                pe.wait_ge(sem("ar_ready"), g + 1)
                if not isinstance(g, int) or g:
                    pe.wait_ge(sem("ada_ready"), g)
                for c in range(ada_width(g) // P):
                    ins = pe.transpose(ps[:, 7, P * c:P * c + P], AR[:, P * c:P * c + P], ident)
                ins.then_inc(sem("ada_tr"), 1)

            def sums(n):
                if n.idx:
                    pe.wait_ge(sem("modded"), n.t0)
                def part(sq, first, last):
                    for t in range(n.T // P):
                        ins = pe.matmul(ps[:, 7, 2 * t:2 * t + 2], sq[:, P * t:P * t + P], ones[:, 0:2],
                                        start=first and t == 0, stop=last and t == n.T // P - 1)
                    return ins

                if n.direct:
                    for k in range(n.n):
                        pe.wait_ge(sem("sq"), n.t0 + k + 1)
                        part(SQ[:, (n.t0 + k) % 4, :], k == 0, k == n.n - 1).then_inc(sem("sq_used"), 1)
                else:
                    pe.wait_ge(sem("sq_used"), n.t0 + n.n - 1)
                    part(RS, True, False)
                    pe.wait_ge(sem("sq"), n.t0 + n.n)
                    part(SQ[:, (n.t0 + n.n - 1) % 4, :], False, True).then_inc(sem("sq_used"), 1)

            def spread(n):
                pe.wait_ge(sem("rstd"), n.idx + 1)
                for t in range(n.T // P):
                    ins = pe.matmul(ps[:, 7, P * t:P * t + P], VR[:, 1, t:t + 1].to_broadcast([P, P]), ident,
                                    start=True, stop=True)
                ins.then_inc(sem("spread"), 1)

            def rot(pr, i):
                t = pr.tiles[i]
                if t.rope is None:
                    return
                r = pr.rope_index(i)
                n, c = (128, C_RQ) if t.rope == "q" else (96, C_RM)
                pe.wait_ge(sem("proj_out"), pr.o0 + i + 1)
                if r >= 2:
                    pe.wait_ge(sem("rope_out"), r - 1)
                pe.matmul(ps[0:n, 4 + r % 2, 0:N], cst[0:n, c:c + n], wk1[0:n, r % 2, 0:N], start=True, stop=True)\
                  .then_inc(sem("rope_rot"), 1)

            def rots(pr, i, late):
                due = [i - 1] if i else []
                if late and i < 5:
                    due = {3: [0, 1], 4: [2, 3]}.get(i, [])
                for n in due:
                    rot(pr, n)

            def project(pr, lo, hi, x, kts=KT, ready=None, after=None):
                groups = [range(i, i + 1) for i in range(lo, hi)]
                if ready is not None:
                    groups = [range(0, TOGETHER)] + groups[TOGETHER:]
                for group in groups:
                    for i in group:
                        pe.wait_ge(sem("w_lo"), pr.u0 + i + 1)
                        if pr.o0 + i >= 4:
                            pe.wait_ge(sem("proj_out"), pr.o0 + i - 3)
                    for k in range(kts):
                        if group[0] == 0 and ready is not None:
                            pe.wait_ge(sem("nlo"), ready + k + 1)
                        for i in group:
                            T = pr.tiles[i].T
                            ins = mm3(ps[:, (pr.o0 + i) % 4, 0:T], wtile((pr.u0 + i) % SLOTS, P * k, P),
                                      (x[0](k)[:, 0:T], x[1](k)[:, 0:T]), k == 0, k == kts - 1)
                            if k == kts - 1:
                                ins.then_inc(sem("w_used"), 1)
                    for i in group:
                        rots(pr, i, ready is not None)
                        if after:
                            after(i)
                if hi == len(pr.tiles):
                    rot(pr, hi - 1)

            def values(u, o0, toks, x, after=None):
                for half in range(2):
                    pe.wait_ge(sem("w_lo"), u + half + 1)
                    for t in range(toks):
                        o = o0 + t
                        if half == 0:
                            pe.wait_ge(sem("proj_out"), o - 3)
                        for k in range(4):
                            kk = 4 * half + k
                            ins = mm3(ps[:, o % 4, 0:N],
                                      (x[0](kk)[:, P * t:P * t + P], x[1](kk)[:, P * t:P * t + P]),
                                      wtile((u + half) % SLOTS, N * k, N), kk == 0, kk == KT - 1)
                    ins.then_inc(sem("w_used"), 1)
                    if after:
                        after(half)

            def attend(j0, j1):
                for s in range(j0, j1 + (5 if jobs[j0].diff else 3)):
                    if s < j1:
                        j = jobs[s]
                        if s - j0 >= 2:
                            pe.wait_ge(sem("x_done"), s - 1)
                        for r in range(2):
                            ins = pe.matmul(ps[:, 2 * (s % 2) + r, 0:j.nk], j.q[r], j.k[r], start=True, stop=True)
                        ins.then_inc(sem("s_done"), 1)
                    if j0 <= s - 2 < j1:
                        g = s - 2
                        j = jobs[g]
                        pe.wait_ge(sem("normed"), g + 1)
                        if g > j0:
                            pe.wait_ge(sem("ev_a"), g)
                            if not j.diff:
                                pe.wait_ge(sem("ev_v"), HL[g - 1])
                        for r in range(1 if j.diff else 2):
                            for kt in range(j.nk // P):
                                o, e = ps[:, 4 + r, P * kt:P * kt + P], E[:, g % 2, r, P * kt:P * kt + P]
                                if j.diff:
                                    ins = pe.transpose(o, e, ident)
                                else:
                                    ins = pe.matmul(o, e, DG[:, g % 2, r, :], start=True, stop=True)
                        ins.then_inc(sem("t_done"), 1)
                    if j0 <= s - 3 < j1:
                        g = s - 3
                        j = jobs[g]
                        pe.wait_ge(sem("ev_a"), g + 1)
                        if not j.diff:
                            pe.wait_ge(sem("ev_v"), HL[g])
                        if g - 2 >= j0:
                            if j.diff:
                                pe.wait_ge(sem("sub_sq"), g - 2 - J_L1[0] + 1)
                            elif j.gate is None:
                                pe.wait_ge(sem("o_lo"), HL[g - 2])
                            else:
                                pe.wait_ge(sem("o_m"), GJOB[g - 2] + 1)
                        nkt = j.nk // P
                        if j.diff:
                            for kt in range(nkt):
                                ins = pe.matmul(ps[:, 6 + g % 2, 0:P], PT[:, g % 2, 0, P * kt:P * kt + P], j.v(kt, 0),
                                                start=(kt == 0), stop=(kt == nkt - 1))
                        else:
                            for r in range(2):
                                for kt in range(nkt):
                                    ins = pe.matmul(ps[64 * r:64 * r + 64, 6 + g % 2, 0:P], j.v(kt, r),
                                                    PT[:, g % 2, r, P * kt:P * kt + P],
                                                    start=(kt == 0), stop=(kt == nkt - 1))
                        ins.then_inc(sem("pv_done"), 1)
                    if j0 <= s - 5 < j1 and jobs[s - 5].diff:
                        g = s - 5
                        pe.wait_ge(sem("sub_diag"), g - j0 + 1)
                        if g > j0:
                            pe.wait_ge(sem("sub_lo"), g - j0)
                        pe.matmul(ps[:, 5, 0:P], OS[:, g % 2, :], DS[:, g % 2, :], start=True, stop=True)\
                          .then_inc(sem("sub_tr"), 1)

            def project_out(u0, o0, T, x):
                for i in range(KT):
                    u = u0 + i
                    pe.wait_ge(sem("w_lo"), u + 1)
                    if i >= 4:
                        pe.wait_ge(sem("out_added"), o0 + i - 3)
                    for k in range(KT):
                        ins = mm3(ps[:, i % 4, 0:T], wtile(u % SLOTS, P * k, P), (x[0](k)[:, 0:T], x[1](k)[:, 0:T]),
                                  k == 0, k == KT - 1)
                    ins.then_inc(sem("w_used"), 1)

            def mlp(u0, h0, T, ready, g0=None):
                with pe.Fori(0, QUARTERS) as it:
                    for group in [range(0, TOGETHER)] + [range(j, j + 1) for j in range(TOGETHER, 16)]:
                        for j in group:
                            pe.wait_ge(sem("w_lo"), 16 * it + (u0 + j + 1))
                            i = j - 8
                            if j in range(4, 8):
                                pe.wait_ge(sem("hid"), 8 * it + (2 + h0 + j - 3))
                            elif i >= 2:
                                pe.wait_ge(sem("mlp_added"), 8 * it + (1 + h0 + i - 1))
                            elif i >= 0:
                                pe.wait_ge(sem("mlp_added"), 8 * it + (1 + h0))
                        for k in range(KT):
                            if group[0] == 0:
                                pe.wait_ge(sem("nlo"), ready + k + 1)
                            if group[0] == 8:
                                pe.wait_ge(sem("hid"), 8 * it + (2 + h0 + k + 1))
                            for j in group:
                                b = ((Hh, Hl) if j < 8 else (HIDh, HIDl))
                                bank = HID_BANKS[j % 4] if j < 8 else 2 + j % 2
                                ins = mm3(ps[:, bank, 0:T], wtile((u0 + j) % SLOTS, P * k, P),
                                          (b[0][:, k, 0:T], b[1][:, k, 0:T]), k == 0, k == KT - 1)
                                if k == KT - 1:
                                    ins.then_inc(sem("w_used"), 1)
                        for j in group:
                            if g0:
                                a = g0 * KT + j
                                ada_mm(None, j % KT, a % ADA_SLOTS, 4 * it + (a // ADA_SLOTS + 1),
                                       2 * it + (g0 + j // KT))
                                if j == 9:
                                    ada_turn(2 * it + g0)
                    if g0:
                        ada_turn(2 * it + (g0 + 1))

            Hx = (lambda k: Hh[:, k, :], lambda k: Hl[:, k, :])
            Gx = (lambda k: Gh[:, k, :], lambda k: Gl[:, k, :])
            Cx = (lambda k: CQh[:, k, :], lambda k: CQl[:, k, :])

            def ada_static(a):
                ada_mm(a, a % KT, a % ADA_SLOTS, a // ADA_SLOTS + 1, a // KT)

            pe.wait_ge(sem("cst_landed"), 16)
            pe.wait_ge(sem("lam_prod"), 1)
            pe.matmul(ps[:, 5, 0:2], ones, lam[:, 0:2], start=True, stop=True).then_inc(sem("lam_sum"), 1)
            pe.wait_ge(sem("scs_ready"), 1)
            for a in range(2 * KT):
                ada_static(a)
                if a == KT - 1:
                    sums(norms["l0a"])
                    pe.wait_ge(sem("var"), 1)
                if a % KT == KT - 1:
                    ada_turn(a // KT)
            pe.wait_ge(sem("ada_ready"), 2)
            spread(norms["l0a"])

            def ada_between(i):
                if i in (5, 9):
                    ada_turn(i // 4 + 1)
                for a in range(2 * KT + 2 * i, 2 * KT + 2 * i + 2):
                    ada_static(a)

            project(p_l0, 0, L0_FM, Hx, ready=norms["l0a"].h0, after=ada_between)
            values(U_L0 + L0_FM, V_L0, 4, Hx, after=lambda h: ada_between(L0_FM + h))
            ada_turn(4)
            pe.wait_ge(sem("proj_out"), V_L0 + 4)
            pe.wait_ge(sem("rope_out"), 5)
            pe.wait_ge(sem("ada_ready"), FIRST)
            pe.wait_ge(sem("l0_zeros"), 1)
            attend(*J_L0)
            pe.wait_ge(sem("o_lo"), HL[J_L0[1] - 1])
            project_out(U_L0_OUT, 0, 512, Hx)
            sums(norms["l0b"])
            spread(norms["l0b"])
            mlp(U_L0_MLP, 0, 512, norms["l0b"].h0, FIRST)
            pe.wait_ge(sem("ada_ready"), ADA_GROUPS)
            sums(norms["l1a"])
            spread(norms["l1a"])
            project(p_l1, 0, L1_FM, Hx, ready=norms["l1a"].h0)
            for c in range(4):
                values(U_L1 + L1_FM + 2 * c, V_L1 + 4 * c, 4, Hx)
            pe.wait_ge(sem("proj_out"), V_L1 + 16)
            pe.wait_ge(sem("rope_out"), p_l1.r0 + 16)
            pe.wait_ge(sem("l1_zeros"), 1)
            attend(*J_L1)
            pe.wait_ge(sem("sub_lo"), 16)
            project_out(U_L1_OUT, 8, 256, Hx)
            sums(norms["l1b"])
            spread(norms["l1b"])
            mlp(U_L1_MLP, 32, 256, norms["l1b"].h0)
            sums(norms["fin"])
            spread(norms["fin"])
            for l in range(2):
                u0 = U_B2 + l * B2_UNITS
                project(p_a[l], 0, B2_FM1, Gx, ready=norms["fin" if l == 0 else "ln0"].h0)
                project(p_b[l], 0, 4, Gx)
                sums(norms[f"q{l}"])
                project(p_b[l], 4, 6, Gx)
                spread(norms[f"q{l}"])
                project(p_b[l], 6, 7, Gx)
                sums(norms[f"kv{l}"])
                project(p_b[l], 7, 9, Gx)
                spread(norms[f"kv{l}"])
                project(p_b[l], 9, B2_FM2, Gx)
                values(u0 + 23, V_B2[l], 2, Gx)
                pe.wait_ge(sem("ki_shift"), l + 1)
                for h in range(8):
                    o = O_IX[l] + h
                    pe.wait_ge(sem("proj_out"), o - 3)
                    q, ki = KQ[:, 5 + h // 2, :], KI[:, h % 2, :]
                    pe.matmul(ps[:, o % 4, 0:P], q[:, 0:P], ki[:, 0:P], start=True, stop=True)
                    pe.matmul(ps[:, o % 4, P:3 * P], q[:, P:2 * P], ki, start=True, stop=True).then_inc(sem("ix_ps"), 1)
                for c in range(1, 3):
                    values(u0 + 23 + 2 * c, V_B2[l] + 8 + 2 * c, 2, Gx)
                project(p_g[l], 0, KT, Gx)
                pe.wait_ge(sem("nlo"), norms[f"q{l}"].h0 + 6)
                project(p_uq[l], 0, 6, Cx, kts=6)
                pe.wait_ge(sem("nlo"), norms[f"kv{l}"].h0 + 2)
                u = u0 + 43
                pe.wait_ge(sem("w_lo"), u + 1)
                for m in range(3):
                    o = p_uk[l] + m
                    pe.wait_ge(sem("proj_out"), o - 3)
                    for k in range(2):
                        ins = mm3(ps[:, o % 4, 0:N], wtile(u % SLOTS, P * (2 * m + k), P),
                                  (Cx[0](6 + k), Cx[1](6 + k)), k == 0, k == 1)
                ins.then_inc(sem("w_used"), 1)
                u = u0 + 44
                pe.wait_ge(sem("w_lo"), u + 1)
                for t in range(2):
                    o = V_UV[l] + t
                    pe.wait_ge(sem("proj_out"), o - 3)
                    for k in range(2):
                        ins = mm3(ps[:, o % 4, 0:384], (Cx[0](6 + k)[:, P * t:P * t + P], Cx[1](6 + k)[:, P * t:P * t + P]),
                                  wtile(u % SLOTS, 384 * k, 384), k == 0, k == 1)
                ins.then_inc(sem("w_used"), 1)
                pe.wait_ge(sem("proj_out"), V_UV[l] + 2)
                pe.wait_ge(sem("rope_out"), p_uq[l].r0 + 6)
                pe.wait_ge(sem("kr_done"), l + 1)
                attend(*J_B2[l])
                pe.wait_ge(sem("o_lo"), HL[J_B2[l][1] - 1])
                project_out(u0 + 45, 16 + 8 * l, 256, Gx)
                pe.wait_ge(sem("tile_summed"), 7 * (l + 1))
                pe.matmul(ps[:, 7, 0:N], ones, RS[:, 0:N], start=True, stop=True).then_inc(sem("mean_sum"), 1)
                sums(norms[f"ln{l}"])
                spread(norms[f"ln{l}"])


def feature_units(w):
    k, n = w.shape
    u = w.reshape(k // P, P, n // P, P).transpose(2, 1, 0, 3).reshape(n // P, P, k)
    return np.concatenate([u, np.zeros((n // P, P, 1024 - k), w.dtype)], axis=2) if k < 1024 else u


def value_units(w):
    c = w.shape[1] // N
    return w.reshape(2, 4, P, c, N).transpose(3, 0, 2, 1, 4).reshape(2 * c, P, 1024)


def mlp_units(w1, w2):
    parts = []
    for q in range(QUARTERS):
        parts += [feature_units(w1[:, 1024 * q:1024 * q + 1024]), feature_units(w2[1024 * q:1024 * q + 1024, :])]
    return np.concatenate(parts)


def one_unit(parts):
    row = np.concatenate(parts, axis=1)
    return np.concatenate([row, np.zeros((P, 1024 - row.shape[1]), row.dtype)], axis=1)[None]


def cols(v):
    return v.reshape(-1, P).T


PAIRS = [0, 4, 1, 5, 2, 6, 3, 7]


def weight_stream(a):
    we, wo = a["even_w_in"][0], a["odd_w_in"][0]
    aq, ak, av, bq, bk, bv = (we[:, x:y] for x, y in ((0, 512), (512, 640), (640, 768), (768, 1280), (1280, 1408),
                                                      (1408, 1536)))

    def pair(w):
        return w.reshape(1024, 8, 64)[:, PAIRS].reshape(1024, 512)

    w_out = a["even_w_out"][0].reshape(2, 8, 64, 1024)[:, PAIRS].reshape(1024, 1024)
    parts = [feature_units(np.concatenate([pair(aq), ak, pair(bq), bk], axis=1)),
             value_units(np.concatenate([av, bv], axis=1)), feature_units(w_out),
             mlp_units(a["mlp_w1"][0], a["mlp_w2"][0]),
             feature_units(wo[:, 0:2048]), value_units(wo[:, 2048:3072]), feature_units(a["odd_w_out"][0]),
             mlp_units(a["mlp_w1"][1], a["mlp_w2"][1])]
    for l in range(2):
        w = a["w_in_2"][l]
        s = np.cumsum([0, 768, 256, 32, 384, 384, 384, 256, 256, 256, 512, 64, 8, 1024])
        cq, ckv, kr, qb, kb, vb, qc, kc, vc, qi, ki, wi, gate = (w[:, s[i]:s[i + 1]] for i in range(13))
        z = np.zeros((1024, 120), w.dtype)
        uq = a["w_uq_2"][l].reshape(768, 6, 96)
        uq = np.concatenate([uq, np.zeros((768, 6, 32), w.dtype)], axis=2).reshape(768, 768)
        uk, uv = a["w_uk_2"][l], a["w_uv_2"][l]
        parts += [feature_units(np.concatenate([cq, ckv, ki, kr, z[:, 0:32], qb, kb, qc, kc, qi], axis=1)),
                  value_units(np.concatenate([vc[:, P:], wi, z, vb, vc[:, :P]], axis=1)), feature_units(gate), feature_units(uq),
                  one_unit([uk[P * k:P * k + P, P * m:P * m + P] for m in range(3) for k in range(2)]),
                  one_unit([uv[0:P], uv[P:2 * P]]), feature_units(a["w_out_2"][l])]
    return np.concatenate(parts)


def ada_stream(a):
    w = np.concatenate([a["ada_w"][0], a["ada_w"][1], a["w_ada_2"][0], a["w_ada_2"][1]], axis=1)
    w = w.reshape(KT, P, -1)
    units = np.zeros((ADA_GROUPS, KT, P, GROUP), w.dtype)
    c = 0
    for g in range(ADA_GROUPS):
        n = 4 * ada_width(g)
        units[g, :, :, 0:n] = w[:, :, c:c + n]
        c += n
    return units.reshape(ADA_UNITS, P, GROUP)


def constants():
    c = np.zeros((P, C_END), np.float32)
    c[:, C_ID:C_ID + P] = np.eye(P)
    c[:, C_ONE:C_ONE + P] = 1.0
    for m in range(P):
        k, v = (m + 16, -1.0) if m % 32 < 16 else (m - 16, 1.0)
        c[k, C_RQ + m] = v
        if 64 <= m < 96:
            c[k, C_RM + m] = v
    t = np.arange(N)
    inv = (10000.0 ** (-np.arange(16) / 16.0)).astype(np.float32)
    row, col = (t // 64).astype(np.float32), (t % 64).astype(np.float32)
    ang = np.concatenate([np.outer(inv, row)] * 2 + [np.outer(inv, col)] * 2).astype(np.float32)
    c[:, C_COS:C_COS + N] = np.cos(np.concatenate([ang, ang]))
    c[:, C_SIN:C_SIN + N] = np.sin(np.concatenate([ang, ang]))
    angm = np.outer(inv, t.astype(np.float32)).astype(np.float32)
    c[:, C_COSM:C_COSM + N] = 1.0
    c[64:96, C_COSM:C_COSM + N] = np.cos(np.concatenate([angm, angm]))
    c[64:96, C_SINM:C_SINM + N] = np.sin(np.concatenate([angm, angm]))
    q, k = np.arange(N)[:, None], np.arange(N)[None, :]
    win = np.where(np.abs(q - k) <= 128, 0.0, NEG)
    start = np.clip(q % 64 - 8, 0, 48)
    nbr = np.where((k % 64 >= start) & (k % 64 < start + 16), 0.0, NEG)
    cau = np.where(k <= q, 0.0, NEG)
    for x, c0 in ((win, C_WIN), (nbr, C_NBR)):
        c[:, c0:c0 + 2 * N] = x.reshape(2, P, N).transpose(1, 0, 2).reshape(P, 2 * N)
    c[:, C_CAU:C_CAU + P] = cau[0:P, 0:P]
    c[:, C_CAU + P:C_CAU + 3 * P] = cau[P:]
    d = q - k
    count = ((d >= 0) & (d <= 128)) * 1.0 + ((d >= 0) & (d % 4 == 0)) + ((d >= 0) & (d % 16 == 0))
    ali = np.zeros((P, 10, 384), np.float32)
    for h in range(10):
        slope = 2.0 ** (-8.0 * (h + 1) / 10)
        x = -slope * d + (np.where(count > 0, np.log(np.maximum(count, 1.0)), NEG) if h < 6
                          else np.where(d >= 0, 0.0, NEG))
        ali[:, h, 0:P] = x[0:P, 0:P]
        ali[:, h, P:] = x[P:]
    return c, ali


def parameters(a):
    p = np.zeros((P, P_END), np.float32)
    p[:, P_CV:P_CV + 24] = np.stack([cols(a["c"][0]), cols(a["c_ctx"]), cols(a["c_2"][0])], axis=2).reshape(P, 24)
    p[:, P_AB:P_AB + 144] = cols(np.concatenate([a["ada_b"][0], a["ada_b"][1], a["b_ada_2"][0], a["b_ada_2"][1]]))
    p[:, P_N1:P_N1 + 16] = cols(a["norm1_g"].reshape(-1))
    p[:, P_N2:P_N2 + 16] = cols(a["norm2_g"].reshape(-1))
    p[:, P_FIN:P_FIN + 8] = cols(a["final_g"])
    p[:, P_LNG:P_LNG + 16] = cols(a["ln_g_2"].reshape(-1))
    p[:, P_LNB:P_LNB + 16] = cols(a["ln_b_2"].reshape(-1))
    p[:, P_QN:P_QN + 12] = cols(a["q_norm_g_2"].reshape(-1))
    p[:, P_KVN:P_KVN + 4] = cols(a["kv_norm_g_2"].reshape(-1))
    p[:, P_SUB:P_SUB + 1] = cols(a["subln_g"].reshape(-1))
    p[:, P_SINK:P_SINK + 8] = np.broadcast_to(a["a_sink"][0][PAIRS], (P, 8))
    for i, name in enumerate(("lam_q1", "lam_q2", "lam_k1", "lam_k2")):
        p[0:64, P_LAM + i] = a[name][0]
    return p


def tokens(x):
    return x.reshape(N, KT, P).transpose(2, 1, 0)


def kernel(**inputs):
    import concourse.bacc as bacc
    from concourse.bass_utils import run_bass_kernel_spmd

    a = {k: np.asarray(v) for k, v in inputs.items()}
    const, ali = constants()
    pad = np.zeros((8, 7, 127), np.float32)
    pad[:, :, 48:79] = a["b_rpb"][0][PAIRS][:, 4:11]
    rpb = np.stack([pad[:, :, 63 - q:127 - q] for q in range(64)]).reshape(64, 8, 7 * 64)
    arrays = {
        "wall": weight_stream(a), "aall": ada_stream(a), "const": const, "prm": parameters(a),
        "xin": np.concatenate([tokens(a["x"][0]), tokens(a["ctx"][0])], axis=2), "rpb": rpb, "ali": ali,
    }
    arrays = {k: np.ascontiguousarray(v) for k, v in arrays.items()}
    assert arrays["wall"].shape == (UNITS, P, 1024) and arrays["aall"].shape == (ADA_UNITS, P, GROUP)
    nc = bacc.Bacc("TRN2", target_bir_lowering=False, num_devices=1)
    args = [nc.dram_tensor(k, v.shape, mybir.dt.from_np(v.dtype), kind="ExternalInput").ap() for k, v in arrays.items()]
    out = nc.dram_tensor("out", (P, KT, N), F32, kind="ExternalOutput").ap()
    program(nc, *args, out)
    r = run_bass_kernel_spmd(nc, [arrays], core_ids=[0])
    return r.results[0]["out"].transpose(2, 1, 0).reshape(1, N, D)
```
